# Optimizing a Trainium2 kernel written in Bass

```python
import jax, jax.numpy as jnp
from jax import lax
import numpy as np

D_MODEL = 2048
BATCH = 1
SEQ = 256
DEPTH = 1

N_META = 16
BLOCK_Q = 128
D_MIX = D_MODEL
D_ATTN = D_MIX // 2
D_CONV = D_MIX - D_ATTN
ATTN_HEAD_DIM = 128
N_ATTN_HEADS = D_ATTN // ATTN_HEAD_DIM
CONV_GROUP_DIM = 128
N_CONV_GROUPS = D_CONV // CONV_GROUP_DIM
GROUP_DIM = 128
N_GROUPS = D_MIX // GROUP_DIM
CONV_WIDTH = 3
D_FF = -(-8 * D_MODEL // (3 * 256)) * 256
D_IN = 3 * D_ATTN + 3 * D_CONV + N_ATTN_HEADS
EPS = 1e-6
NEG = -1e30


def rmsnorm(x, g):
    xf = x.astype(jnp.float32)
    y = xf * lax.rsqrt(jnp.mean(xf * xf, axis=-1, keepdims=True) + EPS)
    return (y * g.astype(jnp.float32)).astype(x.dtype)

def short_conv(u, w):
    L = u.shape[1]
    up = jnp.pad(u, ((0, 0), (CONV_WIDTH - 1, 0), (0, 0)))
    y = w[0] * up[:, 0:L]
    for k in range(1, CONV_WIDTH):
        y = y + w[k] * up[:, k:k + L]
    return y

def forgetting_attention(q, k, v, log_f):
    Bsz, L, H, Dh = q.shape
    n_pad = (-L) % BLOCK_Q
    Lp = L + n_pad
    nb = Lp // BLOCK_Q
    pad4 = ((0, 0), (n_pad, 0), (0, 0), (0, 0))
    qp = jnp.pad(q, pad4).transpose(0, 2, 1, 3)
    kp = jnp.pad(k, pad4).transpose(0, 2, 1, 3)
    vp = jnp.pad(v, pad4).transpose(0, 2, 1, 3)
    lf = jnp.pad(log_f.astype(jnp.float32), ((0, 0), (n_pad, 0), (0, 0)))
    c = jnp.cumsum(lf, axis=1).transpose(0, 2, 1)
    key_pos = jnp.arange(Lp)
    key_valid = key_pos >= n_pad
    scale = ATTN_HEAD_DIM ** -0.5
    qb = qp.reshape(Bsz, H, nb, BLOCK_Q, Dh).transpose(2, 0, 1, 3, 4)
    cqb = c.reshape(Bsz, H, nb, BLOCK_Q).transpose(2, 0, 1, 3)

    def block(args):
        qi, cqi, i = args
        s = jnp.einsum('bhqd,bhkd->bhqk', qi, kp,
                       preferred_element_type=jnp.float32) * scale
        s = s + cqi[..., :, None] - c[:, :, None, :]
        qpos = i * BLOCK_Q + jnp.arange(BLOCK_Q)
        mask = (key_pos[None, :] <= qpos[:, None]) & key_valid[None, :]
        s = jnp.where(mask, s, NEG)
        p = jax.nn.softmax(s, axis=-1)
        return jnp.einsum('bhqk,bhkd->bhqd', p.astype(vp.dtype), vp)

    out = lax.map(block, (qb, cqb, jnp.arange(nb)))
    out = out.transpose(1, 0, 3, 2, 4).reshape(Bsz, Lp, H, Dh)
    return out[:, n_pad:]

def hybrid_mixer(h, w_in, b_f, conv_w, out_gain, w_out):
    Bsz, L, _ = h.shape
    z = h @ w_in
    o = 0
    q = z[..., o:o + D_ATTN]; o += D_ATTN
    k = z[..., o:o + D_ATTN]; o += D_ATTN
    v = z[..., o:o + D_ATTN]; o += D_ATTN
    gate_b = z[..., o:o + D_CONV]; o += D_CONV
    gate_c = z[..., o:o + D_CONV]; o += D_CONV
    hc = z[..., o:o + D_CONV]; o += D_CONV
    f_logit = z[..., o:o + N_ATTN_HEADS]
    shp = (Bsz, L, N_ATTN_HEADS, ATTN_HEAD_DIM)
    log_f = jax.nn.log_sigmoid((f_logit + b_f).astype(jnp.float32))
    attn = forgetting_attention(q.reshape(shp), k.reshape(shp), v.reshape(shp), log_f)
    attn = attn.reshape(Bsz, L, D_ATTN)
    conv = gate_b * short_conv(gate_c * hc, conv_w)
    y = jnp.concatenate([attn, conv], axis=-1).reshape(Bsz, L, N_GROUPS, GROUP_DIM)
    y = rmsnorm(y, out_gain.reshape(N_GROUPS, GROUP_DIM)).reshape(Bsz, L, D_MIX)
    return y @ w_out

def swiglu(h, w_gate, w_up, w_down):
    return (jax.nn.silu(h @ w_gate) * (h @ w_up)) @ w_down

def first_inputs(seed: int = 0) -> dict:
    key = jax.random.key(seed)
    ks = jax.random.split(key, 13)
    f32 = jnp.float32
    nrm = lambda k, s, sc: jax.random.normal(k, s, f32) * sc
    x = nrm(ks[0], (BATCH, SEQ, D_MODEL), 1.0)
    meta = nrm(ks[1], (N_META, D_MODEL), 1.0)
    norm_mix = 1.0 + nrm(ks[2], (DEPTH, D_MODEL), 0.02)
    w_in = nrm(ks[3], (DEPTH, D_MODEL, D_IN), D_MODEL ** -0.5)
    b_f = (jnp.linspace(1.0, 6.0, N_ATTN_HEADS, dtype=f32)[None, :]
           + nrm(ks[4], (DEPTH, N_ATTN_HEADS), 0.1))
    conv_w = nrm(ks[5], (DEPTH, CONV_WIDTH, D_CONV), CONV_WIDTH ** -0.5)
    out_gain = 1.0 + nrm(ks[6], (DEPTH, D_MIX), 0.02)
    w_out = nrm(ks[7], (DEPTH, D_MIX, D_MODEL), D_MIX ** -0.5)
    norm_ffn = 1.0 + nrm(ks[8], (DEPTH, D_MODEL), 0.02)
    w_gate = nrm(ks[9], (DEPTH, D_MODEL, D_FF), D_MODEL ** -0.5)
    w_up = nrm(ks[10], (DEPTH, D_MODEL, D_FF), D_MODEL ** -0.5)
    w_down = nrm(ks[11], (DEPTH, D_FF, D_MODEL), D_FF ** -0.5)
    final_norm = 1.0 + nrm(ks[12], (D_MODEL,), 0.02)
    return {"x": x, "meta": meta, "norm_mix": norm_mix, "w_in": w_in, "b_f": b_f,
            "conv_w": conv_w, "out_gain": out_gain, "w_out": w_out,
            "norm_ffn": norm_ffn, "w_gate": w_gate, "w_up": w_up,
            "w_down": w_down, "final_norm": final_norm}

def first_block(x, meta, norm_mix, w_in, b_f, conv_w, out_gain, w_out,
              norm_ffn, w_gate, w_up, w_down, final_norm):
    Bsz = x.shape[0]
    m = jnp.broadcast_to(meta.astype(x.dtype)[None], (Bsz, N_META, D_MODEL))
    h = jnp.concatenate([m, x], axis=1)
    for l in range(DEPTH):
        h = h + hybrid_mixer(rmsnorm(h, norm_mix[l]), w_in[l], b_f[l], conv_w[l],
                             out_gain[l], w_out[l])
        h = h + swiglu(rmsnorm(h, norm_ffn[l]), w_gate[l], w_up[l], w_down[l])
    h = rmsnorm(h, final_norm)
    return h[:, N_META:]


HEAD_DIM = 128
ATTN_WIDTH = D_MODEL // 2
ATTN_HEADS = ATTN_WIDTH // HEAD_DIM
POOL_WIDTH = D_MODEL // 2
POOL_WINDOWS = (2, 4, 8, 16)
POOL_GROUPS = len(POOL_WINDOWS)
POOL_GROUP_WIDTH = POOL_WIDTH // POOL_GROUPS
DILATED_PATTERNS = ((128, 1), (512, 4), (2048, 16))
SUB_BLOCK = 128
D_FF_2 = 4 * D_MODEL
ROPE_THETA = 10000.0
LN_EPS = 1e-5
DEEPNORM_ALPHA = (2.0 * DEPTH) ** 0.25
DEEPNORM_BETA = (8.0 * DEPTH) ** -0.25
IN_SPLITS = (ATTN_WIDTH, 2 * ATTN_WIDTH, 3 * ATTN_WIDTH, 3 * ATTN_WIDTH + POOL_WIDTH,
             3 * ATTN_WIDTH + POOL_WIDTH + D_MODEL)
IN_WIDTH = 3 * ATTN_WIDTH + POOL_WIDTH + 2 * D_MODEL


def layer_norm(x, g, b):
    xf = x.astype(jnp.float32)
    mu = jnp.mean(xf, axis=-1, keepdims=True)
    var = jnp.mean(jnp.square(xf - mu), axis=-1, keepdims=True)
    return ((xf - mu) * lax.rsqrt(var + LN_EPS) * g.astype(jnp.float32) + b.astype(jnp.float32)).astype(x.dtype)

def rope(t, positions):
    half = HEAD_DIM // 2
    inv_freq = ROPE_THETA ** (-jnp.arange(half, dtype=jnp.float32) / half)
    ang = positions.astype(jnp.float32)[..., None] * inv_freq
    cos = jnp.cos(ang)[:, :, None, :]
    sin = jnp.sin(ang)[:, :, None, :]
    t1 = t[..., :half].astype(jnp.float32)
    t2 = t[..., half:].astype(jnp.float32)
    return jnp.concatenate([t1 * cos - t2 * sin, t2 * cos + t1 * sin], axis=-1).astype(t.dtype)

def dilated_window_attention(q, k, v, window, dilation):
    B, S, H, Dh = q.shape
    span = window // dilation
    blk = SUB_BLOCK
    assert span <= blk
    unit = dilation * blk
    s_pad = -(-S // unit) * unit
    m_len = s_pad // dilation
    nb = m_len // blk

    def to_blocks(t):
        t = jnp.pad(t, ((0, 0), (0, s_pad - S), (0, 0), (0, 0)))
        t = t.reshape(B, m_len, dilation, H, Dh).transpose(0, 2, 1, 3, 4)
        return t.reshape(B, dilation, nb, blk, H, Dh)

    def with_prev(t):
        prev = jnp.pad(t, ((0, 0), (0, 0), (1, 0), (0, 0), (0, 0), (0, 0)))[:, :, :-1]
        return jnp.concatenate([prev, t], axis=3)

    qb = to_blocks(q)
    kw = with_prev(to_blocks(k))
    vw = with_prev(to_blocks(v))
    s = jnp.einsum('brnqhd,brnkhd->brnhqk', qb, kw,
                   preferred_element_type=jnp.float32) * (HEAD_DIM ** -0.5)
    qi = jnp.arange(blk)[:, None]
    kj = jnp.arange(2 * blk)[None, :]
    dist = qi + blk - kj
    band = (dist >= 0) & (dist <= span)
    valid = band[None] & ((jnp.arange(nb)[:, None, None] > 0) | (kj >= blk)[None])
    s = jnp.where(valid[None, None, :, None], s, -jnp.inf)
    mx = jnp.max(s, axis=-1, keepdims=True)
    p = jnp.exp(s - mx)
    l = jnp.sum(p, axis=-1)
    o = jnp.einsum('brnhqk,brnkhd->brnqhd', p, vw.astype(jnp.float32))
    o = o / jnp.swapaxes(l, 3, 4)[..., None]
    lse = jnp.swapaxes(mx[..., 0] + jnp.log(l), 3, 4)
    o = o.reshape(B, dilation, m_len, H, Dh).transpose(0, 2, 1, 3, 4).reshape(B, s_pad, H, Dh)[:, :S]
    lse = lse.reshape(B, dilation, m_len, H).transpose(0, 2, 1, 3).reshape(B, s_pad, H)[:, :S]
    return o, lse

def pool_mixer(u, w_pool, pool_scale):
    B, S, _ = u.shape
    ug = u.reshape(B, S, POOL_GROUPS, POOL_GROUP_WIDTH)
    pooled = []
    for g, w in enumerate(POOL_WINDOWS):
        xg = ug[:, :, g].astype(jnp.float32)
        c = jnp.cumsum(xg, axis=1)
        c_lag = jnp.pad(c, ((0, 0), (w, 0), (0, 0)))[:, :S]
        count = jnp.minimum(jnp.arange(1, S + 1), w).astype(jnp.float32)[None, :, None]
        pooled.append((c - c_lag) / count - xg)
    p = jnp.stack(pooled, axis=2).astype(u.dtype)
    y = jnp.einsum('bsgc,gcd->bsgd', p, w_pool).reshape(B, S, POOL_WIDTH)
    return y * pool_scale

def second_inputs(seed: int = 0) -> dict:
    key = jax.random.key(seed)
    ks = jax.random.split(key, 20)
    f32 = jnp.float32

    def nrm(k, shape, fan_in, gain=1.0):
        return jax.random.normal(k, shape, f32) * (gain * fan_in ** -0.5)

    x = jax.random.normal(ks[0], (BATCH, SEQ, D_MODEL), f32)
    positions = (jnp.arange(SEQ, dtype=jnp.int32)[None, :]
                 + jax.random.randint(ks[1], (BATCH, 1), 0, 1024, dtype=jnp.int32))
    w_in = jnp.concatenate([
        nrm(ks[2], (DEPTH, D_MODEL, 2 * ATTN_WIDTH), D_MODEL),
        nrm(ks[3], (DEPTH, D_MODEL, ATTN_WIDTH), D_MODEL, DEEPNORM_BETA),
        nrm(ks[4], (DEPTH, D_MODEL, POOL_WIDTH), D_MODEL),
        nrm(ks[5], (DEPTH, D_MODEL, 2 * D_MODEL), D_MODEL),
    ], axis=-1)
    w_pool = nrm(ks[6], (DEPTH, POOL_GROUPS, POOL_GROUP_WIDTH, POOL_GROUP_WIDTH), POOL_GROUP_WIDTH)
    pool_scale = 1.0 + 0.1 * jax.random.normal(ks[7], (DEPTH, POOL_WIDTH), f32)
    w_branch_attn = nrm(ks[8], (DEPTH, ATTN_WIDTH, D_MODEL), ATTN_WIDTH, DEEPNORM_BETA)
    w_branch_pool = nrm(ks[9], (DEPTH, POOL_WIDTH, D_MODEL), POOL_WIDTH, DEEPNORM_BETA)
    w_out = nrm(ks[10], (DEPTH, D_MODEL, D_MODEL), D_MODEL, DEEPNORM_BETA)
    ln_mix_g = 1.0 + 0.05 * jax.random.normal(ks[11], (DEPTH, D_MODEL), f32)
    ln_mix_b = 0.02 * jax.random.normal(ks[12], (DEPTH, D_MODEL), f32)
    w_ff1 = nrm(ks[13], (DEPTH, D_MODEL, D_FF_2), D_MODEL, DEEPNORM_BETA)
    w_ff2 = nrm(ks[14], (DEPTH, D_FF_2, D_MODEL), D_FF_2, DEEPNORM_BETA)
    ln_ff_g = 1.0 + 0.05 * jax.random.normal(ks[15], (DEPTH, D_MODEL), f32)
    ln_ff_b = 0.02 * jax.random.normal(ks[16], (DEPTH, D_MODEL), f32)
    return {"x": x, "positions": positions, "w_in": w_in, "w_pool": w_pool,
            "pool_scale": pool_scale, "w_branch_attn": w_branch_attn,
            "w_branch_pool": w_branch_pool, "w_out": w_out, "ln_mix_g": ln_mix_g,
            "ln_mix_b": ln_mix_b, "w_ff1": w_ff1, "w_ff2": w_ff2,
            "ln_ff_g": ln_ff_g, "ln_ff_b": ln_ff_b}

def second_block(x, positions, w_in, w_pool, pool_scale, w_branch_attn, w_branch_pool, w_out,
              ln_mix_g, ln_mix_b, w_ff1, w_ff2, ln_ff_g, ln_ff_b):
    B, S, _ = x.shape
    for layer in range(DEPTH):
        h = x @ w_in[layer]
        q, k, v, u, gate_attn, gate_pool = jnp.split(h, IN_SPLITS, axis=-1)
        q = rope(q.reshape(B, S, ATTN_HEADS, HEAD_DIM), positions)
        k = rope(k.reshape(B, S, ATTN_HEADS, HEAD_DIM), positions)
        v = v.reshape(B, S, ATTN_HEADS, HEAD_DIM)
        outs, lses = [], []
        for window, dilation in DILATED_PATTERNS:
            o_g, lse_g = dilated_window_attention(q, k, v, window, dilation)
            outs.append(o_g)
            lses.append(lse_g)
        mix_w = jax.nn.softmax(jnp.stack(lses, axis=0), axis=0)
        o_attn = jnp.einsum('pbsh,pbshd->bshd', mix_w, jnp.stack(outs, axis=0))
        y_attn = o_attn.reshape(B, S, ATTN_WIDTH).astype(x.dtype) @ w_branch_attn[layer]
        y_pool = pool_mixer(u, w_pool[layer], pool_scale[layer]) @ w_branch_pool[layer]
        merged = jax.nn.sigmoid(gate_attn) * y_attn + jax.nn.sigmoid(gate_pool) * y_pool
        mix = merged @ w_out[layer]
        x = layer_norm(DEEPNORM_ALPHA * x + mix, ln_mix_g[layer], ln_mix_b[layer])
        f = jnp.square(jax.nn.relu(x @ w_ff1[layer])) @ w_ff2[layer]
        x = layer_norm(DEEPNORM_ALPHA * x + f, ln_ff_g[layer], ln_ff_b[layer])
    return x


def setup_inputs(seed=0):
    out = dict(first_inputs(seed))
    for name, value in second_inputs(seed + 1).items():
        if name != "x":
            out[name + "_2"] = value
    return out


def reference(
    x, meta, norm_mix, w_in, b_f, conv_w, out_gain, w_out, norm_ffn, w_gate, w_up, w_down,
    final_norm, positions_2, w_in_2, w_pool_2, pool_scale_2, w_branch_attn_2, w_branch_pool_2,
    w_out_2, ln_mix_g_2, ln_mix_b_2, w_ff1_2, w_ff2_2, ln_ff_g_2, ln_ff_b_2,
):
    x = first_block(
        x, meta, norm_mix, w_in, b_f, conv_w, out_gain, w_out, norm_ffn, w_gate, w_up, w_down,
        final_norm,
    )
    return second_block(
        x, positions_2, w_in_2, w_pool_2, pool_scale_2, w_branch_attn_2, w_branch_pool_2,
        w_out_2, ln_mix_g_2, ln_mix_b_2, w_ff1_2, w_ff2_2, ln_ff_g_2, ln_ff_b_2,
    )


_drawn_inputs = setup_inputs


def setup_inputs(seed=0):
    import zlib

    import numpy as np

    out = dict(_drawn_inputs(seed))
    spreads = {}
    factors = {'out_gain': 3.715,
     'norm_ffn': 5.068,
     'final_norm': 2.877,
     'pool_scale_2': 4.137,
     'ln_mix_b_2': 2.691,
     'ln_ff_b_2': 2.769}
    for name, (base, spread) in spreads.items():
        noise = np.random.default_rng([zlib.crc32(name.encode()), seed]).standard_normal(out[name].shape)
        drawn = base * np.exp(spread * noise) if base else spread * noise
        out[name] = __import__('jax').numpy.asarray(drawn.astype(out[name].dtype))
    for name, factor in factors.items():
        out[name] = (out[name] * factor).astype(out[name].dtype)
    return out
```

```python
from contextlib import ExitStack

import numpy as np

import concourse.bass as bass
from concourse import mybir

F32 = mybir.dt.float32
F32R = mybir.dt.float32r
I32 = mybir.dt.int32
ALU = mybir.AluOpType
ACT = mybir.ActivationFunctionType
AX_X = mybir.AxisListType.X

P = 128
D = 2048
KT = D // P
SEQ = 256
META = 16
TOK = META + SEQ
HEADS = 8
D_FF1 = 5632
D_FF2 = 8192
NEG = -1e30
RMS_EPS = 1e-6
LN_EPS = 1e-5
ALPHA = 2.0 ** 0.25
SCALE = float(P) ** -0.5

UNIT_K = 2
BLOCK = 4
UNIT = UNIT_K * BLOCK * P
RAW = 5
SPLIT = 4
CONV_TOK = SEQ + 2
POOL_WINDOWS = (2, 4, 8, 16)

GROUPS1 = (12, 12, 12, 8)
GROUPS2 = (16, 16, 16, 16)

KEYS1 = (META + P, TOK)
KEYS2 = (P, SEQ)

PARAMS = {}
_at = 0
for _name, _n in (("norm_mix", KT), ("out_gain", KT), ("norm_ffn", KT), ("final_norm", KT),
                  ("conv_w", 24), ("pool_scale", 8), ("ln_mix_g", KT), ("ln_mix_b", KT),
                  ("ln_ff_g", KT), ("ln_ff_b", KT), ("b_f", 1)):
    PARAMS[_name] = _at
    _at += _n
N_PARAMS = _at

C_IDENT, C_FREQ, C_SIGN, C_RAMP = 0, P, P + 1, P + 2
N_CONST = C_RAMP + 4 * 16


class Ticket:

    def __init__(self, sem, value):
        self.sem, self.value = sem, value


class Engine:

    def __init__(self, sem):
        self.sem, self.count, self.steps = sem, 0, []

    def do(self, make, *waits):
        self.count += 1
        self.steps.append((waits, make, self.sem, 1))
        return Ticket(self.sem, self.count)

    def quiet(self, make, *waits):
        self.steps.append((waits, make, None, 0))

    def load(self, make, sem, value, *waits):
        self.steps.append((waits, make, sem, 16))
        return Ticket(sem, value)

    def wait(self, *waits):
        self.steps.append((waits, None, None, 0))

    def now(self):
        return Ticket(self.sem, self.count)

    def play(self, eng):
        reached = {}
        for waits, make, sem, by in self.steps:
            for t in waits:
                if t is not None and t.value > reached.get(id(t.sem), 0):
                    eng.wait_ge(t.sem, t.value)
                    reached[id(t.sem)] = t.value
            if make is not None:
                ins = make(eng)
                if sem is not None:
                    ins.then_inc(sem, by)


class Slot:
    def __init__(self, ap):
        self.ap, self.free, self.held, self.age = ap, (), False, 0

    def release(self, *tickets):
        self.free, self.held = tickets, False


class Ring:

    def __init__(self, aps):
        self.slots, self.turn = [Slot(a) for a in aps], 0

    def take(self):
        free = [s for s in self.slots if not s.held]
        assert free, "no slot is free"
        s = min(free, key=lambda x: x.age)
        self.turn += 1
        s.age, s.held = self.turn, True
        return s


def two_blocks(nc, w, tokens, params, consts, mask1, mask2, positions, out):
    with ExitStack() as ctx:
        def sb(name, shape, dt=F32):
            return ctx.enter_context(nc.sbuf_tensor(name, shape, dt))

        def sem(name):
            return ctx.enter_context(nc.semaphore(name))

        h = sb("h", [P, KT, TOK])
        a_op = sb("a_op", [P, KT, 2, TOK], F32R)
        b_op = sb("b_op", [P, KT, 2, SEQ], F32R)
        raw = sb("raw", [P, RAW, UNIT])
        w_hi = sb("w_hi", [P, SPLIT, UNIT], F32R)
        w_lo = sb("w_lo", [P, SPLIT, UNIT], F32R)
        q = sb("q", [P, HEADS, SEQ])
        k = sb("k", [P, HEADS, TOK])
        v = sb("v", [P, 3, HEADS * P])
        ytile = sb("ytile", [P, KT, SEQ])
        probs = sb("probs", [P, 2, SEQ + TOK])
        probs_t = sb("probs_t", [P, 2 * SEQ])
        probs_t2 = sb("probs_t2", [META, P])
        con = sb("con", [P, N_CONST])
        masks = sb("masks", [P, 2 * (P + SEQ)])
        par = sb("par", [P, N_PARAMS])
        ones = sb("ones", [P, P])
        row = sb("row", [P, TOK])
        shift = sb("shift", [P, SEQ])
        cosr = sb("cosr", [P, SEQ])
        sinr = sb("sinr", [P, SEQ])
        acc = sb("acc", [P, TOK])
        acc2 = sb("acc2", [P, SEQ])
        csum = sb("csum", [HEADS, TOK])
        cneg = sb("cneg", [HEADS, TOK])
        cq = sb("cq", [P, 2, HEADS])
        gms = sb("gms", [P, KT, 2])
        work = Ring([sb(f"work{i}", [P, TOK])[:, :] for i in range(6)])
        tiny = Ring([sb(f"tiny{i}", [P, 6, 16])[:, :, :] for i in range(4)])
        prob_ring = Ring([probs[:, i, :] for i in range(2)])

        def psum(name):
            return ctx.enter_context(nc.psum_tensor(name, [P, 512], F32))

        out_banks = Ring([psum(f"out_bank{i}")[:, :] for i in range(5)])
        side_banks = Ring([psum(f"side_bank{i}")[:, :] for i in range(3)])

        sp = Engine(None)
        pe, act, dve, pool = (Engine(sem(f"{n}_done")) for n in ("pe", "act", "dve", "pool"))
        s_raw = [sem(f"raw_landed{i}") for i in range(RAW)]
        s_h = [sem(f"tokens_landed{i}") for i in range(4)]
        s_par, s_con, s_mask = sem("params_landed"), sem("consts_landed"), sem("masks_landed")
        s_pos, s_out = sem("positions_landed"), sem("outputs_stored")

        ident = con[:, C_IDENT:C_IDENT + P]

        def p_col(name, i):
            c = PARAMS[name] + i
            return par[:, c:c + 1]

        clock = [0]
        later_work = []

        def later(n, fn):
            later_work.append((clock[0] + n, len(later_work), fn))

        def step():
            clock[0] += 1
            due = sorted(x for x in later_work if x[0] <= clock[0])
            later_work[:] = [x for x in later_work if x[0] > clock[0]]
            for _, _, fn in due:
                fn()

        def flush():
            while later_work:
                step()

        order = []

        def stream(name, n_k, blocks, fine=True):
            order.extend((name, b, u, fine) for b in blocks for u in range(n_k // UNIT_K))

        stream("w_in", KT, [0])
        order.extend(("w_f", 0, u, True) for u in range(2))
        stream("w_in", KT, range(1, 12))
        stream("w_out", KT, range(4))
        base = 0
        for n in GROUPS1:
            stream("w_gu", KT, range(base // 2, (base + n) // 2))
            for b in range(4):
                order.extend(("w_down", b, base // UNIT_K + u, True) for u in range(n // UNIT_K))
            base += n
        stream("w_in_2", KT, range(10))
        order.extend(("w_pool", 0, u, False) for u in range(2))
        stream("w_in_2", KT, range(10, 12))
        for b in range(2):
            stream("w_ba", 8, [b])
            stream("w_bp", 8, [b])
        stream("w_in_2", KT, range(12, 16))
        for b in range(2, 4):
            stream("w_ba", 8, [b])
            stream("w_bp", 8, [b])
        stream("w_out_2", KT, range(4))
        base = 0
        for n in GROUPS2:
            stream("w_ff1", KT, range(base // 4, (base + n) // 4))
            for b in range(4):
                order.extend(("w_ff2", b, base // UNIT_K + u, True) for u in range(n // UNIT_K))
            base += n

        raw_free = [()] * RAW
        split_free = [()] * SPLIT
        loaded, landed = 0, {}
        split_next, split_done, fine_count = 0, {}, 0

        def load_units(limit):
            nonlocal loaded
            while loaded < min(limit, len(order)):
                name, b, u, _ = order[loaded]
                i = loaded % RAW
                src = w[name][b, u]
                landed[loaded] = sp.load(lambda e, i=i, src=src: e.dma_start(raw[:, i, :], src),
                                         s_raw[i], 16 * (loaded // RAW + 1), *raw_free[i])
                loaded += 1

        def split_units(limit):
            nonlocal split_next, fine_count
            while split_next < min(limit, len(order)):
                n = split_next
                i = n % RAW
                if not order[n][3]:
                    break
                j = fine_count % SPLIT
                hi = act.do(lambda e, i=i, j=j: e.copy(w_hi[:, j, :], raw[:, i, :]),
                            landed[n], *split_free[j])
                lo = dve.do(lambda e, i=i, j=j: e.tensor_tensor(
                    w_lo[:, j, :], raw[:, i, :], w_hi[:, j, :].bitcast(F32), ALU.subtract), hi)
                split_free[j] = None
                split_done[n] = (j, hi, lo)
                raw_free[i] = (hi, lo)
                fine_count += 1
                split_next += 1
                load_units(n + RAW + 1)

        unit_at = [0]

        def product(n_units, kt_of, moving, ready, tiles, width=P * BLOCK):
            per_unit = UNIT // width
            n_tiles = width // P
            banks = [None] * n_tiles
            chunks = [list(range(c, min(c + 2, n_units))) for c in range(0, n_units, 2)]
            for c, units in enumerate(chunks):
                first = unit_at[0]
                split_units(first + len(units))
                last_use = {}
                held = {n: split_done[first + x] for x, n in enumerate(units)}
                split_units(first + len(units) + 2)
                for t in range(n_tiles):
                    cols, finish = tiles[t]
                    n_col = cols.stop - cols.start
                    dual = n_col == SEQ
                    if c == 0:
                        banks[t] = out_banks.take()
                    bank = banks[t]
                    for n in units:
                        j, hi_t, lo_t = held[n]
                        for i in range(per_unit):
                            start = c == 0 and n == units[0] and i == 0
                            stop = n == n_units - 1 and i == per_unit - 1
                            kt = kt_of(n, i)
                            a_hi, a_lo, a_both = moving(kt, cols)
                            at = i * width + t * P
                            wh, wl = w_hi[:, j, at:at + P], w_lo[:, j, at:at + P]
                            waits = [hi_t, lo_t, *ready(kt)] + (list(bank.free) if start else [])
                            if dual:
                                mm = [(bank.ap[:, 0:2 * SEQ], wh, a_both), (bank.ap[:, 0:SEQ], wl, a_hi)]
                                if not start:
                                    mm.reverse()
                            else:
                                mm = [(bank.ap[:, 0:n_col], wh, a_hi), (bank.ap[:, 0:n_col], wh, a_lo),
                                      (bank.ap[:, 0:n_col], wl, a_hi)]
                            for x, (o, s, m) in enumerate(mm):
                                def make(e, o=o, s=s, m=m, a=start and x == 0, z=stop and x == len(mm) - 1):
                                    return e.matmul(o, s, m, start=a, stop=z, skip_group_check=True)
                                tail = x == len(mm) - 1
                                if tail and (stop or (t == n_tiles - 1 and i == per_unit - 1)):
                                    done = pe.do(make, *waits)
                                    last_use[n] = done
                                else:
                                    pe.quiet(make, *waits)
                    if c == len(chunks) - 1:
                        finish(bank, done)
                    step()
                for n in units:
                    split_free[held[n][0]] = (last_use[n],)
                unit_at[0] += len(units)

        def from_a(kt, cols):
            return (a_op[:, kt, 0, cols], a_op[:, kt, 1, cols], a_op[:, kt, :, cols])

        def from_b(kt, cols):
            return (b_op[:, kt, 0, :], b_op[:, kt, 1, :], b_op[:, kt, :, :])

        REAL, ALL, CONV = slice(META, TOK), slice(0, TOK), slice(META - 2, TOK)

        def joined(bank, done):
            s = work.take()
            y = s.ap[:, 0:SEQ]
            t = act.do(lambda e: e.copy(y, bank.ap[:, SEQ:2 * SEQ]), done, *s.free)
            t = dve.do(lambda e: e.tensor_tensor(y, y, bank.ap[:, 0:SEQ], ALU.add), t)
            bank.release(t)
            return s, y, t

        def split_to(dst_hi, dst_lo, src, scale, *waits):
            if scale is None:
                t = act.do(lambda e: e.copy(dst_hi, src), *waits)
                return dve.do(lambda e: e.tensor_tensor(dst_lo, src, dst_hi.bitcast(F32), ALU.subtract), t)
            t = act.do(lambda e: e.activation(dst_hi, src, ACT.Copy, scale=scale), *waits)
            return dve.do(lambda e: e.scalar_tensor_tensor(
                dst_lo, src, scale, dst_hi.bitcast(F32), ALU.mult, ALU.subtract), t)

        def sums_to_rows(bank, col, src, starts, *waits):
            for n, s in enumerate(starts):
                t = pe.do(lambda e, n=n, s=s: e.matmul(bank.ap[:, col + n:col + n + 1], src[:, s:s + P],
                                                       ones[:, 0:1], start=True, stop=True),
                          *waits, *bank.free)
            return t

        def rsqrt(ms, y, scratch, *waits):
            t = dve.do(lambda e: e.reciprocal(scratch, ms), *waits)
            t = act.do(lambda e: e.activation(y, scratch, ACT.Sqrt), t)
            t = dve.do(lambda e: e.tensor_tensor(scratch, y, y, ALU.mult), t)
            t = dve.do(lambda e: e.tensor_tensor(scratch, scratch, ms, ALU.mult), t)
            t = dve.do(lambda e: e.tensor_scalar(scratch, scratch, -0.5, 1.5, ALU.mult, ALU.add), t)
            return dve.do(lambda e: e.tensor_tensor(y, y, scratch, ALU.mult), t)

        def rows_to_bank(bank, cols, starts, at, *waits):
            for col, s in zip(cols, starts):
                d = work.take()
                dg = d.ap[:, 0:P]
                t = dve.do(lambda e, col=col, dg=dg: e.tensor_scalar(dg, ident, col, None, ALU.mult),
                           *waits, *d.free)
                t = pe.do(lambda e, dg=dg, s=s: e.matmul(bank.ap[:, at + s:at + s + P], ones[:, :], dg,
                                                         start=True, stop=True), t, *bank.free)
                d.release(t)
            return t

        def rms_rows(dst, starts, *waits):
            bank, ty = side_banks.take(), tiny.take()
            n = len(starts)
            t = sums_to_rows(bank, 0, acc, starts, *waits)
            ms, y, z = ty.ap[:, 0, 0:n], ty.ap[:, 1, 0:n], ty.ap[:, 2, 0:n]
            t = dve.do(lambda e: e.tensor_scalar(ms, bank.ap[:, 0:n], 1.0 / D, RMS_EPS, ALU.mult, ALU.add),
                       t, *ty.free)
            bank.release(t)
            t = rsqrt(ms, y, z, t)
            b2 = side_banks.take()
            t = rows_to_bank(b2, [ty.ap[:, 1, i:i + 1] for i in range(n)], starts, 0, t)
            ty.release(dve.now())
            width = starts[-1] + P
            t = act.do(lambda e: e.copy(dst[:, 0:width], b2.ap[:, 0:width]), t, dve.now(), pool.now())
            b2.release(t)
            return t

        acc_ready = [None]

        def add_square(src, first, dst, *waits):
            n = src.shape[-1]
            if first:
                acc_ready[0] = act.do(lambda e: e.activation(dst, src, ACT.Square), *waits, pe.now(), pool.now())
                return
            s = work.take()
            t = act.do(lambda e: e.activation(s.ap[:, 0:n], src, ACT.Square), *waits, *s.free)
            acc_ready[0] = pool.do(lambda e: e.tensor_tensor(dst, dst, s.ap[:, 0:n], ALU.add),
                                   t, acc_ready[0])
            s.release(acc_ready[0])

        got_par = sp.load(lambda e: e.dma_start(par[:, :], params), s_par, 16)
        got_h = []
        for i in range(4):
            got_h.append(sp.load(lambda e, i=i: e.dma_start(h[:, 4 * i:4 * i + 4, :], tokens[:, 4 * i:4 * i + 4, :]),
                                 s_h[i], 16))
            if i == 0:
                load_units(2)
        load_units(RAW)
        got_con = sp.load(lambda e: e.dma_start(con[:, :], consts), s_con, 16)
        got_mask = sp.load(lambda e: e.dma_start(masks[:, 0:sum(KEYS1)], mask1), s_mask, 16)
        made_ones = pool.do(lambda e: e.memset(ones[:, :], 1.0))
        cleared = pool.do(lambda e: e.memset(probs[:, :, :], 0.0))

        a_ready = {}
        split_units(2)
        for kt in range(KT):
            a_ready[kt] = split_to(a_op[:, kt, 0, :], a_op[:, kt, 1, :], h[:, kt, :], p_col("norm_mix", kt),
                                   got_h[kt // 4], got_par)
            add_square(h[:, kt, :], kt == 0, acc[:, :], got_h[kt // 4])
            if kt == 3:
                split_units(4)
        row_ready = [None]

        def first_row():
            row_ready[0] = rms_rows(row, (0, P, TOK - P), acc_ready[0], made_ones, got_con)
        later(6, first_row)

        a_of = lambda kt: (a_ready[kt],)

        q_ready, k_ready, v_ready = {}, {}, {}

        def finish_k(hd):
            def finish(bank, done):
                k_ready[hd] = dve.do(lambda e: e.tensor_tensor(k[:, hd, :], bank.ap[:, 0:TOK], row[:, :], ALU.mult),
                                     done, row_ready[0])
                bank.release(k_ready[hd])
            return ALL, finish

        def finish_q(hd):
            def finish(bank, done):
                s, y, t = joined(bank, done)
                q_ready[hd] = dve.do(lambda e: e.scalar_tensor_tensor(
                    q[:, hd, :], y, SCALE, row[:, REAL], ALU.mult, ALU.mult), t, row_ready[0])
                s.release(q_ready[hd])
            return REAL, finish

        def to_v(hd, src_slot, src, t, n_full, rest):
            bank = side_banks.take()
            for n in range(n_full):
                t2 = pe.do(lambda e, n=n: e.transpose(bank.ap[:, n * P:(n + 1) * P], src[:, n * P:(n + 1) * P], ident),
                           t, got_con, *bank.free)
            if rest:
                t2 = pe.do(lambda e: e.transpose(bank.ap[0:rest, n_full * P:(n_full + 1) * P],
                                                 src[:, n_full * P:n_full * P + rest], ident))
            src_slot.release(t2)
            f = act.do(lambda e: e.copy(v[:, 0:n_full, hd * P:(hd + 1) * P],
                                        bank.ap[:, 0:n_full * P].rearrange("p (n d) -> p n d", d=P)), t2)
            if rest:
                f = act.do(lambda e: e.copy(v[0:rest, n_full, hd * P:(hd + 1) * P],
                                            bank.ap[0:rest, n_full * P:(n_full + 1) * P]), t2)
            bank.release(f)
            v_ready[hd] = f

        def finish_v(hd):
            def finish(bank, done):
                s = work.take()
                t = dve.do(lambda e: e.tensor_tensor(s.ap, bank.ap[:, 0:TOK], row[:, :], ALU.mult),
                           done, row_ready[0], *s.free)
                bank.release(t)
                later(2, lambda: to_v(hd, s, s.ap, t, 2, META))
            return ALL, finish

        c_ready = [None]
        H8 = slice(0, HEADS)

        def finish_f(bank, done):
            s1, s2, s3 = work.take(), work.take(), work.take()
            z, e1, m = s1.ap[H8, :], s2.ap[H8, :], s3.ap[H8, :]
            bf = par[H8, PARAMS["b_f"]:PARAMS["b_f"] + 1]
            t = dve.do(lambda e: e.tensor_tensor(z, bank.ap[H8, 0:TOK], row[H8, :], ALU.mult),
                       done, row_ready[0], *s1.free)
            bank.release(t)
            t = dve.do(lambda e: e.tensor_scalar(z, z, bf, None, ALU.add), t)
            ta = act.do(lambda e: e.activation(e1, z, ACT.Abs), t, *s2.free)
            ta = act.do(lambda e: e.activation(e1, e1, ACT.Exp, scale=-1.0), ta)
            ta = act.do(lambda e: e.activation(e1, e1, ACT.Ln, bias=1.0), ta)
            t = dve.do(lambda e: e.tensor_scalar(z, z, 0.0, None, ALU.min), ta)
            t = dve.do(lambda e: e.tensor_tensor(z, z, e1, ALU.subtract), t)
            t2 = dve.do(lambda e: e.memset(m, 1.0), *s3.free)
            t = dve.do(lambda e: e.tensor_tensor_scan(csum[:, :], m, z, 0.0, ALU.mult, ALU.add), t, t2)
            s1.release(t)
            s2.release(t)
            s3.release(t)
            t = dve.do(lambda e: e.tensor_scalar(cneg[:, :], csum[:, :], -1.0, None, ALU.mult), t)

            def turn():
                b = side_banks.take()
                for i in range(2):
                    a = META + i * P
                    tp = pe.do(lambda e, a=a, i=i: e.transpose(b.ap[:, 8 * i:8 * i + 8], csum[:, a:a + P],
                                                               con[H8, 0:HEADS]), t, got_con, *b.free)
                c_ready[0] = act.do(lambda e: e.copy(cq[:, :, :], b.ap[:, 0:16].rearrange("p (i h) -> p i h", i=2)), tp)
                b.release(c_ready[0])
            later(3, turn)

        kt_plain = lambda n, i: UNIT_K * n + i
        U = KT // UNIT_K
        product(U, kt_plain, from_a, a_of, [finish_k(i) for i in range(4)])
        product(2, lambda n, i: 8 * n + i, from_a, a_of, [(ALL, finish_f)], width=P)
        product(U, kt_plain, from_a, a_of, [finish_k(i) for i in range(4, 8)])
        for b in range(2):
            product(U, kt_plain, from_a, a_of, [finish_q(4 * b + i) for i in range(4)])
        for b in range(2):
            product(U, kt_plain, from_a, a_of, [finish_v(4 * b + i) for i in range(4)])
        flush()

        def softmax(slot, spans, t, counts, *more):
            ty = tiny.take()
            mx, l, r = ty.ap[:, 0, 0:2], ty.ap[:, 1, 0:2], ty.ap[:, 2, 0:2]
            for i, (a, n) in enumerate(spans):
                t = dve.do(lambda e, i=i, a=a, n=n: e.reduce_max(mx[:, i:i + 1], slot.ap[:, a:a + n], AX_X), t, *ty.free)
            t = dve.do(lambda e: e.tensor_scalar(mx, mx, -1.0, None, ALU.mult), t)
            for i, (a, n) in enumerate(spans):
                acc_out = {} if counts else {"accum_out": l[:, i:i + 1]}
                tx = act.do(lambda e, i=i, a=a, n=n, o=acc_out: e.activation(
                    slot.ap[:, a:a + n], slot.ap[:, a:a + n], ACT.Exp, bias=mx[:, i:i + 1], **o), t)
            t = tx
            if counts:
                for i, (a, n) in enumerate(spans):
                    t = dve.do(lambda e, i=i, a=a, n=n: e.scalar_tensor_tensor(
                        slot.ap[:, a:a + n], slot.ap[:, a:a + n], 1.0, counts[i], ALU.mult, ALU.mult,
                        accum_out=l[:, i:i + 1]), tx, *more)
            t = dve.do(lambda e: e.reciprocal(r, l), t)
            for i, (a, n) in enumerate(spans):
                t = dve.do(lambda e, i=i, a=a, n=n: e.tensor_scalar(
                    slot.ap[:, a:a + n], slot.ap[:, a:a + n], r[:, i:i + 1], None, ALU.mult), t)
            ty.release(t)
            return t

        y_ready, ms_ready = {}, {}

        def group_square(g):
            s = work.take()
            y = s.ap[:, 0:SEQ]
            t = act.do(lambda e: e.activation(y, ytile[:, g, :], ACT.Square), y_ready[g], *s.free)

            def sums():
                b = side_banks.take()
                t2 = sums_to_rows(b, 0, s.ap, (0, P), t)
                s.release(t2)
                ms_ready[g] = dve.do(lambda e: e.tensor_scalar(gms[:, g, :], b.ap[:, 0:2], 1.0 / P, RMS_EPS,
                                                               ALU.mult, ALU.add), t2)
                b.release(ms_ready[g])
            later(2, sums)

        probs_t_free = [()]
        q_cols = (0, KEYS1[0])

        def head1(hd):
            state = {}

            def scores():
                b, s = side_banks.take(), prob_ring.take()
                sel = con[H8, hd:hd + 1].to_broadcast([HEADS, P])
                for i in range(2):
                    n, o = KEYS1[i], q_cols[i]
                    pe.quiet(lambda e, i=i, n=n, o=o: e.matmul(
                        b.ap[:, o:o + n], q[:, hd, i * P:(i + 1) * P], k[:, hd, 0:n], start=True, stop=False),
                        q_ready[hd], k_ready[hd], *b.free)
                    t = pe.do(lambda e, n=n, o=o: e.matmul(b.ap[:, o:o + n], sel, cneg[:, 0:n],
                                                           start=False, stop=True), c_ready[0])
                spans = ((0, KEYS1[0]), (SEQ, KEYS1[1]))
                for i, (a, n) in enumerate(spans):
                    o = q_cols[i]
                    t = dve.do(lambda e, i=i, a=a, n=n, o=o: e.scalar_tensor_tensor(
                        s.ap[:, a:a + n], b.ap[:, o:o + n], cq[:, i, hd:hd + 1], masks[:, o:o + n],
                        ALU.add, ALU.add), t, c_ready[0], got_mask, cleared, *s.free)
                b.release(t)
                state.update(s=s, t=softmax(s, spans, t, None))

            def turn():
                s, t = state["s"], state["t"]
                bt, bo = side_banks.take(), side_banks.take()
                for kt in range(2):
                    for i in range(2):
                        o = kt * SEQ + i * P
                        pe.quiet(lambda e, i=i, kt=kt, o=o: e.transpose(
                            bt.ap[:, o:o + P], s.ap[:, i * SEQ + kt * P:i * SEQ + (kt + 1) * P], ident),
                            t, *bt.free)
                t2 = pe.do(lambda e: e.transpose(bo.ap[0:META, SEQ:SEQ + P], s.ap[:, 2 * SEQ:2 * SEQ + META], ident),
                           *bo.free)
                s.release(t2)
                f = act.do(lambda e: e.copy(probs_t[:, :], bt.ap[:, :]), t2, *probs_t_free[0])
                g = dve.do(lambda e: e.tensor_copy(probs_t2[:, :], bo.ap[0:META, SEQ:SEQ + P]), t2, *probs_t_free[0])
                bt.release(f)
                state.update(bo=bo, t=(f, g))

            def values():
                bo = state["bo"]
                hs = slice(hd * P, (hd + 1) * P)
                pe.quiet(lambda e: e.matmul(bo.ap[:, 0:SEQ], v[:, 0, hs], probs_t[:, 0:SEQ], start=True, stop=False,
                                            skip_group_check=True), *state["t"], v_ready[hd])
                pe.quiet(lambda e: e.matmul(bo.ap[:, P:SEQ], v[0:META, 2, hs], probs_t2[:, :], start=False,
                                            stop=False, skip_group_check=True))
                t = pe.do(lambda e: e.matmul(bo.ap[:, 0:SEQ], v[:, 1, hs], probs_t[:, SEQ:2 * SEQ], start=False,
                                             stop=True, skip_group_check=True))
                probs_t_free[0] = (t,)
                y_ready[hd] = act.do(lambda e: e.copy(ytile[:, hd, :], bo.ap[:, 0:SEQ]), t)
                bo.release(y_ready[hd])
                group_square(hd)

            later(4 * hd + 1, scores)
            later(4 * hd + 6, turn)
            later(4 * hd + 9, values)

        b_ready = {}

        def normed_groups(groups, *waits):
            ty = tiny.take()
            n = 2 * len(groups)
            ms = gms[:, groups[0]:groups[-1] + 1, :].rearrange("p g i -> p (g i)")
            y, z = ty.ap[:, 1, 0:n], ty.ap[:, 2, 0:n]
            t = rsqrt(ms, y, z, *[ms_ready[g] for g in groups], *ty.free)

            def one(x, g):
                b, s = side_banks.take(), work.take()
                t2 = rows_to_bank(b, [ty.ap[:, 1, 2 * x + i:2 * x + i + 1] for i in range(2)], (0, P), 0, t)
                if x == len(groups) - 1:
                    ty.release(dve.now())
                yn = s.ap[:, 0:SEQ]
                t3 = dve.do(lambda e: e.tensor_tensor(yn, ytile[:, g, :], b.ap[:, 0:SEQ], ALU.mult), t2, *s.free)
                b.release(t3)
                b_ready[g] = split_to(b_op[:, g, 0, :], b_op[:, g, 1, :], yn, p_col("out_gain", g), t3, *waits)
                s.release(b_ready[g])
            for x, g in enumerate(groups):
                later(1 + x, lambda x=x, g=g: one(x, g))

        for hd in range(HEADS):
            head1(hd)
        later(4 * HEADS + 14, lambda: normed_groups(list(range(HEADS))))
        conv = {}

        def finish_conv(j, what):
            def finish_edge(bank, done):
                s = work.take()
                y = s.ap[:, 0:CONV_TOK]
                t = dve.do(lambda e: e.tensor_tensor(y, bank.ap[:, 0:CONV_TOK], row[:, CONV], ALU.mult), done, *s.free)
                bank.release(t)
                if what == "gate_c":
                    conv["gc"] = (s, y, t)
                    return
                gs, gy, gt = conv["gc"]
                t = pool.do(lambda e: e.tensor_tensor(y, y, gy, ALU.mult), t, gt)
                gs.release(t)
                o = work.take()
                u = o.ap[:, 0:SEQ]
                t = dve.do(lambda e: e.tensor_scalar(u, y[:, 0:SEQ], p_col("conv_w", j), None, ALU.mult), t, *o.free)
                for tap in (1, 2):
                    t = dve.do(lambda e, tap=tap: e.scalar_tensor_tensor(
                        u, y[:, tap:tap + SEQ], p_col("conv_w", 8 * tap + j), u, ALU.mult, ALU.add), t)
                s.release(t)
                conv["u"] = (o, u, t)

            def finish_b(bank, done):
                s, y, t = joined(bank, done)
                t = pool.do(lambda e: e.tensor_tensor(y, y, row[:, REAL], ALU.mult), t)
                o, u, ut = conv["u"]
                g = HEADS + j
                y_ready[g] = pool.do(lambda e: e.tensor_tensor(ytile[:, g, :], y, u, ALU.mult), t, ut)
                s.release(y_ready[g])
                o.release(y_ready[g])
                group_square(g)
                if j in (3, 7):
                    later(5, lambda: normed_groups(list(range(g - 3, g + 1))))
            return (REAL, finish_b) if what == "gate_b" else (CONV, finish_edge)

        conv_tiles = [finish_conv(j, what) for j in range(8) for what in ("gate_c", "h", "gate_b")]
        for b in range(6):
            product(U, kt_plain, from_a, a_of, conv_tiles[4 * b:4 * b + 4])

        h_ready = {}

        def into_h(j, bank, done, first_scale=None):
            hr = h[:, j, REAL]
            old = (h_ready[j],) if j in h_ready else ()
            if first_scale is None:
                t = dve.do(lambda e: e.tensor_tensor(hr, hr, bank.ap[:, 0:SEQ], ALU.add), done, *old)
            else:
                t = dve.do(lambda e: e.scalar_tensor_tensor(hr, hr, first_scale, bank.ap[:, 0:SEQ],
                                                            ALU.mult, ALU.add), done, *old)
            t = dve.do(lambda e: e.tensor_tensor(hr, hr, bank.ap[:, SEQ:2 * SEQ], ALU.add), t)
            bank.release(t)
            h_ready[j] = t
            return t

        def finish_norm_tile(j, gain, row_starts, waits_a):
            def run(t):
                a_ready[j] = split_to(a_op[:, j, 0, REAL], a_op[:, j, 1, REAL], h[:, j, REAL],
                                      p_col(gain, j), t, waits_a)
                add_square(h[:, j, REAL], j == 0, acc[:, REAL], t)
                if j == KT - 1:
                    def rows():
                        row_ready[0] = rms_rows_real(acc_ready[0])
                    later(2, rows)
            return run

        def rms_rows_real(*waits):
            bank, ty = side_banks.take(), tiny.take()
            t = sums_to_rows(bank, 0, acc, (META, META + P), *waits)
            ms, y, z = ty.ap[:, 0, 0:2], ty.ap[:, 1, 0:2], ty.ap[:, 2, 0:2]
            t = dve.do(lambda e: e.tensor_scalar(ms, bank.ap[:, 0:2], 1.0 / D, RMS_EPS, ALU.mult, ALU.add),
                       t, *ty.free)
            bank.release(t)
            t = rsqrt(ms, y, z, t)
            b2 = side_banks.take()
            t = rows_to_bank(b2, [ty.ap[:, 1, i:i + 1] for i in range(2)], (0, P), 0, t)
            ty.release(dve.now())
            t = act.do(lambda e: e.copy(row[:, REAL], b2.ap[:, 0:SEQ]), t, dve.now(), pool.now())
            b2.release(t)
            return t

        b_of = lambda kt: (b_ready[kt],)

        a_free = pe.now()

        def finish_w_out(j):
            run = finish_norm_tile(j, "norm_ffn", None, a_free)
            return REAL, lambda bank, done: run(into_h(j, bank, done))

        late = {g: None for g in range(KT)}

        def b_of_late(kt):
            while kt not in b_ready:
                step()
            return (b_ready[kt],)
        for b in range(4):
            product(U, kt_plain, from_b, b_of_late, [finish_w_out(4 * b + i) for i in range(4)])

        def finish_gate_up(slot, what, keep, b_free):
            def finish(bank, done):
                while row_ready[0] is None:
                    step()
                s, y, t = joined(bank, done)
                t = dve.do(lambda e: e.tensor_tensor(y, y, row[:, REAL], ALU.mult), t, row_ready[0])
                if what == "gate":
                    keep["g"] = (s, y, act.do(lambda e: e.activation(y, y, ACT.Silu), t))
                    return
                gs, gy, gt = keep["g"]
                t = dve.do(lambda e: e.tensor_tensor(y, y, gy, ALU.mult), t, gt)
                gs.release(t)
                b_ready[slot] = split_to(b_op[:, slot, 0, :], b_op[:, slot, 1, :], y, None, t, b_free)
                s.release(b_ready[slot])
            return REAL, finish

        row_ready[0] = None
        keep = {}
        base = 0
        for gi, n in enumerate(GROUPS1):
            b_free = pe.now()
            for b in range(n // 2):
                tiles = [finish_gate_up(2 * b + x // 2, ("gate", "up")[x % 2], keep, b_free) for x in range(4)]
                product(U, kt_plain, from_a, a_of, tiles)
            a_free = pe.now()
            last = gi == len(GROUPS1) - 1

            def finish_down(j):
                if not last:
                    return REAL, lambda bank, done: into_h(j, bank, done)
                run = finish_norm_tile(j, "final_norm", None, a_free)
                return REAL, lambda bank, done: run(into_h(j, bank, done))
            if last:
                row_ready[0] = None
            for b in range(4):
                product(n // UNIT_K, kt_plain, from_b, b_of, [finish_down(4 * b + i) for i in range(4)])
            base += n

        def angles():
            s1, s2, s3 = work.take(), work.take(), work.take()
            ang, n, r = (s.ap[:, 0:SEQ] for s in (s1, s2, s3))
            freq, sign = con[:, C_FREQ:C_FREQ + 1], con[:, C_SIGN:C_SIGN + 1]
            got = sp.load(lambda e: e.dma_start(n.bitcast(I32), positions), s_pos, 16, *s2.free)
            t = dve.do(lambda e: e.tensor_copy(ang, n.bitcast(I32)), got, *s1.free)
            t = dve.do(lambda e: e.tensor_scalar(ang, ang, freq, None, ALU.mult), t)
            t = dve.do(lambda e: e.tensor_scalar(r.bitcast(I32), ang, 1.0 / (2.0 * np.pi), None, ALU.mult), t, *s3.free)
            t = dve.do(lambda e: e.tensor_copy(n, r.bitcast(I32)), t)
            part1 = 6.28125
            part2 = float(np.float32(np.round((2 * np.pi - part1) * 2.0 ** 21) / 2.0 ** 21))
            part3 = float(np.float32(2 * np.pi - part1 - part2))
            for c in (part1, part2, part3):
                t = dve.do(lambda e, c=c: e.scalar_tensor_tensor(ang, n, -c, ang, ALU.mult, ALU.add), t)
            t = dve.do(lambda e: e.tensor_scalar(ang, ang, float(np.float32(3.1415925)), float(np.float32(-3.1415925)),
                                                 ALU.min, ALU.max), t)
            ts = act.do(lambda e: e.activation(r, ang, ACT.Sin), t)
            t2 = act.do(lambda e: e.activation(ang, ang, ACT.Abs), ts)
            t2 = dve.do(lambda e: e.tensor_scalar(ang, ang, -1.0, float(np.pi / 2), ALU.mult, ALU.add), t2)
            t2 = act.do(lambda e: e.activation(n, ang, ACT.Sin), t2)
            state = (s1, s2, s3, n, r, ts, t2, sign)

            def scaled():
                while row_ready[0] is None:
                    step()
                a = dve.do(lambda e: e.tensor_tensor(cosr[:, :], n, row[:, REAL], ALU.mult), t2, row_ready[0])
                b = dve.do(lambda e: e.scalar_tensor_tensor(sinr[:, :], r, sign, row[:, REAL], ALU.mult, ALU.mult), ts)
                s1.release(b)
                s2.release(b)
                s3.release(b)
                return b
            return scaled

        scaled = angles()
        got_mask2 = sp.load(lambda e: e.dma_start(masks[:, :], mask2), s_mask, 32, dve.now())
        rope_ready = [None]

        def finish_rope(dst, hd, book):
            def finish(bank, done):
                if rope_ready[0] is None:
                    rope_ready[0] = scaled()
                s, y, t = joined(bank, done)
                o = work.take()
                w_ = o.ap[:, 0:SEQ]
                act.quiet(lambda e: e.copy(w_[0:64, :], y[64:128, :]), t, *o.free)
                t2 = act.do(lambda e: e.copy(w_[64:128, :], y[0:64, :]))
                t3 = dve.do(lambda e: e.tensor_tensor(y, y, cosr[:, :], ALU.mult), t2, rope_ready[0])
                t2 = pool.do(lambda e: e.tensor_tensor(w_, w_, sinr[:, :], ALU.mult), t2, rope_ready[0])
                book[hd] = pool.do(lambda e: e.tensor_tensor(dst[:, hd, 0:SEQ], y, w_, ALU.add), t2, t3)
                s.release(book[hd])
                o.release(book[hd])
            return REAL, finish

        def finish_v2(hd):
            def finish(bank, done):
                s, y, t = joined(bank, done)
                t = dve.do(lambda e: e.tensor_tensor(y, y, row[:, REAL], ALU.mult), t, row_ready[0])
                later(2, lambda: to_v(hd, s, y, t, 2, 0))
            return REAL, finish

        for b in range(2):
            product(U, kt_plain, from_a, a_of, [finish_rope(k, 4 * b + i, k_ready) for i in range(4)])
        for b in range(2):
            product(U, kt_plain, from_a, a_of, [finish_rope(q, 4 * b + i, q_ready) for i in range(4)])

        def residual(j):
            t = dve.do(lambda e: e.scalar_tensor_tensor(h[:, j, REAL], h[:, j, REAL], p_col("final_norm", j),
                                                        row[:, REAL], ALU.mult, ALU.mult),
                       row_ready[0], h_ready[j], a_ready[j], act.now())
            h_ready[j] = t
        for j in range(KT):
            later(1 + 2 * j, lambda j=j: residual(j))
        for b in range(2):
            product(U, kt_plain, from_a, a_of, [finish_v2(4 * b + i) for i in range(4)])
        flush()

        def head2(hd):
            state = {}
            cols = (0, KEYS2[0])
            spans = ((0, KEYS2[0]), (KEYS2[0], KEYS2[1]))

            def scores():
                b, s = side_banks.take(), prob_ring.take()
                for i in range(2):
                    n, o = KEYS2[i], cols[i]
                    t = pe.do(lambda e, i=i, n=n, o=o: e.matmul(
                        b.ap[:, o:o + n], q[:, hd, i * P:(i + 1) * P], k[:, hd, 0:n], start=True, stop=True),
                        q_ready[hd], k_ready[hd], *b.free)
                t = dve.do(lambda e: e.scalar_tensor_tensor(s.ap[:, 0:P + SEQ], b.ap[:, 0:P + SEQ], SCALE,
                                                            masks[:, 0:P + SEQ], ALU.mult, ALU.add),
                           t, got_mask2, *s.free)
                b.release(t)
                counts = [masks[:, P + SEQ + a:P + SEQ + a + n] for a, n in spans]
                state.update(s=s, t=softmax(s, spans, t, counts))

            def turn():
                s, t = state["s"], state["t"]
                bt = side_banks.take()
                for x, a in enumerate((0, P, 2 * P)):
                    t2 = pe.do(lambda e, a=a: e.transpose(bt.ap[:, a:a + P], s.ap[:, a:a + P], ident), t, *bt.free)
                s.release(t2)
                f = act.do(lambda e: e.copy(probs_t[:, 0:3 * P], bt.ap[:, 0:3 * P]), t2, *probs_t_free[0])
                bt.release(f)
                state["t"] = f

            def values():
                bo = side_banks.take()
                hs = slice(hd * P, (hd + 1) * P)
                pe.quiet(lambda e: e.matmul(bo.ap[:, 0:SEQ], v[:, 0, hs], probs_t[:, 0:SEQ], start=True, stop=False,
                                            skip_group_check=True), state["t"], v_ready[hd], *bo.free)
                t = pe.do(lambda e: e.matmul(bo.ap[:, P:SEQ], v[:, 1, hs], probs_t[:, SEQ:3 * P], start=False,
                                             stop=True, skip_group_check=True))
                probs_t_free[0] = (t,)
                s = work.take()
                y = s.ap[:, 0:SEQ]
                f = act.do(lambda e: e.copy(y, bo.ap[:, 0:SEQ]), t, *s.free)
                bo.release(f)
                b_ready[hd] = split_to(b_op[:, hd, 0, :], b_op[:, hd, 1, :], y, None, f, b_free)
                s.release(b_ready[hd])

            later(4 * hd + 1, scores)
            later(4 * hd + 6, turn)
            later(4 * hd + 9, values)

        b_free = pe.now()
        for hd in range(HEADS):
            head2(hd)

        pool_ready = {}

        def finish_u(j):
            g = j // 2
            win = POOL_WINDOWS[g]

            def finish(bank, done):
                s, y, t = joined(bank, done)
                x = work.take()
                tz = pool.do(lambda e: e.memset(x.ap[:, 0:META], 0.0), *x.free)
                t = dve.do(lambda e: e.tensor_tensor(x.ap[:, REAL], y, row[:, REAL], ALU.mult), t, *x.free)
                s.release(t)
                src, lo, span, t = x, 0, 1, (t, tz)
                while span < win:
                    lo += span
                    o = work.take()
                    t = (pool.do(lambda e, o=o, src=src, lo=lo, span=span: e.tensor_tensor(
                        o.ap[:, lo:TOK], src.ap[:, lo:TOK], src.ap[:, lo - span:TOK - span], ALU.add), *t, *o.free),)
                    if src is not x:
                        src.release(*t)
                    src, span = o, 2 * span
                dst = ytile[:, 8 + j, :]
                ramp = con[:, C_RAMP + 16 * g:C_RAMP + 16 * (g + 1)]
                t1 = dve.do(lambda e: e.scalar_tensor_tensor(dst, src.ap[:, REAL], 1.0 / win, x.ap[:, REAL],
                                                             ALU.mult, ALU.subtract), *t)
                t2 = dve.do(lambda e: e.tensor_tensor(src.ap[:, META:2 * META], src.ap[:, META:2 * META], ramp, ALU.mult), t1)
                pool_ready[j] = dve.do(lambda e: e.tensor_tensor(dst[:, 0:META], src.ap[:, META:2 * META],
                                                                 x.ap[:, META:2 * META], ALU.subtract), t2)
                src.release(pool_ready[j])
                x.release(pool_ready[j])
            return REAL, finish

        for b in range(2):
            product(U, kt_plain, from_a, a_of, [finish_u(4 * b + i) for i in range(4)])

        sig_ready, merged_ready = {}, {}

        def finish_gate(slot, *waits):
            def finish(bank, done):
                s, y, t = joined(bank, done)
                t = dve.do(lambda e: e.tensor_tensor(y, y, row[:, REAL], ALU.mult), t)
                sig_ready[slot] = act.do(lambda e: e.activation(ytile[:, slot, :], y, ACT.Sigmoid), t, *waits)
                s.release(sig_ready[slot])
            return REAL, finish

        product(U, kt_plain, from_a, a_of, [finish_gate(i) for i in range(4)])
        product(U, kt_plain, from_a, a_of, [finish_gate(4 + i) for i in range(4)])

        n0 = unit_at[0]
        for half in range(2):
            n = n0 + half
            for g in (2 * half, 2 * half + 1):
                for m in range(2):
                    bank = out_banks.take()
                    for kt in range(2):
                        at = (g % 2) * 512 + kt * 256 + m * P
                        t = pe.do(lambda e, n=n, at=at, g=g, kt=kt, bank=bank: e.matmul(
                            bank.ap[:, 0:SEQ], raw[:, n % RAW, at:at + P], ytile[:, 8 + 2 * g + kt, :],
                            start=(kt == 0), stop=(kt == 1)), landed[n], pool_ready[2 * g + kt], *bank.free)
                    j = 2 * g + m
                    s = work.take()
                    y = s.ap[:, 0:SEQ]
                    f = act.do(lambda e, y=y, bank=bank: e.copy(y, bank.ap[:, 0:SEQ]), t, *s.free)
                    bank.release(f)
                    b_ready[8 + j] = split_to(b_op[:, 8 + j, 0, :], b_op[:, 8 + j, 1, :], y,
                                              p_col("pool_scale", j), f, b_free)
                    s.release(b_ready[8 + j])
            raw_free[n % RAW] = (t,)
            split_next += 1
            load_units(n + RAW + 1)
        unit_at[0] += 2
        pooled = pe.now()
        product(U, kt_plain, from_a, a_of, [finish_gate(8 + i, pooled) for i in range(4)])
        product(U, kt_plain, from_a, a_of, [finish_gate(12 + i) for i in range(4)])
        flush()
        attended = pe.now()

        def branches(b, base, to_a):
            def attn(i):
                def finish(bank, done):
                    s, y, t = joined(bank, done)
                    sg = ytile[:, base + i, :]
                    sig_ready[base + i] = pool.do(lambda e: e.tensor_tensor(sg, sg, y, ALU.mult), t, sig_ready[base + i])
                    s.release(sig_ready[base + i])
                return REAL, finish

            def pooled_(i):
                j = 4 * b + i

                def finish(bank, done):
                    s, y, t = joined(bank, done)
                    t = dve.do(lambda e: e.tensor_tensor(y, y, ytile[:, base + 4 + i, :], ALU.mult), t,
                               sig_ready[base + 4 + i])
                    if to_a is None:
                        merged_ready[j] = pool.do(lambda e: e.tensor_tensor(q[:, j, :], y, ytile[:, base + i, :], ALU.add),
                                                  t, sig_ready[base + i], attended)
                        s.release(merged_ready[j])
                        return
                    t = pool.do(lambda e: e.tensor_tensor(y, y, ytile[:, base + i, :], ALU.add), t, sig_ready[base + i])
                    merged_ready[j] = t
                    a_ready[j] = split_to(a_op[:, j, 0, REAL], a_op[:, j, 1, REAL], y, None, t, to_a)
                    s.release(a_ready[j])
                return REAL, finish
            product(4, kt_plain, from_b, b_of, [attn(i) for i in range(4)])
            product(4, lambda n, i: 8 + UNIT_K * n + i, from_b, b_of, [pooled_(i) for i in range(4)])

        branches(0, 0, None)
        branches(1, 8, None)
        for x in range(4):
            base = (0, 4, 8, 12)[x]
            product(U, kt_plain, from_a, a_of, [finish_gate(base + i, pool.now(), dve.now()) for i in range(4)])
        a_free = pe.now()
        for j in range(8):
            a_ready[j] = None

        def late_split(j):
            a_ready[j] = split_to(a_op[:, j, 0, REAL], a_op[:, j, 1, REAL], q[:, j, :], None, merged_ready[j], a_free)
        for j in range(8):
            later(1 + j, lambda j=j: late_split(j))
        branches(2, 0, a_free)
        branches(3, 8, a_free)
        flush()

        HALF = KT // 2
        shift_ready = [None]
        sum_ready = [None, None]

        def centre(j, first):
            hr = h[:, j, REAL]
            t = dve.do(lambda e: e.tensor_tensor(hr, hr, shift[:, :], ALU.subtract), h_ready[j], shift_ready[0],
                       pool.now())
            h_ready[j] = t
            if first:
                sum_ready[0] = dve.do(lambda e: e.tensor_copy(acc[:, REAL], hr), t, pool.now(), pe.now())
                sum_ready[1] = act.do(lambda e: e.activation(acc2[:, :], hr, ACT.Square), t, pe.now(), pool.now())
                return
            s = work.take()
            t2 = act.do(lambda e: e.activation(s.ap[:, 0:SEQ], hr, ACT.Square), t, *s.free)
            sum_ready[0] = pool.do(lambda e: e.tensor_tensor(acc[:, REAL], acc[:, REAL], hr, ALU.add), t, sum_ready[0])
            sum_ready[1] = pool.do(lambda e: e.tensor_tensor(acc2[:, :], acc2[:, :], s.ap[:, 0:SEQ], ALU.add),
                                   t2, sum_ready[1])
            s.release(sum_ready[1])

        def norm_tile(j):
            if j < HALF:
                hr = h[:, j, REAL]
                if j == 0:
                    sum_ready[0] = dve.do(lambda e: e.tensor_copy(acc[:, REAL], hr), h_ready[j], pool.now(), pe.now())
                else:
                    sum_ready[0] = pool.do(lambda e: e.tensor_tensor(acc[:, REAL], acc[:, REAL], hr, ALU.add),
                                           h_ready[j], sum_ready[0])
                if j == HALF - 1:
                    def mean():
                        b = side_banks.take()
                        t = pe.do(lambda e: e.matmul(b.ap[:, 0:SEQ], ones[:, :], acc[:, REAL], start=True, stop=True),
                                  sum_ready[0], *b.free)
                        shift_ready[0] = act.do(lambda e: e.activation(shift[:, :], b.ap[:, 0:SEQ], ACT.Copy,
                                                                       scale=1.0 / (HALF * P)), t, dve.now(), pool.now())
                        b.release(shift_ready[0])
                        centre(0, True)
                    later(2, mean)
                return
            while shift_ready[0] is None:
                step()
            centre(j, False)
            for x in {8: (1, 2), 9: (3, 4), 10: (5, 6), 11: (7,)}.get(j, ()):
                centre(x, False)

        def norm_rows():
            bank, ty = side_banks.take(), tiny.take()
            d, m2, y, z, o = (ty.ap[:, i, 0:2] for i in range(5))
            t = sums_to_rows(bank, 0, acc, (META, META + P), sum_ready[0])
            t2 = sums_to_rows(bank, 2, acc2, (0, P), sum_ready[1])
            t = dve.do(lambda e: e.tensor_scalar(d, bank.ap[:, 0:2], 1.0 / D, None, ALU.mult), t2, *ty.free)
            t1 = dve.do(lambda e: e.tensor_scalar(m2, bank.ap[:, 2:4], 1.0 / D, LN_EPS, ALU.mult, ALU.add))
            bank.release(t1)
            t = dve.do(lambda e: e.tensor_tensor(z, d, d, ALU.mult), t)
            t = dve.do(lambda e: e.tensor_tensor(m2, m2, z, ALU.subtract), t, t1)
            t = rsqrt(m2, y, z, t)
            t = dve.do(lambda e: e.scalar_tensor_tensor(o, d, -1.0, y, ALU.mult, ALU.mult), t)
            b2 = side_banks.take()
            rows_to_bank(b2, [ty.ap[:, 2, i:i + 1] for i in range(2)], (0, P), 0, t)
            t = rows_to_bank(b2, [ty.ap[:, 4, i:i + 1] for i in range(2)], (0, P), SEQ, t)
            ty.release(dve.now())
            f = act.do(lambda e: e.copy(row[:, REAL], b2.ap[:, 0:SEQ]), t, dve.now(), pool.now())
            g = act.do(lambda e: e.copy(shift[:, :], b2.ap[:, SEQ:2 * SEQ]), t)
            b2.release(g)
            return g

        def normed_tile(j, gain, bias, ready):
            hr = h[:, j, REAL]
            t = dve.do(lambda e: e.tensor_tensor(hr, hr, row[:, REAL], ALU.mult), h_ready[j], ready, *sum_ready)
            t = dve.do(lambda e: e.tensor_tensor(hr, hr, shift[:, :], ALU.add), t)
            h_ready[j] = act.do(lambda e: e.activation(hr, hr, ACT.Identity, scale=p_col(gain, j), bias=p_col(bias, j)), t)
            return h_ready[j]

        def finish_mix(j):
            def finish(bank, done):
                into_h(j, bank, done, ALPHA)
                norm_tile(j)
            return REAL, finish

        for b in range(4):
            product(U, kt_plain, from_a, a_of, [finish_mix(4 * b + i) for i in range(4)])
        a_free = pe.now()
        flush()
        ready = norm_rows()
        for j in range(KT):
            t = normed_tile(j, "ln_mix_g", "ln_mix_b", ready)
            a_ready[j] = split_to(a_op[:, j, 0, REAL], a_op[:, j, 1, REAL], h[:, j, REAL], None, t, a_free)

        shift_ready[0] = None

        def finish_ff1(slot, b_free):
            def finish(bank, done):
                s, y, t = joined(bank, done)
                t = dve.do(lambda e: e.tensor_scalar(y, y, 0.0, None, ALU.max), t)
                t = pool.do(lambda e: e.tensor_tensor(y, y, y, ALU.mult), t)
                b_ready[slot] = split_to(b_op[:, slot, 0, :], b_op[:, slot, 1, :], y, None, t, b_free)
                s.release(b_ready[slot])
            return REAL, finish

        for gi, n in enumerate(GROUPS2):
            b_free = pe.now()
            for b in range(n // BLOCK):
                product(U, kt_plain, from_a, a_of, [finish_ff1(BLOCK * b + i, b_free) for i in range(4)])

            def finish_ff2(j, gi=gi):
                def finish(bank, done):
                    into_h(j, bank, done, ALPHA if gi == 0 else None)
                    if gi == len(GROUPS2) - 1:
                        norm_tile(j)
                return REAL, finish
            for b in range(4):
                product(n // UNIT_K, kt_plain, from_b, b_of, [finish_ff2(4 * b + i) for i in range(4)])
        flush()

        ready = norm_rows()
        stored = 0
        for j in range(KT):
            normed_tile(j, "ln_ff_g", "ln_ff_b", ready)
            if j % 2 == 1:
                stored += 16
                sp.load(lambda e, j=j: e.dma_start(out[:, j - 1:j + 1, :], h[:, j - 1:j + 1, REAL]), s_out, stored,
                        h_ready[j])
        assert unit_at[0] == len(order)
        sp.wait(Ticket(s_out, stored))

        block = ctx.enter_context(nc.Block())
        block.sync(sp.play)
        block.tensor(pe.play)
        block.scalar(act.play)
        block.vector(dve.play)
        block.gpsimd(pool.play)



def pack_weight(m, tiles=None):
    rows, cols = m.shape
    m = m.reshape(rows // (UNIT_K * P), UNIT_K, P, cols // P, P)
    if tiles is not None:
        m = m[:, :, :, tiles, :]
    m = m.reshape(rows // (UNIT_K * P), UNIT_K, P, cols // (BLOCK * P), BLOCK * P)
    m = m.transpose(3, 0, 2, 1, 4)
    return np.ascontiguousarray(m).reshape(m.shape[0], m.shape[1], P, UNIT)


def feature_columns(vec):
    return vec.reshape(-1, P).T


def shape_constants():
    con = np.zeros((P, N_CONST), np.float32)
    con[:, C_IDENT:C_IDENT + P] = np.eye(P, dtype=np.float32)
    half = P // 2
    freq = np.float32(10000.0) ** (-np.arange(half, dtype=np.float32) / np.float32(half))
    con[:, C_FREQ] = np.concatenate([freq, freq])
    con[:, C_SIGN] = np.concatenate([-np.ones(half), np.ones(half)])
    for g, win in enumerate(POOL_WINDOWS):
        con[:, C_RAMP + 16 * g:C_RAMP + 16 * (g + 1)] = 1.0 / np.minimum(np.arange(1, 17), win)
    rows = np.arange(P)[:, None]
    mask1 = np.concatenate([np.where(np.arange(n)[None] <= META + i * P + rows, 0.0, NEG)
                            for i, n in enumerate(KEYS1)], axis=1).astype(np.float32)
    count = []
    for i, n in enumerate(KEYS2):
        dist = i * P + rows - np.arange(n)[None]
        count.append(sum(((dist >= 0) & (dist <= span * dil) & (dist % dil == 0)).astype(np.float32)
                         for span, dil in ((128, 1), (128, 4), (128, 16))))
    count = np.concatenate(count, axis=1)
    mask2 = np.concatenate([np.where(count > 0, 0.0, NEG), count], axis=1).astype(np.float32)
    return con, mask1, mask2


def kernel(**inputs):
    import concourse.bacc as bacc
    from concourse.bass_utils import run_bass_kernel_spmd

    a = {n: np.asarray(x) for n, x in inputs.items()}
    w_in = a["w_in"][0]
    tiles1 = list(range(8, 16)) + list(range(0, 8)) + list(range(16, 24))
    for j in range(8):
        tiles1 += [32 + j, 40 + j, 24 + j]
    n_main = 48 * P
    w_f = np.zeros((D, P), w_in.dtype)
    w_f[:, 0:HEADS] = w_in[:, n_main:]
    w_f = np.ascontiguousarray(w_f.reshape(2, 8, P, P).transpose(0, 2, 1, 3)).reshape(1, 2, P, UNIT)
    gu = np.concatenate([a["w_gate"][0], a["w_up"][0]], axis=1)
    n_ff = D_FF1 // P
    tiles_gu = [x for j in range(n_ff) for x in (j, n_ff + j)]
    tiles2 = list(range(8, 16)) + list(range(0, 8)) + list(range(16, 32))
    for b in range(4):
        tiles2 += [32 + 4 * b + i for i in range(4)] + [48 + 4 * b + i for i in range(4)]
    w_pool = a["w_pool_2"][0].reshape(2, 2, 2, P, 256).transpose(0, 3, 1, 2, 4)
    weights = {
        "w_in": pack_weight(w_in[:, 0:n_main], tiles1),
        "w_f": w_f,
        "w_out": pack_weight(a["w_out"][0]),
        "w_gu": pack_weight(gu, tiles_gu),
        "w_down": pack_weight(a["w_down"][0]),
        "w_in_2": pack_weight(a["w_in_2"][0], tiles2),
        "w_pool": np.ascontiguousarray(w_pool).reshape(1, 2, P, UNIT),
        "w_ba": pack_weight(a["w_branch_attn_2"][0]),
        "w_bp": pack_weight(a["w_branch_pool_2"][0]),
        "w_out_2": pack_weight(a["w_out_2"][0]),
        "w_ff1": pack_weight(a["w_ff1_2"][0]),
        "w_ff2": pack_weight(a["w_ff2_2"][0]),
    }
    tokens = np.concatenate([a["meta"], a["x"][0]], axis=0).T.reshape(KT, P, TOK).transpose(1, 0, 2)
    params = np.zeros((P, N_PARAMS), np.float32)

    def put(name, cols):
        params[0:cols.shape[0], PARAMS[name]:PARAMS[name] + cols.shape[1]] = cols
    put("norm_mix", feature_columns(a["norm_mix"][0]))
    put("out_gain", feature_columns(a["out_gain"][0]))
    put("norm_ffn", feature_columns(a["norm_ffn"][0]))
    put("final_norm", feature_columns(a["final_norm"]))
    put("conv_w", feature_columns(a["conv_w"][0].reshape(-1)))
    put("pool_scale", feature_columns(a["pool_scale_2"][0]))
    put("ln_mix_g", feature_columns(a["ln_mix_g_2"][0]))
    put("ln_mix_b", feature_columns(a["ln_mix_b_2"][0]))
    put("ln_ff_g", feature_columns(a["ln_ff_g_2"][0]))
    put("ln_ff_b", feature_columns(a["ln_ff_b_2"][0]))
    put("b_f", a["b_f"][0].reshape(HEADS, 1))
    con, mask1, mask2 = shape_constants()
    positions = np.broadcast_to(a["positions_2"][0][None, :], (P, SEQ))

    arrays = {f"in_{n}": x for n, x in weights.items()}
    arrays |= {"in_tokens": tokens, "in_params": params, "in_consts": con, "in_mask1": mask1,
               "in_mask2": mask2, "in_positions": positions}
    arrays = {n: np.ascontiguousarray(x) for n, x in arrays.items()}
    nc = bacc.Bacc("TRN2", target_bir_lowering=False, num_devices=1)
    aps = {n: nc.dram_tensor(n, x.shape, mybir.dt.from_np(x.dtype), kind="ExternalInput").ap()
           for n, x in arrays.items()}
    out = nc.dram_tensor("out", (P, KT, SEQ), F32, kind="ExternalOutput").ap()
    two_blocks(nc, {n: aps[f"in_{n}"] for n in weights}, aps["in_tokens"], aps["in_params"], aps["in_consts"],
               aps["in_mask1"], aps["in_mask2"], aps["in_positions"], out)
    r = run_bass_kernel_spmd(nc, [arrays], core_ids=[0])
    got = r.results[0]["out"]
    return np.ascontiguousarray(got.transpose(2, 1, 0)).reshape(1, SEQ, D)
```

```python
from contextlib import ExitStack

import numpy as np

import concourse.bass as bass
from concourse import mybir

F32 = mybir.dt.float32
F32R = mybir.dt.float32r
I32 = mybir.dt.int32
ALU = mybir.AluOpType
ACT = mybir.ActivationFunctionType
AX_X = mybir.AxisListType.X

P = 128
D = 2048
KT = D // P
SEQ = 256
META = 16
TOK = META + SEQ
HEADS = 8
D_FF1 = 5632
D_FF2 = 8192
NEG = -1e30
RMS_EPS = 1e-6
LN_EPS = 1e-5
ALPHA = 2.0 ** 0.25
SCALE = float(P) ** -0.5

UNIT_K = 2
BLOCK = 4
UNIT = UNIT_K * BLOCK * P
RAW = 5
HEAD_STEPS = 16
SPLIT = 4
CONV_TOK = SEQ + 2
POOL_WINDOWS = (2, 4, 8, 16)

GROUPS1 = (8, 12, 12, 12)
GROUPS2 = (16, 16, 16, 16)

KEYS1 = (META + P, TOK)
KEYS2 = (P, SEQ)

PARAMS = {}
_at = 0
for _name, _n in (("norm_mix", KT), ("out_gain", KT), ("norm_ffn", KT), ("final_norm", KT),
                  ("conv_w", 24), ("pool_scale", 8), ("ln_mix_g", KT), ("ln_mix_b", KT),
                  ("ln_ff_g", KT), ("ln_ff_b", KT), ("b_f", 1)):
    PARAMS[_name] = _at
    _at += _n
N_PARAMS = _at

C_IDENT, C_FREQ, C_SIGN, C_RAMP = 0, P, P + 1, P + 2
N_CONST = C_RAMP + 4 * 16


class Ticket:

    def __init__(self, sem, value):
        self.sem, self.value = sem, value


class Engine:

    def __init__(self, sem):
        self.sem, self.count, self.steps = sem, 0, []

    def do(self, make, *waits):
        self.count += 1
        self.steps.append((waits, make, self.sem, 1))
        return Ticket(self.sem, self.count)

    def quiet(self, make, *waits):
        self.steps.append((waits, make, None, 0))

    def load(self, make, sem, value, *waits):
        self.steps.append((waits, make, sem, 16))
        return Ticket(sem, value)

    def wait(self, *waits):
        self.steps.append((waits, None, None, 0))

    def now(self):
        return Ticket(self.sem, self.count)

    def play(self, eng):
        reached = {}
        for waits, make, sem, by in self.steps:
            for t in waits:
                if t is not None and t.value > reached.get(id(t.sem), 0):
                    eng.wait_ge(t.sem, t.value)
                    reached[id(t.sem)] = t.value
            if make is not None:
                ins = make(eng)
                if sem is not None:
                    ins.then_inc(sem, by)


class Slot:
    def __init__(self, ap):
        self.ap, self.free, self.held, self.age = ap, (), False, 0

    def release(self, *tickets):
        self.free, self.held = tickets, False


class Ring:

    def __init__(self, aps):
        self.slots, self.turn = [Slot(a) for a in aps], 0

    def lend(self, aps, *free):
        lent = [Slot(a) for a in aps]
        for s in lent:
            s.free = free
        self.slots += lent
        return lent

    def take_back(self, lent):
        assert not any(s.held for s in lent)
        self.slots = [s for s in self.slots if s not in lent]
        return [t for s in lent for t in s.free]

    def take(self):
        free = [s for s in self.slots if not s.held]
        assert free, "no slot is free"
        s = min(free, key=lambda x: x.age)
        self.turn += 1
        s.age, s.held = self.turn, True
        return s


def two_blocks(nc, w, tokens, params, consts, mask1, mask2, positions, out):
    with ExitStack() as ctx:
        def sb(name, shape, dt=F32):
            return ctx.enter_context(nc.sbuf_tensor(name, shape, dt))

        def sem(name):
            return ctx.enter_context(nc.semaphore(name))

        h = sb("h", [P, KT, TOK])
        a_op = sb("a_op", [P, KT, 2, TOK], F32R)
        b_op = sb("b_op", [P, KT, 2, SEQ], F32R)
        raw = sb("raw", [P, RAW, UNIT])
        w_hi = sb("w_hi", [P, SPLIT, UNIT], F32R)
        w_lo = sb("w_lo", [P, SPLIT, UNIT], F32R)
        q = sb("q", [P, HEADS, SEQ])
        k = sb("k", [P, HEADS, TOK])
        v = sb("v", [P, 3, HEADS * P])
        ytile = sb("ytile", [P, KT, SEQ])
        probs = sb("probs", [P, 2, SEQ + TOK])
        probs_t = sb("probs_t", [P, 2 * SEQ])
        probs_t2 = sb("probs_t2", [META, P])
        con = sb("con", [P, N_CONST])
        masks = sb("masks", [P, 2 * (P + SEQ)])
        par = sb("par", [P, N_PARAMS])
        ones = sb("ones", [P, P])
        row = sb("row", [P, TOK])
        shift = sb("shift", [P, SEQ])
        turn_tab = sb("turn_tab", [P, 2 * SEQ])
        cosr, sinr = turn_tab[:, 0:SEQ], turn_tab[:, SEQ:2 * SEQ]
        acc = sb("acc", [P, TOK])
        acc2 = sb("acc2", [P, SEQ])
        csum = turn_tab[0:HEADS, 0:TOK]
        cneg = masks[0:HEADS, sum(KEYS1):sum(KEYS1) + TOK]
        cq = sb("cq", [P, 2, HEADS])
        gms = sb("gms", [P, KT, 2])
        work = Ring([sb(f"work{i}", [P, TOK])[:, :] for i in range(8)])
        tiny = Ring([sb(f"tiny{i}", [P, 6, 16])[:, :, :] for i in range(4)])
        prob_ring = Ring([probs[:, i, :] for i in range(2)])

        def psum(name):
            return ctx.enter_context(nc.psum_tensor(name, [P, 512], F32))

        out_banks = Ring([psum(f"out_bank{i}")[:, :] for i in range(6)])
        side_banks = Ring([psum(f"side_bank{i}")[:, :] for i in range(2)])

        sp = Engine(None)
        pe, act, dve, pool = (Engine(sem(f"{n}_done")) for n in ("pe", "act", "dve", "pool"))
        s_raw = [sem(f"raw_landed{i}") for i in range(RAW)]
        s_h = [sem(f"tokens_landed{i}") for i in range(KT // 2)]
        s_par, s_con, s_mask = sem("params_landed"), sem("consts_landed"), sem("masks_landed")
        s_pos, s_out = sem("positions_landed"), sem("outputs_stored")

        ident = con[:, C_IDENT:C_IDENT + P]

        def p_col(name, i):
            c = PARAMS[name] + i
            return par[:, c:c + 1]

        clock, asked = [0], [0]
        later_work = []

        def later(n, fn):
            asked[0] += 1
            later_work.append((clock[0] + n, asked[0], fn))

        def step():
            clock[0] += 1
            while later_work and min(later_work)[0] <= clock[0]:
                due = min(later_work)
                later_work.remove(due)
                due[2]()

        def staged(steps, gap=1):
            if next(steps, None) is not None:
                later(gap, lambda: staged(steps, gap))

        def need(book, key):
            while book.get(key) is None:
                assert later_work
                step()
            return (book[key],)

        def flush_until(book, n):
            for key in range(n):
                need(book, key)

        def flush():
            while later_work:
                step()

        order = []

        def stream(name, n_k, blocks, fine=True):
            order.extend((name, b, u, fine) for b in blocks for u in range(n_k // UNIT_K))

        stream("w_in", KT, [0])
        order.extend(("w_f", 0, u, True) for u in range(2))
        stream("w_in", KT, range(1, 12))
        stream("w_out", KT, range(4))
        base = 0
        for n in GROUPS1:
            stream("w_gu", KT, range(base // 2, (base + n) // 2))
            for b in range(4):
                order.extend(("w_down", b, base // UNIT_K + u, True) for u in range(n // UNIT_K))
            base += n
        stream("w_in_2", KT, range(10))
        order.extend(("w_pool", 0, u, False) for u in range(2))
        stream("w_in_2", KT, range(10, 12))
        for b in range(2):
            stream("w_ba", 8, [b])
            stream("w_bp", 8, [b])
        stream("w_in_2", KT, range(12, 16))
        for b in range(2, 4):
            stream("w_ba", 8, [b])
            stream("w_bp", 8, [b])
        stream("w_out_2", KT, range(4))
        base = 0
        for n in GROUPS2:
            stream("w_ff1", KT, range(base // 4, (base + n) // 4))
            for b in range(4):
                order.extend(("w_ff2", b, base // UNIT_K + u, True) for u in range(n // UNIT_K))
            base += n

        raw_free = [()] * RAW
        raw_read = set()
        split_free = [()] * SPLIT
        split_of = [n for n, x in enumerate(order) if x[3]]
        place = {n: i % SPLIT for i, n in enumerate(split_of)}
        after = dict(zip(split_of, split_of[SPLIT - 1:]))
        loaded, landed, hi_done, lo_done = 0, {}, {}, {}

        def load_units(limit=len(order)):
            nonlocal loaded
            while loaded < limit and (loaded < RAW or loaded - RAW in raw_read):
                name, b, u, _ = order[loaded]
                i = loaded % RAW
                src = w[name][b, u]
                landed[loaded] = sp.load(lambda e, i=i, src=src: e.dma_start(raw[:, i, :], src),
                                         s_raw[i], 16 * (loaded // RAW + 1), *raw_free[i])
                loaded += 1

        def raw_done(n, *readers):
            raw_free[n % RAW] = readers
            raw_read.add(n)
            load_units()

        def split_hi(n):
            if n is not None and n not in hi_done:
                i, j = n % RAW, place[n]
                hi_done[n] = act.do(lambda e: e.copy(w_hi[:, j, :], raw[:, i, :]), landed[n], *split_free[j])

        def split_lo(n):
            if n is not None and n not in lo_done:
                split_hi(n)
                i, j = n % RAW, place[n]
                lo_done[n] = dve.do(lambda e: e.tensor_tensor(
                    w_lo[:, j, :], raw[:, i, :], w_hi[:, j, :].bitcast(F32), ALU.subtract), hi_done[n])
                raw_done(n, hi_done[n], lo_done[n])

        unit_at = [0]

        def product(n_units, kt_of, moving, ready, tiles, width=P * BLOCK, tail=0):
            per_unit = UNIT // width
            n_tiles = width // P
            banks = [None] * n_tiles
            runs = [[n] for n in range(n_units - tail)]
            if tail:
                runs.append(list(range(n_units - tail, n_units)))
            for run in runs:
                first = unit_at[0]
                for x in range(len(run)):
                    split_lo(first + x)
                ahead = after.get(first)
                done_at = {}
                for t in range(n_tiles):
                    if t == 0:
                        split_hi(ahead)
                    if t == min(1, n_tiles - 1):
                        split_lo(ahead)
                    cols, finish = tiles[t]
                    n_col = cols.stop - cols.start
                    if run[0] == 0:
                        banks[t] = out_banks.take()
                    bank = banks[t]
                    for x, n in enumerate(run):
                        unit, j = first + x, place[first + x]
                        for i in range(per_unit):
                            start, stop = n == 0 and i == 0, n == n_units - 1 and i == per_unit - 1
                            kt = kt_of(n, i)
                            a_hi, a_lo, a_both = moving(kt, cols)
                            at = i * width + t * P
                            wh, wl = w_hi[:, j, at:at + P], w_lo[:, j, at:at + P]
                            waits = [lo_done[unit], *ready(kt)] + (list(bank.free) if start else [])
                            if n_col == SEQ:
                                mm = [(bank.ap[:, 0:2 * SEQ], wh, a_both), (bank.ap[:, 0:SEQ], wl, a_hi)]
                                if not start:
                                    mm.reverse()
                            else:
                                mm = [(bank.ap[:, 0:n_col], wh, a_hi), (bank.ap[:, 0:n_col], wh, a_lo),
                                      (bank.ap[:, 0:n_col], wl, a_hi)]
                            for y, (o, st, m) in enumerate(mm):
                                last = y == len(mm) - 1

                                def make(e, o=o, st=st, m=m, a=start and y == 0, z=stop and last):
                                    return e.matmul(o, st, m, start=a, stop=z, skip_group_check=True)
                                if last and (stop or (t == n_tiles - 1 and i == per_unit - 1)):
                                    done_at[n] = pe.do(make, *waits)
                                else:
                                    pe.quiet(make, *waits)
                    if run[-1] == n_units - 1:
                        staged(finish(bank, done_at[n_units - 1]))
                    step()
                for x, n in enumerate(run):
                    split_free[place[first + x]] = (done_at[n],)
                for x in range(1, len(run)):
                    split_lo(after.get(first + x))
                unit_at[0] += len(run)

        def from_a(kt, cols):
            return (a_op[:, kt, 0, cols], a_op[:, kt, 1, cols], a_op[:, kt, :, cols])

        def from_b(kt, cols):
            return (b_op[:, kt, 0, :], b_op[:, kt, 1, :], b_op[:, kt, :, :])

        REAL, ALL, CONV = slice(META, TOK), slice(0, TOK), slice(META - 2, TOK)

        def joined(bank, done):
            s = work.take()
            y = s.ap[:, 0:SEQ]
            t = act.do(lambda e: e.copy(y, bank.ap[:, SEQ:2 * SEQ]), done, *s.free)
            t = dve.do(lambda e: e.tensor_tensor(y, y, bank.ap[:, 0:SEQ], ALU.add), t)
            bank.release(t)
            return s, y, t

        def split_to(dst_hi, dst_lo, src, scale, *waits):
            if scale is None:
                t = act.do(lambda e: e.copy(dst_hi, src), *waits)
                return dve.do(lambda e: e.tensor_tensor(dst_lo, src, dst_hi.bitcast(F32), ALU.subtract), t)
            t = act.do(lambda e: e.activation(dst_hi, src, ACT.Copy, scale=scale), *waits)
            return dve.do(lambda e: e.scalar_tensor_tensor(
                dst_lo, src, scale, dst_hi.bitcast(F32), ALU.mult, ALU.subtract), t)

        def sums_to_rows(bank, col, src, starts, *waits):
            for n, s in enumerate(starts):
                t = pe.do(lambda e, n=n, s=s: e.matmul(bank.ap[:, col + n:col + n + 1], src[:, s:s + P],
                                                       ones[:, 0:1], start=True, stop=True),
                          *waits, *bank.free)
            return t

        def rsqrt(ms, y, scratch, *waits):
            t = dve.do(lambda e: e.reciprocal(scratch, ms), *waits)
            t = act.do(lambda e: e.activation(y, scratch, ACT.Sqrt), t)
            t = dve.do(lambda e: e.tensor_tensor(scratch, y, y, ALU.mult), t)
            t = dve.do(lambda e: e.tensor_tensor(scratch, scratch, ms, ALU.mult), t)
            t = dve.do(lambda e: e.tensor_scalar(scratch, scratch, -0.5, 1.5, ALU.mult, ALU.add), t)
            return dve.do(lambda e: e.tensor_tensor(y, y, scratch, ALU.mult), t)

        def diagonals(cols, *waits):
            got = []
            for x, col in enumerate(cols):
                if x % 2 == 0:
                    d = work.take()
                dg = d.ap[:, x % 2 * P:(x % 2 + 1) * P]
                t = dve.do(lambda e, col=col, dg=dg: e.tensor_scalar(dg, ident, col, None, ALU.mult),
                           *waits, *d.free)
                got.append((d, dg, t))
            return got

        def rows_to_bank(bank, diags, starts):
            for (d, dg, t), s in zip(diags, starts):
                t = pe.do(lambda e, dg=dg, s=s: e.matmul(bank.ap[:, s:s + P], ones[:, :], dg,
                                                         start=True, stop=True), t, *bank.free)
                d.release(t)
            return t

        row_ready = [None]

        def rms_rows(at, starts, *waits):
            bank, ty = side_banks.take(), tiny.take()
            n = len(starts)
            t = sums_to_rows(bank, 0, acc, starts, *waits)
            ms, y, z = ty.ap[:, 0, 0:n], ty.ap[:, 1, 0:n], ty.ap[:, 2, 0:n]
            t = dve.do(lambda e: e.tensor_scalar(ms, bank.ap[:, 0:n], 1.0 / D, RMS_EPS, ALU.mult, ALU.add),
                       t, *ty.free)
            bank.release(t)
            t = rsqrt(ms, y, z, t)
            yield True
            dg = diagonals([ty.ap[:, 1, i:i + 1] for i in range(n)], t)
            ty.release(dve.now())
            yield True
            spread = side_banks.take()
            t = rows_to_bank(spread, dg, [s - at for s in starts])
            row_ready[0] = act.do(lambda e: e.copy(row[:, at:TOK], spread.ap[:, 0:TOK - at]),
                                  t, dve.now(), pool.now())
            spread.release(row_ready[0])

        acc_ready = [None]

        def add_square(src, first, dst, *waits, on_dve=False):
            n = src.shape[-1]
            if first:
                acc_ready[0] = act.do(lambda e: e.activation(dst, src, ACT.Square), *waits, pe.now(), pool.now())
                return
            s = work.take()
            if on_dve:
                t = dve.do(lambda e: e.tensor_tensor(s.ap[:, 0:n], src, src, ALU.mult), *waits, *s.free)
            else:
                t = act.do(lambda e: e.activation(s.ap[:, 0:n], src, ACT.Square), *waits, *s.free)
            acc_ready[0] = pool.do(lambda e: e.tensor_tensor(dst, dst, s.ap[:, 0:n], ALU.add),
                                   t, acc_ready[0])
            s.release(acc_ready[0])

        got_h = []

        def load_h(i):
            got_h.append(sp.load(lambda e: e.dma_start(h[:, 2 * i:2 * i + 2, :], tokens[:, 2 * i:2 * i + 2, :]),
                                 s_h[i], 16))
        load_units(1)
        load_h(0)
        got_par = sp.load(lambda e: e.dma_start(par[:, :], params), s_par, 16)
        load_units(2)
        load_h(1)
        load_units(3)
        load_h(2)
        load_units()
        for i in range(3, KT // 2):
            load_h(i)
        got_con = sp.load(lambda e: e.dma_start(con[:, :], consts), s_con, 16)
        got_mask = sp.load(lambda e: e.dma_start(masks[:, 0:sum(KEYS1)], mask1), s_mask, 16)
        made_ones = pool.do(lambda e: e.memset(ones[:, :], 1.0))
        cleared = pool.do(lambda e: e.memset(probs[:, :, :], 0.0))

        a_ready = {}

        def first_operand(kt):
            a_ready[kt] = split_to(a_op[:, kt, 0, :], a_op[:, kt, 1, :], h[:, kt, :], p_col("norm_mix", kt),
                                   got_h[kt // 2], got_par)

        def first_square(kt):
            add_square(h[:, kt, :], kt == 0, acc[:, :], got_h[kt // 2], on_dve=kt % 2 == 1)
        split_lo(0)
        first_operand(0)
        first_operand(1)
        split_lo(1)
        first_operand(2)
        first_operand(3)
        split_lo(2)
        for kt in range(4, KT):
            later(2 * kt - 7, lambda kt=kt: first_operand(kt))
        for kt in range(KT):
            later(5 * kt // 4, lambda kt=kt: first_square(kt))
        later(24, lambda: staged(rms_rows(0, (0, P, TOK - P), acc_ready[0], made_ones, got_con), 3))

        a_of = lambda kt: need(a_ready, kt)

        q_ready, k_ready, v_ready = {}, {}, {}

        def finish_k(hd):
            def finish(bank, done):
                while row_ready[0] is None:
                    yield True
                k_ready[hd] = dve.do(lambda e: e.tensor_tensor(k[:, hd, :], bank.ap[:, 0:TOK], row[:, :], ALU.mult),
                                     done, row_ready[0])
                bank.release(k_ready[hd])
                yield
            return ALL, finish

        def finish_q(hd):
            def finish(bank, done):
                s, y, t = joined(bank, done)
                yield True
                q_ready[hd] = dve.do(lambda e: e.scalar_tensor_tensor(
                    q[:, hd, :], y, SCALE, row[:, REAL], ALU.mult, ALU.mult), t, row_ready[0])
                s.release(q_ready[hd])
            return REAL, finish

        def to_v(hd, src_slot, src, t, n_full, rest):
            bank = side_banks.take()
            for n in range(n_full):
                t2 = pe.do(lambda e, n=n: e.transpose(bank.ap[:, n * P:(n + 1) * P], src[:, n * P:(n + 1) * P], ident),
                           t, got_con, *bank.free)
            if rest:
                t2 = pe.do(lambda e: e.transpose(bank.ap[0:rest, n_full * P:(n_full + 1) * P],
                                                 src[:, n_full * P:n_full * P + rest], ident))
            src_slot.release(t2)
            f = act.do(lambda e: e.copy(v[:, 0:n_full, hd * P:(hd + 1) * P],
                                        bank.ap[:, 0:n_full * P].rearrange("p (n d) -> p n d", d=P)), t2)
            if rest:
                f = act.do(lambda e: e.copy(v[0:rest, n_full, hd * P:(hd + 1) * P],
                                            bank.ap[0:rest, n_full * P:(n_full + 1) * P]), t2)
            bank.release(f)
            v_ready[hd] = f

        def finish_v(hd):
            def finish(bank, done):
                s = work.take()
                t = dve.do(lambda e: e.tensor_tensor(s.ap, bank.ap[:, 0:TOK], row[:, :], ALU.mult),
                           done, row_ready[0], *s.free)
                bank.release(t)
                yield True
                yield True
                to_v(hd, s, s.ap, t, 2, META)
            return ALL, finish

        c_ready = [None]
        H8 = slice(0, HEADS)

        def finish_f(bank, done):
            s1, s2, s3 = work.take(), work.take(), work.take()
            z, e1, m = s1.ap[H8, :], s2.ap[H8, :], s3.ap[H8, :]
            bf = par[H8, PARAMS["b_f"]:PARAMS["b_f"] + 1]
            t = dve.do(lambda e: e.tensor_tensor(z, bank.ap[H8, 0:TOK], row[H8, :], ALU.mult),
                       done, row_ready[0], *s1.free)
            bank.release(t)
            t = dve.do(lambda e: e.tensor_scalar(z, z, bf, None, ALU.add), t)
            ta = act.do(lambda e: e.activation(e1, z, ACT.Abs), t, *s2.free)
            ta = act.do(lambda e: e.activation(e1, e1, ACT.Exp, scale=-1.0), ta)
            ta = act.do(lambda e: e.activation(e1, e1, ACT.Ln, bias=1.0), ta)
            t = dve.do(lambda e: e.tensor_scalar(z, z, 0.0, None, ALU.min), ta)
            t = dve.do(lambda e: e.tensor_tensor(z, z, e1, ALU.subtract), t)
            t2 = dve.do(lambda e: e.memset(m, 1.0), *s3.free)
            t = dve.do(lambda e: e.tensor_tensor_scan(csum, m, z, 0.0, ALU.mult, ALU.add), t, t2)
            s1.release(t)
            s2.release(t)
            s3.release(t)
            t = dve.do(lambda e: e.tensor_scalar(cneg, csum, -1.0, None, ALU.mult), t)

            def turn():
                b = side_banks.take()
                for i in range(2):
                    a = META + i * P
                    tp = pe.do(lambda e, a=a, i=i: e.transpose(b.ap[:, 8 * i:8 * i + 8], csum[:, a:a + P],
                                                               con[H8, 0:HEADS]), t, got_con, *b.free)
                c_ready[0] = act.do(lambda e: e.copy(cq[:, :, :], b.ap[:, 0:16].rearrange("p (i h) -> p i h", i=2)), tp)
                b.release(c_ready[0])
            later(3, turn)
            yield

        kt_plain = lambda n, i: UNIT_K * n + i
        U = KT // UNIT_K
        product(U, kt_plain, from_a, a_of, [finish_k(i) for i in range(4)])
        product(2, lambda n, i: 8 * n + i, from_a, a_of, [(ALL, finish_f)], width=P)
        product(U, kt_plain, from_a, a_of, [finish_k(i) for i in range(4, 8)])
        for b in range(2):
            product(U, kt_plain, from_a, a_of, [finish_q(4 * b + i) for i in range(4)])
        for b in range(2):
            product(U, kt_plain, from_a, a_of, [finish_v(4 * b + i) for i in range(4)])
        flush()

        def softmax(state, slot, spans, t, counts, *more):
            ty = tiny.take()
            mx, l, r = ty.ap[:, 0, 0:2], ty.ap[:, 1, 0:2], ty.ap[:, 2, 0:2]
            for i, (a, n) in enumerate(spans):
                t = dve.do(lambda e, i=i, a=a, n=n: e.reduce_max(mx[:, i:i + 1], slot.ap[:, a:a + n], AX_X), t, *ty.free)
            t = dve.do(lambda e: e.tensor_scalar(mx, mx, -1.0, None, ALU.mult), t)
            yield True
            for i, (a, n) in enumerate(spans):
                acc_out = {} if counts else {"accum_out": l[:, i:i + 1]}
                tx = act.do(lambda e, i=i, a=a, n=n, o=acc_out: e.activation(
                    slot.ap[:, a:a + n], slot.ap[:, a:a + n], ACT.Exp, bias=mx[:, i:i + 1], **o), t)
            yield True
            yield True
            t = tx
            if counts:
                for i, (a, n) in enumerate(spans):
                    t = dve.do(lambda e, i=i, a=a, n=n: e.scalar_tensor_tensor(
                        slot.ap[:, a:a + n], slot.ap[:, a:a + n], 1.0, counts[i], ALU.mult, ALU.mult,
                        accum_out=l[:, i:i + 1]), tx, *more)
            t = dve.do(lambda e: e.reciprocal(r, l), t)
            for i, (a, n) in enumerate(spans):
                t = dve.do(lambda e, i=i, a=a, n=n: e.tensor_scalar(
                    slot.ap[:, a:a + n], slot.ap[:, a:a + n], r[:, i:i + 1], None, ALU.mult), t)
            ty.release(t)
            state["t"] = t

        y_ready, ms_ready = {}, {}

        def group_square(g):
            s = work.take()
            y = s.ap[:, 0:SEQ]
            t = act.do(lambda e: e.activation(y, ytile[:, g, :], ACT.Square), y_ready[g], *s.free)

            def sums():
                b = side_banks.take()
                t2 = sums_to_rows(b, 0, s.ap, (0, P), t)
                s.release(t2)
                ms_ready[g] = dve.do(lambda e: e.tensor_scalar(gms[:, g, :], b.ap[:, 0:2], 1.0 / P, RMS_EPS,
                                                               ALU.mult, ALU.add), t2)
                b.release(ms_ready[g])
            later(3, sums)

        probs_t_free = [()]
        q_cols = (0, KEYS1[0])

        def head1(hd):
            state = {}

            def scores():
                b, s = side_banks.take(), prob_ring.take()
                sel = con[H8, hd:hd + 1].to_broadcast([HEADS, P])
                for i in range(2):
                    n, o = KEYS1[i], q_cols[i]
                    pe.quiet(lambda e, i=i, n=n, o=o: e.matmul(
                        b.ap[:, o:o + n], q[:, hd, i * P:(i + 1) * P], k[:, hd, 0:n], start=True, stop=False),
                        q_ready[hd], k_ready[hd], *b.free)
                    t = pe.do(lambda e, n=n, o=o: e.matmul(b.ap[:, o:o + n], sel, cneg[:, 0:n],
                                                           start=False, stop=True), c_ready[0])
                spans = ((0, KEYS1[0]), (SEQ, KEYS1[1]))
                for i, (a, n) in enumerate(spans):
                    o = q_cols[i]
                    t = dve.do(lambda e, i=i, a=a, n=n, o=o: e.scalar_tensor_tensor(
                        s.ap[:, a:a + n], b.ap[:, o:o + n], cq[:, i, hd:hd + 1], masks[:, o:o + n],
                        ALU.add, ALU.add), t, c_ready[0], got_mask, cleared, *s.free)
                b.release(t)
                state["s"] = s
                staged(softmax(state, s, spans, t, None))

            def turn():
                s, t = state["s"], state["t"]
                got = []
                for kt in range(2):
                    b = side_banks.take()
                    for i in range(2):
                        t2 = pe.do(lambda e, i=i, kt=kt, b=b: e.transpose(
                            b.ap[:, i * P:(i + 1) * P], s.ap[:, i * SEQ + kt * P:i * SEQ + (kt + 1) * P], ident),
                            t, *b.free)
                    if kt == 0:
                        t2 = pe.do(lambda e, b=b: e.transpose(b.ap[0:META, SEQ:SEQ + P],
                                                              s.ap[:, 2 * SEQ:2 * SEQ + META], ident))
                        got.append(act.do(lambda e, b=b: e.copy(probs_t2[:, :], b.ap[0:META, SEQ:SEQ + P]),
                                          t2, *probs_t_free[0]))
                    got.append(act.do(lambda e, b=b, kt=kt: e.copy(probs_t[:, kt * SEQ:(kt + 1) * SEQ],
                                                                   b.ap[:, 0:SEQ]), t2, *probs_t_free[0]))
                    b.release(*got)
                s.release(t2)
                state["t"] = got

            def values():
                bo = side_banks.take()
                hs = slice(hd * P, (hd + 1) * P)
                pe.quiet(lambda e: e.matmul(bo.ap[:, 0:SEQ], v[:, 0, hs], probs_t[:, 0:SEQ], start=True, stop=False,
                                            skip_group_check=True), *state["t"], v_ready[hd], *bo.free)
                pe.quiet(lambda e: e.matmul(bo.ap[:, P:SEQ], v[0:META, 2, hs], probs_t2[:, :], start=False,
                                            stop=False, skip_group_check=True))
                t = pe.do(lambda e: e.matmul(bo.ap[:, 0:SEQ], v[:, 1, hs], probs_t[:, SEQ:2 * SEQ], start=False,
                                             stop=True, skip_group_check=True))
                probs_t_free[0] = (t,)
                y_ready[hd] = act.do(lambda e: e.copy(ytile[:, hd, :], bo.ap[:, 0:SEQ]), t)
                bo.release(y_ready[hd])
                group_square(hd)

            later(HEAD_STEPS * hd + 1, scores)
            later(HEAD_STEPS * hd + 15, turn)
            later(HEAD_STEPS * hd + 24, values)

        b_ready = {}

        def normed_groups(groups, *waits):
            ty = tiny.take()
            n = 2 * len(groups)
            ms = gms[:, groups[0]:groups[-1] + 1, :].rearrange("p g i -> p (g i)")
            y, z = ty.ap[:, 1, 0:n], ty.ap[:, 2, 0:n]
            t = rsqrt(ms, y, z, *[ms_ready[g] for g in groups], *ty.free)

            def one(x, g):
                dg = diagonals([ty.ap[:, 1, 2 * x + i:2 * x + i + 1] for i in range(2)], t)
                if x == len(groups) - 1:
                    ty.release(dve.now())
                yield True
                yield True
                b = side_banks.take()
                t2 = rows_to_bank(b, dg, (0, P))
                yield True
                s = work.take()
                yn = s.ap[:, 0:SEQ]
                t3 = dve.do(lambda e: e.tensor_tensor(yn, ytile[:, g, :], b.ap[:, 0:SEQ], ALU.mult), t2, *s.free)
                b.release(t3)
                b_ready[g] = split_to(b_op[:, g, 0, :], b_op[:, g, 1, :], yn, p_col("out_gain", g), t3, *waits)
                s.release(b_ready[g])
            for x, g in enumerate(groups):
                later(3 + 2 * x, lambda x=x, g=g: staged(one(x, g)))

        for hd in range(HEADS):
            head1(hd)
        later(HEAD_STEPS * HEADS + 22, lambda: normed_groups(list(range(HEADS))))
        conv = {}

        def finish_conv(j, what):
            def finish_edge(bank, done):
                s = work.take()
                y = s.ap[:, 0:CONV_TOK]
                t = dve.do(lambda e: e.tensor_tensor(y, bank.ap[:, 0:CONV_TOK], row[:, CONV], ALU.mult), done, *s.free)
                bank.release(t)
                if what == "gate_c":
                    conv["gc", j] = (s, y, t)
                    return
                yield True
                gs, gy, gt = conv["gc", j]
                t = pool.do(lambda e: e.tensor_tensor(y, y, gy, ALU.mult), t, gt)
                gs.release(t)
                yield True
                yield True
                o = work.take()
                u = o.ap[:, 0:SEQ]
                t = dve.do(lambda e: e.tensor_scalar(u, y[:, 0:SEQ], p_col("conv_w", j), None, ALU.mult), t, *o.free)
                for tap in (1, 2):
                    t = dve.do(lambda e, tap=tap: e.scalar_tensor_tensor(
                        u, y[:, tap:tap + SEQ], p_col("conv_w", 8 * tap + j), u, ALU.mult, ALU.add), t)
                s.release(t)
                conv["u", j] = (o, u, t)

            def finish_b(bank, done):
                s, y, t = joined(bank, done)
                yield True
                t = pool.do(lambda e: e.tensor_tensor(y, y, row[:, REAL], ALU.mult), t)
                yield True
                need(conv, ("u", j))
                yield True
                o, u, ut = conv["u", j]
                g = HEADS + j
                y_ready[g] = pool.do(lambda e: e.tensor_tensor(ytile[:, g, :], y, u, ALU.mult), t, ut)
                s.release(y_ready[g])
                o.release(y_ready[g])
                group_square(g)
                if j in (3, 7):
                    later(5, lambda: normed_groups(list(range(g - 3, g + 1))))
            return (REAL, finish_b) if what == "gate_b" else (CONV, finish_edge)

        conv_tiles = [finish_conv(j, what) for j in range(8) for what in ("gate_c", "h", "gate_b")]
        for b in range(6):
            product(U, kt_plain, from_a, a_of, conv_tiles[4 * b:4 * b + 4])

        h_ready = {}

        def into_h(j, bank, done, first_scale=None):
            hr = h[:, j, REAL]
            old = (h_ready[j],) if j in h_ready else ()
            if first_scale is None:
                t = dve.do(lambda e: e.tensor_tensor(hr, hr, bank.ap[:, 0:SEQ], ALU.add), done, *old)
            else:
                t = dve.do(lambda e: e.scalar_tensor_tensor(hr, hr, first_scale, bank.ap[:, 0:SEQ],
                                                            ALU.mult, ALU.add), done, *old)
            t = dve.do(lambda e: e.tensor_tensor(hr, hr, bank.ap[:, SEQ:2 * SEQ], ALU.add), t)
            bank.release(t)
            h_ready[j] = t
            return t

        def finish_norm_tile(j, gain, waits_a):
            def run(bank, done):
                t = into_h(j, bank, done)
                yield True
                a_ready[j] = split_to(a_op[:, j, 0, REAL], a_op[:, j, 1, REAL], h[:, j, REAL],
                                      p_col(gain, j), t, waits_a)
                yield True
                add_square(h[:, j, REAL], j == 0, acc[:, REAL], t)
                if j == KT - 1:
                    later(10, lambda: staged(rms_rows(META, (META, META + P), acc_ready[0]), 6))
            return REAL, run

        b_of = lambda kt: need(b_ready, kt)

        a_free = pe.now()

        for kt in range(KT):
            a_ready[kt] = None
        row_ready[0] = None
        for b in range(4):
            product(U, kt_plain, from_b, b_of, [finish_norm_tile(4 * b + i, "norm_ffn", a_free) for i in range(4)])

        def finish_gate_up(slot, what, keep, b_free):
            def finish(bank, done):
                s, y, t = joined(bank, done)
                yield True
                while row_ready[0] is None:
                    step()
                t = dve.do(lambda e: e.tensor_tensor(y, y, row[:, REAL], ALU.mult), t, row_ready[0])
                yield True
                if what == "gate":
                    keep[slot] = (s, y, act.do(lambda e: e.activation(y, y, ACT.Silu), t))
                    return
                while slot not in keep:
                    step()
                gs, gy, gt = keep.pop(slot)
                t = dve.do(lambda e: e.tensor_tensor(y, y, gy, ALU.mult), t, gt)
                gs.release(t)
                yield True
                b_ready[slot] = split_to(b_op[:, slot, 0, :], b_op[:, slot, 1, :], y, None, t, b_free)
                s.release(b_ready[slot])
            return REAL, finish

        def angles():
            s1, s2, s3 = work.take(), work.take(), work.take()
            ang, n, r = (s.ap[:, 0:SEQ] for s in (s1, s2, s3))
            freq, sign = con[:, C_FREQ:C_FREQ + 1], con[:, C_SIGN:C_SIGN + 1]
            got = sp.load(lambda e: e.dma_start(n.bitcast(I32), positions), s_pos, 16, *s2.free)
            for _ in range(12):
                yield True
            t = dve.do(lambda e: e.tensor_copy(ang, n.bitcast(I32)), got, *s1.free)
            t = dve.do(lambda e: e.tensor_scalar(ang, ang, freq, None, ALU.mult), t)
            t = dve.do(lambda e: e.tensor_scalar(r.bitcast(I32), ang, 1.0 / (2.0 * np.pi), None, ALU.mult), t, *s3.free)
            t = dve.do(lambda e: e.tensor_copy(n, r.bitcast(I32)), t)
            yield True
            part1 = 6.28125
            part2 = float(np.float32(np.round((2 * np.pi - part1) * 2.0 ** 21) / 2.0 ** 21))
            part3 = float(np.float32(2 * np.pi - part1 - part2))
            for c in (part1, part2, part3):
                t = dve.do(lambda e, c=c: e.scalar_tensor_tensor(ang, n, -c, ang, ALU.mult, ALU.add), t)
            t = dve.do(lambda e: e.tensor_scalar(ang, ang, float(np.float32(3.1415925)), float(np.float32(-3.1415925)),
                                                 ALU.min, ALU.max), t)
            yield True
            ts = act.do(lambda e: e.activation(sinr, ang, ACT.Sin), t, pe.now())
            t = act.do(lambda e: e.activation(ang, ang, ACT.Abs), ts)
            yield True
            ts = dve.do(lambda e: e.tensor_scalar(sinr, sinr, sign, None, ALU.mult), ts)
            t = dve.do(lambda e: e.tensor_scalar(ang, ang, -1.0, float(np.pi / 2), ALU.mult, ALU.add), t)
            yield True
            t = act.do(lambda e: e.activation(cosr, ang, ACT.Sin), t)
            for slot in (s1, s2, s3):
                slot.release(t)
            turned["angles"] = (ts, t)

        turned = {}
        later(40, lambda: staged(angles()))

        def scaled_angles():
            while row_ready[0] is None:
                step()
            t1, t2 = turned["angles"]
            dve.do(lambda e: e.tensor_tensor(cosr, cosr, row[:, REAL], ALU.mult), t1, t2, row_ready[0])
            return dve.do(lambda e: e.tensor_tensor(sinr, sinr, row[:, REAL], ALU.mult))

        keep = {}
        base = 0
        for gi, n in enumerate(GROUPS1):
            b_free = pe.now()
            for slot in range(n):
                b_ready[slot] = None
            for b in range(n // 2):
                tiles = [finish_gate_up(2 * b + x // 2, ("gate", "up")[x % 2], keep, b_free) for x in range(4)]
                product(U, kt_plain, from_a, a_of, tiles)
            a_free = pe.now()
            last = gi == len(GROUPS1) - 1

            def finish_down(j):
                def add(bank, done):
                    into_h(j, bank, done)
                    yield
                return (REAL, add) if not last else finish_norm_tile(j, "final_norm", a_free)
            if last:
                flush_until(b_ready, n)
                row_ready[0] = None
                for kt in range(KT):
                    a_ready[kt] = None
            for b in range(4):
                product(n // UNIT_K, kt_plain, from_b, b_of, [finish_down(4 * b + i) for i in range(4)])
            base += n

        got_mask2 = sp.load(lambda e: e.dma_start(masks[:, :], mask2), s_mask, 32, dve.now())
        rope_ready = [None]

        def finish_rope(dst, hd, book):
            def finish(bank, done):
                if rope_ready[0] is None:
                    rope_ready[0] = scaled_angles()
                s, y, t = joined(bank, done)
                yield True
                o = work.take()
                w_ = o.ap[:, 0:SEQ]
                act.quiet(lambda e: e.copy(w_[0:64, :], y[64:128, :]), t, *o.free)
                t2 = act.do(lambda e: e.copy(w_[64:128, :], y[0:64, :]))
                yield True
                t3 = dve.do(lambda e: e.tensor_tensor(y, y, cosr, ALU.mult), t2, rope_ready[0])
                t2 = pool.do(lambda e: e.tensor_tensor(w_, w_, sinr, ALU.mult), t2, rope_ready[0])
                yield True
                book[hd] = pool.do(lambda e: e.tensor_tensor(dst[:, hd, 0:SEQ], y, w_, ALU.add), t2, t3)
                s.release(book[hd])
                o.release(book[hd])
            return REAL, finish

        def finish_v2(hd):
            def finish(bank, done):
                s, y, t = joined(bank, done)
                yield True
                t = dve.do(lambda e: e.tensor_tensor(y, y, row[:, REAL], ALU.mult), t, row_ready[0])
                yield True
                yield True
                to_v(hd, s, y, t, 2, 0)
            return REAL, finish

        for b in range(2):
            product(U, kt_plain, from_a, a_of, [finish_rope(k, 4 * b + i, k_ready) for i in range(4)])
        for b in range(2):
            product(U, kt_plain, from_a, a_of, [finish_rope(q, 4 * b + i, q_ready) for i in range(4)])

        def residual(j):
            t = dve.do(lambda e: e.scalar_tensor_tensor(h[:, j, REAL], h[:, j, REAL], p_col("final_norm", j),
                                                        row[:, REAL], ALU.mult, ALU.mult),
                       row_ready[0], h_ready[j], a_ready[j], act.now())
            h_ready[j] = t
        for j in range(KT):
            later(1 + 2 * j, lambda j=j: residual(j))
        for b in range(2):
            product(U, kt_plain, from_a, a_of, [finish_v2(4 * b + i) for i in range(4)])
        flush()

        def head2(hd):
            state = {}
            cols = (0, KEYS2[0])
            spans = ((0, KEYS2[0]), (KEYS2[0], KEYS2[1]))

            def scores():
                b, s = side_banks.take(), prob_ring.take()
                for i in range(2):
                    n, o = KEYS2[i], cols[i]
                    t = pe.do(lambda e, i=i, n=n, o=o: e.matmul(
                        b.ap[:, o:o + n], q[:, hd, i * P:(i + 1) * P], k[:, hd, 0:n], start=True, stop=True),
                        q_ready[hd], k_ready[hd], *b.free)
                t = dve.do(lambda e: e.scalar_tensor_tensor(s.ap[:, 0:P + SEQ], b.ap[:, 0:P + SEQ], SCALE,
                                                            masks[:, 0:P + SEQ], ALU.mult, ALU.add),
                           t, got_mask2, *s.free)
                b.release(t)
                counts = [masks[:, P + SEQ + a:P + SEQ + a + n] for a, n in spans]
                state["s"] = s
                staged(softmax(state, s, spans, t, counts))

            def turn():
                s, t = state["s"], state["t"]
                bt = side_banks.take()
                for x, a in enumerate((0, P, 2 * P)):
                    t2 = pe.do(lambda e, a=a: e.transpose(bt.ap[:, a:a + P], s.ap[:, a:a + P], ident), t, *bt.free)
                s.release(t2)
                f = act.do(lambda e: e.copy(probs_t[:, 0:3 * P], bt.ap[:, 0:3 * P]), t2, *probs_t_free[0])
                bt.release(f)
                state["t"] = f

            def values():
                bo = side_banks.take()
                hs = slice(hd * P, (hd + 1) * P)
                pe.quiet(lambda e: e.matmul(bo.ap[:, 0:SEQ], v[:, 0, hs], probs_t[:, 0:SEQ], start=True, stop=False,
                                            skip_group_check=True), state["t"], v_ready[hd], *bo.free)
                t = pe.do(lambda e: e.matmul(bo.ap[:, P:SEQ], v[:, 1, hs], probs_t[:, SEQ:3 * P], start=False,
                                             stop=True, skip_group_check=True))
                probs_t_free[0] = (t,)
                s = work.take()
                y = s.ap[:, 0:SEQ]
                f = act.do(lambda e: e.copy(y, bo.ap[:, 0:SEQ]), t, *s.free)
                bo.release(f)
                b_ready[hd] = split_to(b_op[:, hd, 0, :], b_op[:, hd, 1, :], y, None, f, b_free)
                s.release(b_ready[hd])

            later(HEAD_STEPS * hd + 1, scores)
            later(HEAD_STEPS * hd + 15, turn)
            later(HEAD_STEPS * hd + 24, values)

        b_free = pe.now()
        for hd in range(HEADS):
            head2(hd)

        pool_ready = {}

        def finish_u(j):
            g = j // 2
            win = POOL_WINDOWS[g]

            def finish(bank, done):
                s, y, t = joined(bank, done)
                yield True
                x = work.take()
                tz = pool.do(lambda e: e.memset(x.ap[:, 0:META], 0.0), *x.free)
                t = dve.do(lambda e: e.tensor_tensor(x.ap[:, REAL], y, row[:, REAL], ALU.mult), t, *x.free)
                s.release(t)
                src, lo, span, t = x, 0, 1, (t, tz)
                while span < win:
                    lo += span
                    o = work.take()
                    t = (pool.do(lambda e, o=o, src=src, lo=lo, span=span: e.tensor_tensor(
                        o.ap[:, lo:TOK], src.ap[:, lo:TOK], src.ap[:, lo - span:TOK - span], ALU.add), *t, *o.free),)
                    if src is not x:
                        src.release(*t)
                    src, span = o, 2 * span
                yield True
                yield True
                dst = ytile[:, 8 + j, :]
                ramp = con[:, C_RAMP + 16 * g:C_RAMP + 16 * (g + 1)]
                t1 = dve.do(lambda e: e.scalar_tensor_tensor(dst, src.ap[:, REAL], 1.0 / win, x.ap[:, REAL],
                                                             ALU.mult, ALU.subtract), *t)
                t2 = dve.do(lambda e: e.tensor_tensor(src.ap[:, META:2 * META], src.ap[:, META:2 * META], ramp, ALU.mult), t1)
                pool_ready[j] = dve.do(lambda e: e.tensor_tensor(dst[:, 0:META], src.ap[:, META:2 * META],
                                                                 x.ap[:, META:2 * META], ALU.subtract), t2)
                src.release(pool_ready[j])
                x.release(pool_ready[j])
            return REAL, finish

        for b in range(2):
            product(U, kt_plain, from_a, a_of, [finish_u(4 * b + i) for i in range(4)])

        sig_ready, merged_ready = {}, {}

        def finish_gate(slot, *waits):
            def finish(bank, done):
                s, y, t = joined(bank, done)
                yield True
                t = dve.do(lambda e: e.tensor_tensor(y, y, row[:, REAL], ALU.mult), t)
                yield True
                sig_ready[slot] = act.do(lambda e: e.activation(ytile[:, slot, :], y, ACT.Sigmoid), t, *waits)
                s.release(sig_ready[slot])
            return REAL, finish

        product(U, kt_plain, from_a, a_of, [finish_gate(i) for i in range(4)])
        product(U, kt_plain, from_a, a_of, [finish_gate(4 + i) for i in range(4)])

        flush_until(pool_ready, 8)
        n0 = unit_at[0]
        for half in range(2):
            n = n0 + half
            for g in (2 * half, 2 * half + 1):
                for m in range(2):
                    bank = out_banks.take()
                    for kt in range(2):
                        at = (g % 2) * 512 + kt * 256 + m * P
                        t = pe.do(lambda e, n=n, at=at, g=g, kt=kt, bank=bank: e.matmul(
                            bank.ap[:, 0:SEQ], raw[:, n % RAW, at:at + P], ytile[:, 8 + 2 * g + kt, :],
                            start=(kt == 0), stop=(kt == 1)), landed[n], pool_ready[2 * g + kt], *bank.free)
                    j = 2 * g + m
                    s = work.take()
                    y = s.ap[:, 0:SEQ]
                    f = act.do(lambda e, y=y, bank=bank: e.copy(y, bank.ap[:, 0:SEQ]), t, *s.free)
                    bank.release(f)
                    b_ready[8 + j] = split_to(b_op[:, 8 + j, 0, :], b_op[:, 8 + j, 1, :], y,
                                              p_col("pool_scale", j), f, b_free)
                    s.release(b_ready[8 + j])
            raw_done(n, t)
        unit_at[0] += 2
        pooled = pe.now()
        product(U, kt_plain, from_a, a_of, [finish_gate(8 + i, pooled) for i in range(4)])
        product(U, kt_plain, from_a, a_of, [finish_gate(12 + i) for i in range(4)])
        flush()
        attended = pe.now()

        def branches(b, base, to_a):
            def attn(i):
                def finish(bank, done):
                    s, y, t = joined(bank, done)
                    yield True
                    sg = ytile[:, base + i, :]
                    sig_ready[base + i] = pool.do(lambda e: e.tensor_tensor(sg, sg, y, ALU.mult), t, sig_ready[base + i])
                    s.release(sig_ready[base + i])
                return REAL, finish

            def pooled_(i):
                j = 4 * b + i

                def finish(bank, done):
                    s, y, t = joined(bank, done)
                    yield True
                    t = dve.do(lambda e: e.tensor_tensor(y, y, ytile[:, base + 4 + i, :], ALU.mult), t,
                               sig_ready[base + 4 + i])
                    yield True
                    if to_a is None:
                        merged_ready[j] = pool.do(lambda e: e.tensor_tensor(q[:, j, :], y, ytile[:, base + i, :], ALU.add),
                                                  t, sig_ready[base + i], attended)
                        s.release(merged_ready[j])
                        return
                    t = pool.do(lambda e: e.tensor_tensor(y, y, ytile[:, base + i, :], ALU.add), t, sig_ready[base + i])
                    merged_ready[j] = t
                    yield True
                    a_ready[j] = split_to(a_op[:, j, 0, REAL], a_op[:, j, 1, REAL], y, None, t, to_a)
                    s.release(a_ready[j])
                return REAL, finish
            product(4, kt_plain, from_b, b_of, [attn(i) for i in range(4)])
            product(4, lambda n, i: 8 + UNIT_K * n + i, from_b, b_of, [pooled_(i) for i in range(4)])

        branches(0, 0, None)
        branches(1, 8, None)
        flush()
        for x in range(4):
            base = (0, 4, 8, 12)[x]
            product(U, kt_plain, from_a, a_of, [finish_gate(base + i, pool.now(), dve.now()) for i in range(4)])
        a_free = pe.now()
        flush()
        for j in range(KT):
            a_ready[j] = None

        def late_split(j):
            a_ready[j] = split_to(a_op[:, j, 0, REAL], a_op[:, j, 1, REAL], q[:, j, :], None, merged_ready[j], a_free)
        for j in range(8):
            later(1 + j, lambda j=j: late_split(j))
        branches(2, 0, a_free)
        branches(3, 8, a_free)
        flush()

        FIRST = KT // 4
        shift_ready = [None]
        sum_ready = [None, None]

        def centre(j, first):
            hr = h[:, j, REAL]
            t = dve.do(lambda e: e.tensor_tensor(hr, hr, shift[:, :], ALU.subtract), h_ready[j], shift_ready[0],
                       pool.now())
            h_ready[j] = t
            if first:
                sum_ready[0] = dve.do(lambda e: e.tensor_copy(acc[:, REAL], hr), t, pool.now(), pe.now())
                sum_ready[1] = act.do(lambda e: e.activation(acc2[:, :], hr, ACT.Square), t, pe.now(), pool.now())
                return
            s = work.take()
            t2 = act.do(lambda e: e.activation(s.ap[:, 0:SEQ], hr, ACT.Square), t, *s.free)
            adder = dve if j == KT - 1 else pool
            sum_ready[0] = adder.do(lambda e: e.tensor_tensor(acc[:, REAL], acc[:, REAL], hr, ALU.add), t, sum_ready[0])
            sum_ready[1] = adder.do(lambda e: e.tensor_tensor(acc2[:, :], acc2[:, :], s.ap[:, 0:SEQ], ALU.add),
                                   t2, sum_ready[1])
            s.release(sum_ready[1])

        def norm_tile(j):
            if j < FIRST:
                hr = h[:, j, REAL]
                if j == 0:
                    sum_ready[0] = dve.do(lambda e: e.tensor_copy(acc[:, REAL], hr), h_ready[j], pool.now(), pe.now())
                else:
                    sum_ready[0] = pool.do(lambda e: e.tensor_tensor(acc[:, REAL], acc[:, REAL], hr, ALU.add),
                                           h_ready[j], sum_ready[0])
                if j == FIRST - 1:
                    def mean():
                        b = side_banks.take()
                        t = pe.do(lambda e: e.matmul(b.ap[:, 0:SEQ], ones[:, :], acc[:, REAL], start=True, stop=True),
                                  sum_ready[0], *b.free)
                        shift_ready[0] = act.do(lambda e: e.activation(shift[:, :], b.ap[:, 0:SEQ], ACT.Copy,
                                                                       scale=1.0 / (FIRST * P)), t, dve.now(), pool.now())
                        b.release(shift_ready[0])
                    later(9, mean)
                    for x in range(FIRST):
                        later(14 + 3 * x, lambda x=x: centre(x, x == 0))
                return
            while shift_ready[0] is None:
                step()
            centre(j, False)

        def norm_rows():
            bank, ty = side_banks.take(), tiny.take()
            d, y, z, o, m2 = (ty.ap[:, i, 0:2] for i in (0, 1, 2, 3, 4))
            means = ty.ap[:, 5, 0:4]
            warm = act.do(lambda e: e.activation(ty.ap[:, 1, 0:1], ones[:, 0:1], ACT.Sqrt), *ty.free)
            t = sums_to_rows(bank, 0, acc, (META, META + P), sum_ready[0])
            t = sums_to_rows(bank, 2, acc2, (0, P), sum_ready[1])
            t = dve.do(lambda e: e.tensor_scalar(means, bank.ap[:, 0:4], 1.0 / D, None, ALU.mult), t, *ty.free)
            bank.release(t)
            d = means[:, 0:2]
            t = dve.do(lambda e: e.tensor_tensor(z, d, d, ALU.mult), t)
            t = dve.do(lambda e: e.scalar_tensor_tensor(m2, means[:, 2:4], LN_EPS, z, ALU.add, ALU.subtract), t)
            t = rsqrt(m2, y, z, t, warm)
            t = dve.do(lambda e: e.scalar_tensor_tensor(o, d, -1.0, y, ALU.mult, ALU.mult), t)
            rows = side_banks.take()
            dg = diagonals([ty.ap[:, r, i:i + 1] for r in (1, 3) for i in range(2)], t)
            t = rows_to_bank(rows, dg, (0, P, SEQ, SEQ + P))
            ty.release(dve.now())
            return rows, t

        def normed_tile(j, gain, bias, rows, ready):
            hr = h[:, j, REAL]
            t = dve.do(lambda e: e.tensor_tensor(hr, hr, rows.ap[:, 0:SEQ], ALU.mult), h_ready[j], ready, *sum_ready)
            t = dve.do(lambda e: e.tensor_tensor(hr, hr, rows.ap[:, SEQ:2 * SEQ], ALU.add), t)
            h_ready[j] = act.do(lambda e: e.activation(hr, hr, ACT.Identity, scale=p_col(gain, j), bias=p_col(bias, j)), t)
            if j == KT - 1:
                rows.release(t)
            return h_ready[j]

        def finish_mix(j):
            def finish(bank, done):
                into_h(j, bank, done, ALPHA)
                yield True
                norm_tile(j)
            return REAL, finish

        for b in range(4):
            product(U, kt_plain, from_a, a_of, [finish_mix(4 * b + i) for i in range(4)], tail=2 * (b == 3))
        a_free = pe.now()
        flush()
        rows, ready = norm_rows()
        for j in range(KT):
            a_ready[j] = None

        def normed_pair(j):
            his = []
            for x in (j, j + 1):
                t = normed_tile(x, "ln_mix_g", "ln_mix_b", rows, ready)
                his.append(act.do(lambda e, x=x: e.copy(a_op[:, x, 0, REAL], h[:, x, REAL]), t, a_free))
            for x, t in zip((j, j + 1), his):
                a_ready[x] = pool.do(lambda e, x=x: e.tensor_tensor(
                    a_op[:, x, 1, REAL], h[:, x, REAL], a_op[:, x, 0, REAL].bitcast(F32), ALU.subtract), t)
        normed_pair(0)
        normed_pair(2)
        for j in range(4, KT, 2):
            later(2 * j - 6, lambda j=j: normed_pair(j))

        shift_ready[0] = None

        def finish_ff1(slot, b_free):
            def finish(bank, done):
                s, y, t = joined(bank, done)
                yield True
                t = dve.do(lambda e: e.tensor_scalar(y, y, 0.0, None, ALU.max), t)
                t = pool.do(lambda e: e.tensor_tensor(y, y, y, ALU.mult), t)
                yield True
                yield True
                b_ready[slot] = split_to(b_op[:, slot, 0, :], b_op[:, slot, 1, :], y, None, t, b_free)
                s.release(b_ready[slot])
            return REAL, finish

        for gi, n in enumerate(GROUPS2):
            b_free = pe.now()
            for slot in range(n):
                b_ready[slot] = None
            for b in range(n // BLOCK):
                product(U, kt_plain, from_a, a_of, [finish_ff1(BLOCK * b + i, b_free) for i in range(4)])

            def finish_ff2(j, gi=gi):
                def finish(bank, done):
                    into_h(j, bank, done, ALPHA if gi == 0 else None)
                    yield True
                    if gi == len(GROUPS2) - 1:
                        norm_tile(j)
                return REAL, finish
            for b in range(4):
                product(n // UNIT_K, kt_plain, from_b, b_of, [finish_ff2(4 * b + i) for i in range(4)],
                        tail=SPLIT * (gi == len(GROUPS2) - 1 and b == 3))
        flush()

        rows, ready = norm_rows()
        stored = 0
        for j in range(KT):
            normed_tile(j, "ln_ff_g", "ln_ff_b", rows, ready)
            if j % 2 == 1:
                stored += 16
                sp.load(lambda e, j=j: e.dma_start(out[:, j - 1:j + 1, :], h[:, j - 1:j + 1, REAL]), s_out, stored,
                        h_ready[j])
        assert unit_at[0] == len(order)
        sp.wait(Ticket(s_out, stored))

        block = ctx.enter_context(nc.Block())
        block.sync(sp.play)
        block.tensor(pe.play)
        block.scalar(act.play)
        block.vector(dve.play)
        block.gpsimd(pool.play)



def pack_weight(m, tiles=None):
    rows, cols = m.shape
    m = m.reshape(rows // (UNIT_K * P), UNIT_K, P, cols // P, P)
    if tiles is not None:
        m = m[:, :, :, tiles, :]
    m = m.reshape(rows // (UNIT_K * P), UNIT_K, P, cols // (BLOCK * P), BLOCK * P)
    m = m.transpose(3, 0, 2, 1, 4)
    return np.ascontiguousarray(m).reshape(m.shape[0], m.shape[1], P, UNIT)


def feature_columns(vec):
    return vec.reshape(-1, P).T


def shape_constants():
    con = np.zeros((P, N_CONST), np.float32)
    con[:, C_IDENT:C_IDENT + P] = np.eye(P, dtype=np.float32)
    half = P // 2
    freq = np.float32(10000.0) ** (-np.arange(half, dtype=np.float32) / np.float32(half))
    con[:, C_FREQ] = np.concatenate([freq, freq])
    con[:, C_SIGN] = np.concatenate([-np.ones(half), np.ones(half)])
    for g, win in enumerate(POOL_WINDOWS):
        con[:, C_RAMP + 16 * g:C_RAMP + 16 * (g + 1)] = 1.0 / np.minimum(np.arange(1, 17), win)
    rows = np.arange(P)[:, None]
    mask1 = np.concatenate([np.where(np.arange(n)[None] <= META + i * P + rows, 0.0, NEG)
                            for i, n in enumerate(KEYS1)], axis=1).astype(np.float32)
    count = []
    for i, n in enumerate(KEYS2):
        dist = i * P + rows - np.arange(n)[None]
        count.append(sum(((dist >= 0) & (dist <= span * dil) & (dist % dil == 0)).astype(np.float32)
                         for span, dil in ((128, 1), (128, 4), (128, 16))))
    count = np.concatenate(count, axis=1)
    mask2 = np.concatenate([np.where(count > 0, 0.0, NEG), count], axis=1).astype(np.float32)
    return con, mask1, mask2


def kernel(**inputs):
    import concourse.bacc as bacc
    from concourse.bass_utils import run_bass_kernel_spmd

    a = {n: np.asarray(x) for n, x in inputs.items()}
    w_in = a["w_in"][0]
    tiles1 = list(range(8, 16)) + list(range(0, 8)) + list(range(16, 24))
    for j in range(8):
        tiles1 += [32 + j, 40 + j, 24 + j]
    n_main = 48 * P
    w_f = np.zeros((D, P), w_in.dtype)
    w_f[:, 0:HEADS] = w_in[:, n_main:]
    w_f = np.ascontiguousarray(w_f.reshape(2, 8, P, P).transpose(0, 2, 1, 3)).reshape(1, 2, P, UNIT)
    gu = np.concatenate([a["w_gate"][0], a["w_up"][0]], axis=1)
    n_ff = D_FF1 // P
    tiles_gu = [x for j in range(n_ff) for x in (j, n_ff + j)]
    tiles2 = list(range(8, 16)) + list(range(0, 8)) + list(range(16, 32))
    for b in range(4):
        tiles2 += [32 + 4 * b + i for i in range(4)] + [48 + 4 * b + i for i in range(4)]
    w_pool = a["w_pool_2"][0].reshape(2, 2, 2, P, 256).transpose(0, 3, 1, 2, 4)
    weights = {
        "w_in": pack_weight(w_in[:, 0:n_main], tiles1),
        "w_f": w_f,
        "w_out": pack_weight(a["w_out"][0]),
        "w_gu": pack_weight(gu, tiles_gu),
        "w_down": pack_weight(a["w_down"][0]),
        "w_in_2": pack_weight(a["w_in_2"][0], tiles2),
        "w_pool": np.ascontiguousarray(w_pool).reshape(1, 2, P, UNIT),
        "w_ba": pack_weight(a["w_branch_attn_2"][0]),
        "w_bp": pack_weight(a["w_branch_pool_2"][0]),
        "w_out_2": pack_weight(a["w_out_2"][0]),
        "w_ff1": pack_weight(a["w_ff1_2"][0]),
        "w_ff2": pack_weight(a["w_ff2_2"][0]),
    }
    tokens = np.concatenate([a["meta"], a["x"][0]], axis=0).T.reshape(KT, P, TOK).transpose(1, 0, 2)
    params = np.zeros((P, N_PARAMS), np.float32)

    def put(name, cols):
        params[0:cols.shape[0], PARAMS[name]:PARAMS[name] + cols.shape[1]] = cols
    put("norm_mix", feature_columns(a["norm_mix"][0]))
    put("out_gain", feature_columns(a["out_gain"][0]))
    put("norm_ffn", feature_columns(a["norm_ffn"][0]))
    put("final_norm", feature_columns(a["final_norm"]))
    put("conv_w", feature_columns(a["conv_w"][0].reshape(-1)))
    put("pool_scale", feature_columns(a["pool_scale_2"][0]))
    put("ln_mix_g", feature_columns(a["ln_mix_g_2"][0]))
    put("ln_mix_b", feature_columns(a["ln_mix_b_2"][0]))
    put("ln_ff_g", feature_columns(a["ln_ff_g_2"][0]))
    put("ln_ff_b", feature_columns(a["ln_ff_b_2"][0]))
    put("b_f", a["b_f"][0].reshape(HEADS, 1))
    con, mask1, mask2 = shape_constants()
    positions = np.broadcast_to(a["positions_2"][0][None, :], (P, SEQ))

    arrays = {f"in_{n}": x for n, x in weights.items()}
    arrays |= {"in_tokens": tokens, "in_params": params, "in_consts": con, "in_mask1": mask1,
               "in_mask2": mask2, "in_positions": positions}
    arrays = {n: np.ascontiguousarray(x) for n, x in arrays.items()}
    nc = bacc.Bacc("TRN2", target_bir_lowering=False, num_devices=1)
    aps = {n: nc.dram_tensor(n, x.shape, mybir.dt.from_np(x.dtype), kind="ExternalInput").ap()
           for n, x in arrays.items()}
    out = nc.dram_tensor("out", (P, KT, SEQ), F32, kind="ExternalOutput").ap()
    two_blocks(nc, {n: aps[f"in_{n}"] for n in weights}, aps["in_tokens"], aps["in_params"], aps["in_consts"],
               aps["in_mask1"], aps["in_mask2"], aps["in_positions"], out)
    r = run_bass_kernel_spmd(nc, [arrays], core_ids=[0])
    got = r.results[0]["out"]
    return np.ascontiguousarray(got.transpose(2, 1, 0)).reshape(1, SEQ, D)
```

```python
from contextlib import ExitStack

import numpy as np

import concourse.bass as bass
from concourse import mybir

F32 = mybir.dt.float32
F32R = mybir.dt.float32r
I32 = mybir.dt.int32
ALU = mybir.AluOpType
ACT = mybir.ActivationFunctionType
AX_X = mybir.AxisListType.X

P = 128
D = 2048
KT = D // P
SEQ = 256
META = 16
TOK = META + SEQ
HEADS = 8
D_FF1 = 5632
D_FF2 = 8192
NEG = -1e30
RMS_EPS = 1e-6
LN_EPS = 1e-5
ALPHA = 2.0 ** 0.25
SCALE = float(P) ** -0.5

UNIT_K = 2
BLOCK = 4
UNIT = UNIT_K * BLOCK * P
RAW = 5
HEAD_STEPS = 16
SPLIT = 4
CONV_TOK = SEQ + 2
POOL_WINDOWS = (2, 4, 8, 16)

GROUPS1 = (8, 12, 12, 12)
GROUPS2 = (16, 16, 16, 16)
assert sum(GROUPS1) * P == D_FF1 and sum(GROUPS2) * P == D_FF2

KEYS1 = (META + P, TOK)
KEYS2 = (P, SEQ)

PARAMS = {}
_at = 0
for _name, _n in (("norm_mix", KT), ("out_gain", KT), ("norm_ffn", KT), ("final_norm", KT),
                  ("conv_w", 24), ("pool_scale", 8), ("ln_mix_g", KT), ("ln_mix_b", KT),
                  ("ln_ff_g", KT), ("ln_ff_b", KT), ("b_f", 1)):
    PARAMS[_name] = _at
    _at += _n
N_PARAMS = _at

C_IDENT, C_FREQ, C_SIGN, C_RAMP = 0, P, P + 1, P + 2
N_CONST = C_RAMP + 4 * 16


class Ticket:

    def __init__(self, sem, value):
        self.sem, self.value = sem, value


class Engine:

    def __init__(self, sem):
        self.sem, self.count, self.steps = sem, 0, []

    def do(self, make, *waits):
        self.count += 1
        self.steps.append((waits, make, self.sem, 1))
        return Ticket(self.sem, self.count)

    def quiet(self, make, *waits):
        self.steps.append((waits, make, None, 0))

    def load(self, make, sem, value, *waits):
        self.steps.append((waits, make, sem, 16))
        return Ticket(sem, value)

    def wait(self, *waits):
        self.steps.append((waits, None, None, 0))

    def now(self):
        return Ticket(self.sem, self.count)

    def play(self, eng):
        reached = {}
        for waits, make, sem, by in self.steps:
            for t in waits:
                if t is not None and t.value > reached.get(id(t.sem), 0):
                    eng.wait_ge(t.sem, t.value)
                    reached[id(t.sem)] = t.value
            if make is not None:
                ins = make(eng)
                if sem is not None:
                    ins.then_inc(sem, by)


class Slot:
    def __init__(self, ap):
        self.ap, self.free, self.held, self.age = ap, (), False, 0

    def release(self, *tickets):
        self.free, self.held = tickets, False


class Ring:

    def __init__(self, aps):
        self.slots, self.turn = [Slot(a) for a in aps], 0

    def take(self):
        free = [s for s in self.slots if not s.held]
        assert free, "no slot is free"
        s = min(free, key=lambda x: x.age)
        self.turn += 1
        s.age, s.held = self.turn, True
        return s


def two_blocks(nc, w, tokens, params, consts, mask1, mask2, positions, out):
    with ExitStack() as ctx:
        def sb(name, shape, dt=F32):
            return ctx.enter_context(nc.sbuf_tensor(name, shape, dt))

        def sem(name):
            return ctx.enter_context(nc.semaphore(name))

        h = sb("h", [P, KT, TOK])
        a_op = sb("a_op", [P, KT, 2, TOK], F32R)
        b_op = sb("b_op", [P, KT, 2, SEQ + 2], F32R)
        raw = sb("raw", [P, RAW, UNIT])
        w_hi = sb("w_hi", [P, SPLIT, UNIT], F32R)
        w_lo = sb("w_lo", [P, SPLIT, UNIT], F32R)
        q = sb("q", [P, HEADS, SEQ])
        k = sb("k", [P, HEADS, TOK])
        v = sb("v", [P, 3, HEADS * P])
        ytile = sb("ytile", [P, KT, SEQ])
        probs = sb("probs", [P, 2, SEQ + TOK])
        probs_t = sb("probs_t", [P, 2 * SEQ])
        probs_t2 = sb("probs_t2", [META, P])
        con = sb("con", [P, N_CONST])
        masks = sb("masks", [P, 2 * (P + SEQ)])
        par = sb("par", [P, N_PARAMS])
        ones = sb("ones", [P, P])
        row = sb("row", [P, TOK])
        shift = sb("shift", [P, SEQ])
        turn_tab = sb("turn_tab", [P, 2 * SEQ])
        cosr, sinr = turn_tab[:, 0:SEQ], turn_tab[:, SEQ:2 * SEQ]
        acc = sb("acc", [P, TOK])
        acc2 = sb("acc2", [P, SEQ])
        csum = turn_tab[0:HEADS, 0:TOK]
        cneg = masks[0:HEADS, sum(KEYS1):sum(KEYS1) + TOK]
        cq = sb("cq", [P, 2, HEADS])
        gms = sb("gms", [P, KT, 2])
        work = Ring([sb(f"work{i}", [P, TOK])[:, :] for i in range(8)])
        tiny = Ring([sb(f"tiny{i}", [P, 6, 16])[:, :, :] for i in range(4)])
        prob_ring = Ring([probs[:, i, :] for i in range(2)])

        def psum(name):
            return ctx.enter_context(nc.psum_tensor(name, [P, 512], F32))

        out_banks = Ring([psum(f"out_bank{i}")[:, :] for i in range(6)])
        side_banks = Ring([psum(f"side_bank{i}")[:, :] for i in range(2)])

        sp = Engine(None)
        pe, act, dve, pool = (Engine(sem(f"{n}_done")) for n in ("pe", "act", "dve", "pool"))
        s_raw = [sem(f"raw_landed{i}") for i in range(RAW)]
        s_h = [sem(f"tokens_landed{i}") for i in range(KT // 2)]
        s_par, s_con, s_mask = sem("params_landed"), sem("consts_landed"), sem("masks_landed")
        s_pos, s_out = sem("positions_landed"), sem("outputs_stored")

        ident = con[:, C_IDENT:C_IDENT + P]

        def p_col(name, i):
            c = PARAMS[name] + i
            return par[:, c:c + 1]

        clock, asked = [0], [0]
        later_work = []

        def later(n, fn):
            asked[0] += 1
            later_work.append((clock[0] + n, asked[0], fn))

        def step():
            clock[0] += 1
            while later_work and min(later_work)[0] <= clock[0]:
                due = min(later_work)
                later_work.remove(due)
                due[2]()

        def staged(steps, gap=1):
            if next(steps, None) is not None:
                later(gap, lambda: staged(steps, gap))

        def need(book, key):
            while book.get(key) is None:
                assert later_work
                step()
            return (book[key],)

        def flush_until(book, n):
            for key in range(n):
                need(book, key)

        def flush():
            while later_work:
                step()

        order = []

        def stream(name, n_k, blocks, fine=True):
            order.extend((name, b, u, fine) for b in blocks for u in range(n_k // UNIT_K))

        stream("w_in", KT, [0])
        order.extend(("w_f", 0, u, True) for u in range(2))
        stream("w_in", KT, range(1, 12))
        stream("w_out", KT, range(4))
        base = 0
        for n in GROUPS1:
            stream("w_gu", KT, range(base // 2, (base + n) // 2))
            for b in range(4):
                order.extend(("w_down", b, base // UNIT_K + u, True) for u in range(n // UNIT_K))
            base += n
        stream("w_in_2", KT, range(10))
        order.extend(("w_pool", 0, u, False) for u in range(2))
        stream("w_in_2", KT, range(10, 12))
        for b in range(2):
            stream("w_ba", 8, [b])
            stream("w_bp", 8, [b])
        stream("w_in_2", KT, range(12, 16))
        for b in range(2, 4):
            stream("w_ba", 8, [b])
            stream("w_bp", 8, [b])
        stream("w_out_2", KT, range(4))
        base = 0
        for n in GROUPS2:
            stream("w_ff1", KT, range(base // 4, (base + n) // 4))
            for b in range(4):
                order.extend(("w_ff2", b, base // UNIT_K + u, True) for u in range(n // UNIT_K))
            base += n

        raw_free = [()] * RAW
        raw_read = set()
        split_free = [()] * SPLIT
        split_of = [n for n, x in enumerate(order) if x[3]]
        place = {n: i % SPLIT for i, n in enumerate(split_of)}
        after = dict(zip(split_of, split_of[SPLIT - 1:]))
        loaded, landed, hi_done, lo_done = 0, {}, {}, {}

        def load_units(limit=len(order)):
            nonlocal loaded
            while loaded < limit and (loaded < RAW or loaded - RAW in raw_read):
                name, b, u, _ = order[loaded]
                i = loaded % RAW
                src = w[name][b, u]
                landed[loaded] = sp.load(lambda e, i=i, src=src: e.dma_start(raw[:, i, :], src),
                                         s_raw[i], 16 * (loaded // RAW + 1), *raw_free[i])
                loaded += 1

        def raw_done(n, *readers):
            raw_free[n % RAW] = readers
            raw_read.add(n)
            load_units()

        def split_hi(n):
            if n is not None and n not in hi_done:
                i, j = n % RAW, place[n]
                hi_done[n] = act.do(lambda e: e.copy(w_hi[:, j, :], raw[:, i, :]), landed[n], *split_free[j])

        def split_lo(n):
            if n is not None and n not in lo_done:
                split_hi(n)
                i, j = n % RAW, place[n]
                lo_done[n] = dve.do(lambda e: e.tensor_tensor(
                    w_lo[:, j, :], raw[:, i, :], w_hi[:, j, :].bitcast(F32), ALU.subtract), hi_done[n])
                raw_done(n, hi_done[n], lo_done[n])

        unit_at = [0]

        def product(n_units, kt_of, moving, ready, tiles, width=P * BLOCK, tail=0):
            per_unit = UNIT // width
            n_tiles = width // P
            banks = [None] * n_tiles
            runs = [[n] for n in range(n_units - tail)]
            if tail:
                runs.append(list(range(n_units - tail, n_units)))
            for run in runs:
                first = unit_at[0]
                for x in range(len(run)):
                    split_lo(first + x)
                ahead = after.get(first)
                done_at = {}
                for t in range(n_tiles):
                    if t == 0:
                        split_hi(ahead)
                    if t == min(1, n_tiles - 1):
                        split_lo(ahead)
                    cols, finish = tiles[t]
                    n_col = cols.stop - cols.start
                    if run[0] == 0:
                        banks[t] = out_banks.take()
                    bank = banks[t]
                    for x, n in enumerate(run):
                        unit, j = first + x, place[first + x]
                        for i in range(per_unit):
                            start, stop = n == 0 and i == 0, n == n_units - 1 and i == per_unit - 1
                            kt = kt_of(n, i)
                            a_hi, a_lo, a_both = moving(kt, cols)
                            at = i * width + t * P
                            wh, wl = w_hi[:, j, at:at + P], w_lo[:, j, at:at + P]
                            waits = [lo_done[unit], *ready(kt)] + (list(bank.free) if start else [])
                            if n_col == SEQ:
                                mm = [(bank.ap[:, 0:2 * SEQ], wh, a_both), (bank.ap[:, 0:SEQ], wl, a_hi)]
                                if not start:
                                    mm.reverse()
                            else:
                                mm = [(bank.ap[:, 0:n_col], wh, a_hi), (bank.ap[:, 0:n_col], wh, a_lo),
                                      (bank.ap[:, 0:n_col], wl, a_hi)]
                            for y, (o, st, m) in enumerate(mm):
                                last = y == len(mm) - 1

                                def make(e, o=o, st=st, m=m, a=start and y == 0, z=stop and last):
                                    return e.matmul(o, st, m, start=a, stop=z, skip_group_check=True)
                                if last and (stop or (t == n_tiles - 1 and i == per_unit - 1)):
                                    done_at[n] = pe.do(make, *waits)
                                else:
                                    pe.quiet(make, *waits)
                    if run[-1] == n_units - 1:
                        staged(finish(bank, done_at[n_units - 1]))
                    step()
                for x, n in enumerate(run):
                    split_free[place[first + x]] = (done_at[n],)
                for x in range(1, len(run)):
                    split_lo(after.get(first + x))
                unit_at[0] += len(run)

        def from_a(kt, cols):
            return (a_op[:, kt, 0, cols], a_op[:, kt, 1, cols], a_op[:, kt, :, cols])

        def from_b(kt, cols):
            cols = slice(cols.start - META, cols.stop - META)
            return (b_op[:, kt, 0, cols], b_op[:, kt, 1, cols], b_op[:, kt, :, cols])

        REAL, ALL, CONV = slice(META, TOK), slice(0, TOK), slice(META - 2, TOK)
        WITH_AFFINE = slice(META, TOK + 2)

        def joined(bank, done):
            s = work.take()
            y = s.ap[:, 0:SEQ]
            t = act.do(lambda e: e.copy(y, bank.ap[:, SEQ:2 * SEQ]), done, *s.free)
            t = dve.do(lambda e: e.tensor_tensor(y, y, bank.ap[:, 0:SEQ], ALU.add), t)
            bank.release(t)
            return s, y, t

        def split_to(dst_hi, dst_lo, src, scale, *waits):
            if scale is None:
                t = act.do(lambda e: e.copy(dst_hi, src), *waits)
                return dve.do(lambda e: e.tensor_tensor(dst_lo, src, dst_hi.bitcast(F32), ALU.subtract), t)
            t = act.do(lambda e: e.activation(dst_hi, src, ACT.Copy, scale=scale), *waits)
            return dve.do(lambda e: e.scalar_tensor_tensor(
                dst_lo, src, scale, dst_hi.bitcast(F32), ALU.mult, ALU.subtract), t)

        def split_later(book, key, dst_hi, dst_lo, src, scale, slot, *waits):
            if scale is None:
                t = act.do(lambda e: e.copy(dst_hi, src), *waits)
            else:
                t = act.do(lambda e: e.activation(dst_hi, src, ACT.Copy, scale=scale), *waits)
            yield True
            if scale is None:
                t = dve.do(lambda e: e.tensor_tensor(dst_lo, src, dst_hi.bitcast(F32), ALU.subtract), t)
            else:
                t = dve.do(lambda e: e.scalar_tensor_tensor(dst_lo, src, scale, dst_hi.bitcast(F32),
                                                            ALU.mult, ALU.subtract), t)
            book[key] = t
            if slot is not None:
                slot.release(t)

        def sums_to_rows(bank, col, src, starts, *waits, more=None):
            for n, s in enumerate(starts):
                to = bank.ap[:, col + n:col + n + 1]
                t = pe.do(lambda e, s=s, to=to: e.matmul(to, src[:, s:s + P], ones[:, 0:1], start=True,
                                                         stop=more is None), *waits, *bank.free)
                if more is not None:
                    t = pe.do(lambda e, s=s, to=to: e.matmul(to, more[0][:, s:s + P], ones[:, 0:1], start=False,
                                                             stop=True), more[1])
            return t

        def rsqrt(got, ms, y, scratch, *waits):
            t = dve.do(lambda e: e.reciprocal(scratch, ms), *waits)
            t = act.do(lambda e: e.activation(y, scratch, ACT.Sqrt), t)
            yield True
            yield True
            t = dve.do(lambda e: e.tensor_tensor(scratch, y, y, ALU.mult), t)
            t = dve.do(lambda e: e.tensor_tensor(scratch, scratch, ms, ALU.mult), t)
            t = dve.do(lambda e: e.tensor_scalar(scratch, scratch, -0.5, 1.5, ALU.mult, ALU.add), t)
            got["t"] = dve.do(lambda e: e.tensor_tensor(y, y, scratch, ALU.mult), t)

        def diagonals(cols, *waits):
            got = []
            for x, col in enumerate(cols):
                if x % 2 == 0:
                    d = work.take()
                dg = d.ap[:, x % 2 * P:(x % 2 + 1) * P]
                t = dve.do(lambda e, col=col, dg=dg: e.tensor_scalar(dg, ident, col, None, ALU.mult),
                           *waits, *d.free)
                got.append((d, dg, t))
            return got

        def rows_to_bank(bank, diags, starts):
            for (d, dg, t), s in zip(diags, starts):
                t = pe.do(lambda e, dg=dg, s=s: e.matmul(bank.ap[:, s:s + P], ones[:, :], dg,
                                                         start=True, stop=True), t, *bank.free)
                d.release(t)
            return t

        row_ready = [None]
        row_read = [()]
        acc_free = [None]

        def rms_rows(at, starts, *waits):
            bank, ty = side_banks.take(), tiny.take()
            n, got = len(starts), {}
            t = acc_free[0] = sums_to_rows(bank, 0, acc, starts, *waits)
            yield True
            ms, y, z = ty.ap[:, 0, 0:n], ty.ap[:, 1, 0:n], ty.ap[:, 2, 0:n]
            t = dve.do(lambda e: e.tensor_scalar(ms, bank.ap[:, 0:n], 1.0 / D, RMS_EPS, ALU.mult, ALU.add),
                       t, *ty.free)
            bank.release(t)
            yield from rsqrt(got, ms, y, z, t)
            dg = diagonals([ty.ap[:, 1, i:i + 1] for i in range(n)], got["t"])
            ty.release(dve.now())
            yield True
            spread = side_banks.take()
            t = rows_to_bank(spread, dg, [s - at for s in starts])
            row_ready[0] = act.do(lambda e: e.copy(row[:, at:TOK], spread.ap[:, 0:TOK - at]), t, *row_read[0])
            spread.release(row_ready[0])

        acc_ready = [None]

        def add_square(src, first, dst, *waits, on_dve=False):
            n = src.shape[-1]
            if first:
                acc_ready[0] = act.do(lambda e: e.activation(dst, src, ACT.Square), *waits, acc_free[0])
                return
            s = work.take()
            if on_dve:
                t = dve.do(lambda e: e.tensor_tensor(s.ap[:, 0:n], src, src, ALU.mult), *waits, *s.free)
            else:
                t = act.do(lambda e: e.activation(s.ap[:, 0:n], src, ACT.Square), *waits, *s.free)
            acc_ready[0] = pool.do(lambda e: e.tensor_tensor(dst, dst, s.ap[:, 0:n], ALU.add),
                                   t, acc_ready[0])
            s.release(acc_ready[0])

        got_h = []

        def load_h(i):
            got_h.append(sp.load(lambda e: e.dma_start(h[:, 2 * i:2 * i + 2, :], tokens[:, 2 * i:2 * i + 2, :]),
                                 s_h[i], 16))
        load_units(1)
        load_h(0)
        got_par = sp.load(lambda e: e.dma_start(par[:, :], params), s_par, 16)
        load_units(2)
        load_h(1)
        load_units(3)
        load_h(2)
        load_units()
        for i in range(3, KT // 2):
            load_h(i)
        got_con = sp.load(lambda e: e.dma_start(con[:, :], consts), s_con, 16)
        got_mask = sp.load(lambda e: e.dma_start(masks[:, 0:sum(KEYS1)], mask1), s_mask, 16)
        made_ones = pool.do(lambda e: e.memset(ones[:, :], 1.0))
        cleared = pool.do(lambda e: e.memset(probs[:, :, :], 0.0))

        a_ready = {}

        def first_operand(kt):
            a_ready[kt] = split_to(a_op[:, kt, 0, :], a_op[:, kt, 1, :], h[:, kt, :], p_col("norm_mix", kt),
                                   got_h[kt // 2], got_par)

        def first_square(kt):
            add_square(h[:, kt, :], kt == 0, acc[:, :], got_h[kt // 2], on_dve=kt % 2 == 1)
        split_lo(0)
        first_operand(0)
        first_operand(1)
        split_lo(1)
        first_operand(2)
        first_operand(3)
        split_lo(2)
        for kt in range(4, KT):
            later(2 * kt - 7, lambda kt=kt: first_operand(kt))
        for kt in range(KT):
            later(5 * kt // 4, lambda kt=kt: first_square(kt))
        later(24, lambda: staged(rms_rows(0, (0, P, TOK - P), acc_ready[0], made_ones, got_con), 2))

        a_of = lambda kt: need(a_ready, kt)

        for x, name in enumerate(("ln_mix_g", "ln_mix_b")):
            src = par[:, PARAMS[name]:PARAMS[name] + KT]
            t = act.do(lambda e, x=x, src=src: e.copy(b_op[:, :, 0, SEQ + x], src), got_par)
            affine = dve.do(lambda e, x=x, src=src: e.tensor_tensor(
                b_op[:, :, 1, SEQ + x], src, b_op[:, :, 0, SEQ + x].bitcast(F32), ALU.subtract), t)

        q_ready, k_ready, v_ready = {}, {}, {}

        def finish_k(hd):
            def finish(bank, done):
                while row_ready[0] is None:
                    yield True
                k_ready[hd] = dve.do(lambda e: e.tensor_tensor(k[:, hd, :], bank.ap[:, 0:TOK], row[:, :], ALU.mult),
                                     done, row_ready[0])
                bank.release(k_ready[hd])
                yield
            return ALL, finish

        def finish_q(hd):
            def finish(bank, done):
                s, y, t = joined(bank, done)
                yield True
                q_ready[hd] = dve.do(lambda e: e.scalar_tensor_tensor(
                    q[:, hd, :], y, SCALE, row[:, REAL], ALU.mult, ALU.mult), t, row_ready[0])
                s.release(q_ready[hd])
            return REAL, finish

        def to_v(hd, src_slot, src, t, n_full, rest):
            bank = side_banks.take()
            for n in range(n_full):
                t2 = pe.do(lambda e, n=n: e.transpose(bank.ap[:, n * P:(n + 1) * P], src[:, n * P:(n + 1) * P], ident),
                           t, got_con, *bank.free)
            if rest:
                t2 = pe.do(lambda e: e.transpose(bank.ap[0:rest, n_full * P:(n_full + 1) * P],
                                                 src[:, n_full * P:n_full * P + rest], ident))
            src_slot.release(t2)
            f = act.do(lambda e: e.copy(v[:, 0:n_full, hd * P:(hd + 1) * P],
                                        bank.ap[:, 0:n_full * P].rearrange("p (n d) -> p n d", d=P)), t2)
            if rest:
                f = act.do(lambda e: e.copy(v[0:rest, n_full, hd * P:(hd + 1) * P],
                                            bank.ap[0:rest, n_full * P:(n_full + 1) * P]), t2)
            bank.release(f)
            v_ready[hd] = f

        def finish_v(hd):
            def finish(bank, done):
                s = work.take()
                t = dve.do(lambda e: e.tensor_tensor(s.ap, bank.ap[:, 0:TOK], row[:, :], ALU.mult),
                           done, row_ready[0], *s.free)
                bank.release(t)
                yield True
                yield True
                yield True
                to_v(hd, s, s.ap, t, 2, META)
            return ALL, finish

        c_ready = [None]
        H8 = slice(0, HEADS)

        def finish_f(bank, done):
            s1, s2, s3 = work.take(), work.take(), work.take()
            z, e1, m = s1.ap[H8, :], s2.ap[H8, :], s3.ap[H8, :]
            bf = par[H8, PARAMS["b_f"]:PARAMS["b_f"] + 1]
            t = dve.do(lambda e: e.tensor_tensor(z, bank.ap[H8, 0:TOK], row[H8, :], ALU.mult),
                       done, row_ready[0], *s1.free)
            bank.release(t)
            t = dve.do(lambda e: e.tensor_scalar(z, z, bf, None, ALU.add), t)
            ta = act.do(lambda e: e.activation(e1, z, ACT.Abs), t, *s2.free)
            ta = act.do(lambda e: e.activation(e1, e1, ACT.Exp, scale=-1.0), ta)
            ta = act.do(lambda e: e.activation(e1, e1, ACT.Ln, bias=1.0), ta)
            t = dve.do(lambda e: e.tensor_scalar(z, z, 0.0, None, ALU.min), ta)
            t = dve.do(lambda e: e.tensor_tensor(z, z, e1, ALU.subtract), t)
            t2 = dve.do(lambda e: e.memset(m, 1.0), *s3.free)
            t = dve.do(lambda e: e.tensor_tensor_scan(csum, m, z, 0.0, ALU.mult, ALU.add), t, t2)
            s1.release(t)
            s2.release(t)
            s3.release(t)
            t = dve.do(lambda e: e.tensor_scalar(cneg, csum, -1.0, None, ALU.mult), t)

            def turn():
                b = side_banks.take()
                for i in range(2):
                    a = META + i * P
                    tp = pe.do(lambda e, a=a, i=i: e.transpose(b.ap[:, 8 * i:8 * i + 8], csum[:, a:a + P],
                                                               con[H8, 0:HEADS]), t, got_con, *b.free)
                c_ready[0] = act.do(lambda e: e.copy(cq[:, :, :], b.ap[:, 0:16].rearrange("p (i h) -> p i h", i=2)), tp)
                b.release(c_ready[0])
            later(12, turn)
            yield

        kt_plain = lambda n, i: UNIT_K * n + i
        U = KT // UNIT_K
        product(U, kt_plain, from_a, a_of, [finish_k(i) for i in range(4)])
        product(2, lambda n, i: 8 * n + i, from_a, a_of, [(ALL, finish_f)], width=P)
        product(U, kt_plain, from_a, a_of, [finish_k(i) for i in range(4, 8)])
        for b in range(2):
            product(U, kt_plain, from_a, a_of, [finish_q(4 * b + i) for i in range(4)])
        for b in range(2):
            product(U, kt_plain, from_a, a_of, [finish_v(4 * b + i) for i in range(4)])
        flush()

        def softmax(state, slot, spans, t, counts, *more):
            ty = tiny.take()
            mx, l, r = ty.ap[:, 0, 0:2], ty.ap[:, 1, 0:2], ty.ap[:, 2, 0:2]
            for i, (a, n) in enumerate(spans):
                t = dve.do(lambda e, i=i, a=a, n=n: e.reduce_max(mx[:, i:i + 1], slot.ap[:, a:a + n], AX_X), t, *ty.free)
            t = dve.do(lambda e: e.tensor_scalar(mx, mx, -1.0, None, ALU.mult), t)
            yield True
            for i, (a, n) in enumerate(spans):
                acc_out = {} if counts else {"accum_out": l[:, i:i + 1]}
                tx = act.do(lambda e, i=i, a=a, n=n, o=acc_out: e.activation(
                    slot.ap[:, a:a + n], slot.ap[:, a:a + n], ACT.Exp, bias=mx[:, i:i + 1], **o), t)
            yield True
            yield True
            t = tx
            if counts:
                for i, (a, n) in enumerate(spans):
                    t = dve.do(lambda e, i=i, a=a, n=n: e.scalar_tensor_tensor(
                        slot.ap[:, a:a + n], slot.ap[:, a:a + n], 1.0, counts[i], ALU.mult, ALU.mult,
                        accum_out=l[:, i:i + 1]), tx, *more)
            t = dve.do(lambda e: e.reciprocal(r, l), t)
            for i, (a, n) in enumerate(spans):
                t = dve.do(lambda e, i=i, a=a, n=n: e.tensor_scalar(
                    slot.ap[:, a:a + n], slot.ap[:, a:a + n], r[:, i:i + 1], None, ALU.mult), t)
            ty.release(t)
            state["t"] = t

        y_ready, ms_ready = {}, {}

        def group_square(g):
            s = work.take()
            y = s.ap[:, 0:SEQ]
            t = act.do(lambda e: e.activation(y, ytile[:, g, :], ACT.Square), y_ready[g], *s.free)

            def sums():
                b = side_banks.take()
                t2 = sums_to_rows(b, 0, s.ap, (0, P), t)
                s.release(t2)
                yield True
                ms_ready[g] = dve.do(lambda e: e.tensor_scalar(gms[:, g, :], b.ap[:, 0:2], 1.0 / P, RMS_EPS,
                                                               ALU.mult, ALU.add), t2)
                b.release(ms_ready[g])
            later(4, lambda: staged(sums()))

        probs_t_free = [()]
        q_cols = (0, KEYS1[0])

        def head1(hd):
            state = {}

            def scores():
                b, s = side_banks.take(), prob_ring.take()
                sel = con[H8, hd:hd + 1].to_broadcast([HEADS, P])
                for i in range(2):
                    n, o = KEYS1[i], q_cols[i]
                    pe.quiet(lambda e, i=i, n=n, o=o: e.matmul(
                        b.ap[:, o:o + n], q[:, hd, i * P:(i + 1) * P], k[:, hd, 0:n], start=True, stop=False),
                        q_ready[hd], k_ready[hd], *b.free)
                    t = pe.do(lambda e, n=n, o=o: e.matmul(b.ap[:, o:o + n], sel, cneg[:, 0:n],
                                                           start=False, stop=True), c_ready[0])
                spans = ((0, KEYS1[0]), (SEQ, KEYS1[1]))
                for i, (a, n) in enumerate(spans):
                    o = q_cols[i]
                    t = dve.do(lambda e, i=i, a=a, n=n, o=o: e.scalar_tensor_tensor(
                        s.ap[:, a:a + n], b.ap[:, o:o + n], cq[:, i, hd:hd + 1], masks[:, o:o + n],
                        ALU.add, ALU.add), t, c_ready[0], got_mask, cleared, *s.free)
                b.release(t)
                state["s"] = s
                staged(softmax(state, s, spans, t, None))

            def turn():
                s, t = state["s"], state["t"]
                got = []
                for kt in range(2):
                    b = side_banks.take()
                    for i in range(2):
                        t2 = pe.do(lambda e, i=i, kt=kt, b=b: e.transpose(
                            b.ap[:, i * P:(i + 1) * P], s.ap[:, i * SEQ + kt * P:i * SEQ + (kt + 1) * P], ident),
                            t, *b.free)
                    if kt == 0:
                        t2 = pe.do(lambda e, b=b: e.transpose(b.ap[0:META, SEQ:SEQ + P],
                                                              s.ap[:, 2 * SEQ:2 * SEQ + META], ident))
                        got.append(act.do(lambda e, b=b: e.copy(probs_t2[:, :], b.ap[0:META, SEQ:SEQ + P]),
                                          t2, *probs_t_free[0]))
                    got.append(act.do(lambda e, b=b, kt=kt: e.copy(probs_t[:, kt * SEQ:(kt + 1) * SEQ],
                                                                   b.ap[:, 0:SEQ]), t2, *probs_t_free[0]))
                    b.release(*got)
                s.release(t2)
                state["t"] = got

            def values():
                bo = side_banks.take()
                hs = slice(hd * P, (hd + 1) * P)
                pe.quiet(lambda e: e.matmul(bo.ap[:, 0:SEQ], v[:, 0, hs], probs_t[:, 0:SEQ], start=True, stop=False,
                                            skip_group_check=True), *state["t"], v_ready[hd], *bo.free)
                pe.quiet(lambda e: e.matmul(bo.ap[:, P:SEQ], v[0:META, 2, hs], probs_t2[:, :], start=False,
                                            stop=False, skip_group_check=True))
                t = pe.do(lambda e: e.matmul(bo.ap[:, 0:SEQ], v[:, 1, hs], probs_t[:, SEQ:2 * SEQ], start=False,
                                             stop=True, skip_group_check=True))
                probs_t_free[0] = (t,)
                y_ready[hd] = act.do(lambda e: e.copy(ytile[:, hd, :], bo.ap[:, 0:SEQ]), t)
                bo.release(y_ready[hd])
                group_square(hd)

            later(HEAD_STEPS * hd + 1, scores)
            later(HEAD_STEPS * hd + 15, turn)
            later(HEAD_STEPS * hd + 24, values)

        b_ready = {}

        def normed_groups(groups, *waits):
            ty = tiny.take()
            n = 2 * len(groups)
            ms = gms[:, groups[0]:groups[-1] + 1, :].rearrange("p g i -> p (g i)")
            y, z, got = ty.ap[:, 1, 0:n], ty.ap[:, 2, 0:n], {}
            staged(rsqrt(got, ms, y, z, *[ms_ready[g] for g in groups], *ty.free), 1)

            def pair(x):
                dg = diagonals([ty.ap[:, 1, 2 * x + i:2 * x + i + 1] for i in range(4)], got["t"])
                if x == len(groups) - 2:
                    ty.release(dve.now())
                yield True
                yield True
                b = side_banks.take()
                t = rows_to_bank(b, dg, (0, P, SEQ, SEQ + P))
                yield True
                for y, g in enumerate(groups[x:x + 2]):
                    s = work.take()
                    yn = s.ap[:, 0:SEQ]
                    t3 = dve.do(lambda e, g=g, y=y, yn=yn: e.tensor_tensor(
                        yn, ytile[:, g, :], b.ap[:, y * SEQ:(y + 1) * SEQ], ALU.mult), t, *s.free)
                    staged(split_later(b_ready, g, b_op[:, g, 0, 0:SEQ], b_op[:, g, 1, 0:SEQ], yn,
                                       p_col("out_gain", g), s, t3, *waits))
                b.release(t3)
            for x in range(0, len(groups), 2):
                later(5 + 2 * x, lambda x=x: staged(pair(x)))

        for hd in range(HEADS):
            head1(hd)
        later(HEAD_STEPS * HEADS + 22, lambda: normed_groups(list(range(HEADS))))
        conv = {}

        def finish_conv(j, what):
            def finish_edge(bank, done):
                s = work.take()
                y = s.ap[:, 0:CONV_TOK]
                t = dve.do(lambda e: e.tensor_tensor(y, bank.ap[:, 0:CONV_TOK], row[:, CONV], ALU.mult), done, *s.free)
                bank.release(t)
                if what == "gate_c":
                    conv["gc", j] = (s, y, t)
                    return
                yield True
                gs, gy, gt = conv["gc", j]
                t = pool.do(lambda e: e.tensor_tensor(y, y, gy, ALU.mult), t, gt)
                gs.release(t)
                yield True
                yield True
                o = work.take()
                u = o.ap[:, 0:SEQ]
                t = dve.do(lambda e: e.tensor_scalar(u, y[:, 0:SEQ], p_col("conv_w", j), None, ALU.mult), t, *o.free)
                for tap in (1, 2):
                    t = dve.do(lambda e, tap=tap: e.scalar_tensor_tensor(
                        u, y[:, tap:tap + SEQ], p_col("conv_w", 8 * tap + j), u, ALU.mult, ALU.add), t)
                s.release(t)
                conv["u", j] = (o, u, t)

            def finish_b(bank, done):
                s, y, t = joined(bank, done)
                yield True
                t = pool.do(lambda e: e.tensor_tensor(y, y, row[:, REAL], ALU.mult), t)
                yield True
                need(conv, ("u", j))
                yield True
                o, u, ut = conv["u", j]
                g = HEADS + j
                y_ready[g] = pool.do(lambda e: e.tensor_tensor(ytile[:, g, :], y, u, ALU.mult), t, ut)
                s.release(y_ready[g])
                o.release(y_ready[g])
                group_square(g)
                if j in (3, 7):
                    later(6, lambda: normed_groups(list(range(g - 3, g + 1))))
            return (REAL, finish_b) if what == "gate_b" else (CONV, finish_edge)

        conv_tiles = [finish_conv(j, what) for j in range(8) for what in ("gate_c", "h", "gate_b")]
        for b in range(6):
            product(U, kt_plain, from_a, a_of, conv_tiles[4 * b:4 * b + 4], tail=2 * (b == 5))

        h_ready = {}

        def into_h(j, bank, done, first_scale=None):
            hr = h[:, j, REAL]
            old = (h_ready[j],) if j in h_ready else ()
            if first_scale is None:
                t = dve.do(lambda e: e.tensor_tensor(hr, hr, bank.ap[:, 0:SEQ], ALU.add), done, *old)
            else:
                t = dve.do(lambda e: e.scalar_tensor_tensor(hr, hr, first_scale, bank.ap[:, 0:SEQ],
                                                            ALU.mult, ALU.add), done, *old)
            t = dve.do(lambda e: e.tensor_tensor(hr, hr, bank.ap[:, SEQ:2 * SEQ], ALU.add), t)
            bank.release(t)
            h_ready[j] = t
            return t

        def finish_norm_tile(j, gain, waits_a):
            def run(bank, done):
                t = into_h(j, bank, done)
                yield True
                yield from split_later(a_ready, j, a_op[:, j, 0, REAL], a_op[:, j, 1, REAL], h[:, j, REAL],
                                       p_col(gain, j), None, t, waits_a)
                add_square(h[:, j, REAL], j == 0, acc[:, REAL], t)
                if j == KT - 1:
                    later(10, lambda: staged(rms_rows(META, (META, META + P), acc_ready[0]), 3))
            return REAL, run

        b_of = lambda kt: need(b_ready, kt)

        a_free = pe.now()

        for kt in range(KT):
            a_ready[kt] = None
        row_ready[0], row_read[0] = None, (dve.now(), pool.now())
        for b in range(4):
            product(U, kt_plain, from_b, b_of, [finish_norm_tile(4 * b + i, "norm_ffn", a_free) for i in range(4)])

        masks_free = (dve.now(), pe.now())

        def finish_gate_up(slot, what, keep, b_free):
            def finish(bank, done):
                s, y, t = joined(bank, done)
                yield True
                while row_ready[0] is None:
                    step()
                t = dve.do(lambda e: e.tensor_tensor(y, y, row[:, REAL], ALU.mult), t, row_ready[0])
                yield True
                if what == "gate":
                    keep[slot] = (s, y, act.do(lambda e: e.activation(y, y, ACT.Silu), t))
                    return
                while slot not in keep:
                    step()
                gs, gy, gt = keep.pop(slot)
                t = dve.do(lambda e: e.tensor_tensor(y, y, gy, ALU.mult), t, gt)
                gs.release(t)
                yield True
                yield from split_later(b_ready, slot, b_op[:, slot, 0, 0:SEQ], b_op[:, slot, 1, 0:SEQ], y, None, s,
                                       t, b_free)
            return REAL, finish

        def angles():
            s1, s2, s3 = work.take(), work.take(), work.take()
            ang, n, r = (s.ap[:, 0:SEQ] for s in (s1, s2, s3))
            freq, sign = con[:, C_FREQ:C_FREQ + 1], con[:, C_SIGN:C_SIGN + 1]
            got = sp.load(lambda e: e.dma_start(n.bitcast(I32), positions), s_pos, 16, *s2.free)
            for _ in range(12):
                yield True
            t = dve.do(lambda e: e.tensor_copy(ang, n.bitcast(I32)), got, *s1.free)
            t = dve.do(lambda e: e.tensor_scalar(ang, ang, freq, None, ALU.mult), t)
            t = dve.do(lambda e: e.tensor_scalar(r.bitcast(I32), ang, 1.0 / (2.0 * np.pi), None, ALU.mult), t, *s3.free)
            t = dve.do(lambda e: e.tensor_copy(n, r.bitcast(I32)), t)
            yield True
            part1 = 6.28125
            part2 = float(np.float32(np.round((2 * np.pi - part1) * 2.0 ** 21) / 2.0 ** 21))
            part3 = float(np.float32(2 * np.pi - part1 - part2))
            for c in (part1, part2, part3):
                t = dve.do(lambda e, c=c: e.scalar_tensor_tensor(ang, n, -c, ang, ALU.mult, ALU.add), t)
            t = dve.do(lambda e: e.tensor_scalar(ang, ang, float(np.float32(3.1415925)), float(np.float32(-3.1415925)),
                                                 ALU.min, ALU.max), t)
            yield True
            ts = act.do(lambda e: e.activation(sinr, ang, ACT.Sin), t, c_ready[0])
            t = act.do(lambda e: e.activation(ang, ang, ACT.Abs), ts)
            yield True
            ts = dve.do(lambda e: e.tensor_scalar(sinr, sinr, sign, None, ALU.mult), ts)
            t = dve.do(lambda e: e.tensor_scalar(ang, ang, -1.0, float(np.pi / 2), ALU.mult, ALU.add), t)
            yield True
            t = act.do(lambda e: e.activation(cosr, ang, ACT.Sin), t)
            for slot in (s1, s2, s3):
                slot.release(t)
            turned["angles"] = (ts, t)

        turned = {}
        later(40, lambda: staged(angles()))

        def scaled_angles():
            while row_ready[0] is None:
                step()
            t1, t2 = turned["angles"]
            dve.do(lambda e: e.tensor_tensor(cosr, cosr, row[:, REAL], ALU.mult), t1, t2, row_ready[0])
            return dve.do(lambda e: e.tensor_tensor(sinr, sinr, row[:, REAL], ALU.mult))

        keep = {}
        base = 0
        for gi, n in enumerate(GROUPS1):
            b_free = pe.now()
            for slot in range(n):
                b_ready[slot] = None
            for b in range(n // 2):
                tiles = [finish_gate_up(2 * b + x // 2, ("gate", "up")[x % 2], keep, b_free) for x in range(4)]
                product(U, kt_plain, from_a, a_of, tiles)
            a_free = pe.now()
            last = gi == len(GROUPS1) - 1

            def finish_down(j):
                def add(bank, done):
                    into_h(j, bank, done)
                    yield
                return (REAL, add) if not last else finish_norm_tile(j, "final_norm", a_free)
            if last:
                flush_until(b_ready, n)
                row_ready[0], row_read[0] = None, (dve.now(), pool.now())
                for kt in range(KT):
                    a_ready[kt] = None
            for b in range(4):
                product(n // UNIT_K, kt_plain, from_b, b_of, [finish_down(4 * b + i) for i in range(4)])
            base += n

        got_mask2 = sp.load(lambda e: e.dma_start(masks[:, :], mask2), s_mask, 32, *masks_free)
        rope_ready = [None]

        def finish_rope(dst, hd, book):
            def finish(bank, done):
                if rope_ready[0] is None:
                    rope_ready[0] = scaled_angles()
                s, y, t = joined(bank, done)
                yield True
                o = work.take()
                w_ = o.ap[:, 0:SEQ]
                act.quiet(lambda e: e.copy(w_[0:64, :], y[64:128, :]), t, *o.free)
                t2 = act.do(lambda e: e.copy(w_[64:128, :], y[0:64, :]))
                yield True
                t3 = dve.do(lambda e: e.tensor_tensor(y, y, cosr, ALU.mult), t2, rope_ready[0])
                t2 = pool.do(lambda e: e.tensor_tensor(w_, w_, sinr, ALU.mult), t2, rope_ready[0])
                yield True
                book[hd] = pool.do(lambda e: e.tensor_tensor(dst[:, hd, 0:SEQ], y, w_, ALU.add), t2, t3)
                s.release(book[hd])
                o.release(book[hd])
            return REAL, finish

        def finish_v2(hd):
            def finish(bank, done):
                s, y, t = joined(bank, done)
                yield True
                t = dve.do(lambda e: e.tensor_tensor(y, y, row[:, REAL], ALU.mult), t, row_ready[0])
                for _ in range(4):
                    yield True
                to_v(hd, s, y, t, 2, 0)
            return REAL, finish

        for b in range(2):
            product(U, kt_plain, from_a, a_of, [finish_rope(k, 4 * b + i, k_ready) for i in range(4)])
        for b in range(2):
            product(U, kt_plain, from_a, a_of, [finish_rope(q, 4 * b + i, q_ready) for i in range(4)])

        def residual(j):
            t = dve.do(lambda e: e.scalar_tensor_tensor(h[:, j, REAL], h[:, j, REAL], p_col("final_norm", j),
                                                        row[:, REAL], ALU.mult, ALU.mult),
                       row_ready[0], h_ready[j], a_ready[j])
            h_ready[j] = t
        for j in range(KT):
            later(1 + 3 * j, lambda j=j: residual(j))
        for b in range(2):
            product(U, kt_plain, from_a, a_of, [finish_v2(4 * b + i) for i in range(4)])
        flush()

        def head2(hd):
            state = {}
            cols = (0, KEYS2[0])
            spans = ((0, KEYS2[0]), (KEYS2[0], KEYS2[1]))

            def scores():
                b, s = side_banks.take(), prob_ring.take()
                for i in range(2):
                    n, o = KEYS2[i], cols[i]
                    t = pe.do(lambda e, i=i, n=n, o=o: e.matmul(
                        b.ap[:, o:o + n], q[:, hd, i * P:(i + 1) * P], k[:, hd, 0:n], start=True, stop=True),
                        q_ready[hd], k_ready[hd], *b.free)
                t = dve.do(lambda e: e.scalar_tensor_tensor(s.ap[:, 0:P + SEQ], b.ap[:, 0:P + SEQ], SCALE,
                                                            masks[:, 0:P + SEQ], ALU.mult, ALU.add),
                           t, got_mask2, *s.free)
                b.release(t)
                counts = [masks[:, P + SEQ + a:P + SEQ + a + n] for a, n in spans]
                state["s"] = s
                staged(softmax(state, s, spans, t, counts))

            def turn():
                s, t = state["s"], state["t"]
                bt = side_banks.take()
                for x, a in enumerate((0, P, 2 * P)):
                    t2 = pe.do(lambda e, a=a: e.transpose(bt.ap[:, a:a + P], s.ap[:, a:a + P], ident), t, *bt.free)
                s.release(t2)
                f = act.do(lambda e: e.copy(probs_t[:, 0:3 * P], bt.ap[:, 0:3 * P]), t2, *probs_t_free[0])
                bt.release(f)
                state["t"] = f

            def values():
                bo = side_banks.take()
                hs = slice(hd * P, (hd + 1) * P)
                pe.quiet(lambda e: e.matmul(bo.ap[:, 0:SEQ], v[:, 0, hs], probs_t[:, 0:SEQ], start=True, stop=False,
                                            skip_group_check=True), state["t"], v_ready[hd], *bo.free)
                t = pe.do(lambda e: e.matmul(bo.ap[:, P:SEQ], v[:, 1, hs], probs_t[:, SEQ:3 * P], start=False,
                                             stop=True, skip_group_check=True))
                probs_t_free[0] = (t,)
                s = work.take()
                y = s.ap[:, 0:SEQ]
                f = act.do(lambda e: e.copy(y, bo.ap[:, 0:SEQ]), t, *s.free)
                bo.release(f)
                staged(split_later(b_ready, hd, b_op[:, hd, 0, 0:SEQ], b_op[:, hd, 1, 0:SEQ], y, None, s, f, b_free))

            later(HEAD_STEPS * hd + 1, scores)
            later(HEAD_STEPS * hd + 17, turn)
            later(HEAD_STEPS * hd + 26, values)

        b_free = pe.now()
        for hd in range(HEADS):
            head2(hd)

        pool_ready = {}

        def finish_u(j):
            g = j // 2
            win = POOL_WINDOWS[g]

            def finish(bank, done):
                s, y, t = joined(bank, done)
                yield True
                x = work.take()
                tz = pool.do(lambda e: e.memset(x.ap[:, 0:META], 0.0), *x.free)
                t = dve.do(lambda e: e.tensor_tensor(x.ap[:, REAL], y, row[:, REAL], ALU.mult), t, *x.free)
                s.release(t)
                src, lo, span, t = x, 0, 1, (t, tz)
                while span < win:
                    lo += span
                    o = work.take()
                    t = (pool.do(lambda e, o=o, src=src, lo=lo, span=span: e.tensor_tensor(
                        o.ap[:, lo:TOK], src.ap[:, lo:TOK], src.ap[:, lo - span:TOK - span], ALU.add), *t, *o.free),)
                    if src is not x:
                        src.release(*t)
                    src, span = o, 2 * span
                yield True
                yield True
                dst = ytile[:, 8 + j, :]
                ramp = con[:, C_RAMP + 16 * g:C_RAMP + 16 * (g + 1)]
                t1 = dve.do(lambda e: e.scalar_tensor_tensor(dst, src.ap[:, REAL], 1.0 / win, x.ap[:, REAL],
                                                             ALU.mult, ALU.subtract), *t)
                t2 = dve.do(lambda e: e.tensor_tensor(src.ap[:, META:2 * META], src.ap[:, META:2 * META], ramp, ALU.mult), t1)
                pool_ready[j] = dve.do(lambda e: e.tensor_tensor(dst[:, 0:META], src.ap[:, META:2 * META],
                                                                 x.ap[:, META:2 * META], ALU.subtract), t2)
                src.release(pool_ready[j])
                x.release(pool_ready[j])
            return REAL, finish

        for b in range(2):
            product(U, kt_plain, from_a, a_of, [finish_u(4 * b + i) for i in range(4)])

        sig_ready, merged_ready = {}, {}

        def finish_gate(slot, *waits):
            def finish(bank, done):
                s, y, t = joined(bank, done)
                yield True
                t = dve.do(lambda e: e.tensor_tensor(y, y, row[:, REAL], ALU.mult), t)
                yield True
                sig_ready[slot] = act.do(lambda e: e.activation(ytile[:, slot, :], y, ACT.Sigmoid), t, *waits)
                s.release(sig_ready[slot])
            return REAL, finish

        product(U, kt_plain, from_a, a_of, [finish_gate(i) for i in range(4)])
        product(U, kt_plain, from_a, a_of, [finish_gate(4 + i) for i in range(4)])

        flush_until(pool_ready, 8)
        n0 = unit_at[0]
        for half in range(2):
            n = n0 + half
            for g in (2 * half, 2 * half + 1):
                for m in range(2):
                    bank = out_banks.take()
                    for kt in range(2):
                        at = (g % 2) * 512 + kt * 256 + m * P
                        t = pe.do(lambda e, n=n, at=at, g=g, kt=kt, bank=bank: e.matmul(
                            bank.ap[:, 0:SEQ], raw[:, n % RAW, at:at + P], ytile[:, 8 + 2 * g + kt, :],
                            start=(kt == 0), stop=(kt == 1)), landed[n], pool_ready[2 * g + kt], *bank.free)
                    j = 2 * g + m
                    s = work.take()
                    y = s.ap[:, 0:SEQ]
                    f = act.do(lambda e, y=y, bank=bank: e.copy(y, bank.ap[:, 0:SEQ]), t, *s.free)
                    bank.release(f)
                    b_ready[8 + j] = split_to(b_op[:, 8 + j, 0, 0:SEQ], b_op[:, 8 + j, 1, 0:SEQ], y,
                                              p_col("pool_scale", j), f, b_free)
                    s.release(b_ready[8 + j])
            raw_done(n, t)
        unit_at[0] += 2
        pooled = pe.now()
        product(U, kt_plain, from_a, a_of, [finish_gate(8 + i, pooled) for i in range(4)])
        product(U, kt_plain, from_a, a_of, [finish_gate(12 + i) for i in range(4)])
        flush()
        attended = pe.now()

        def branches(b, base, to_a):
            def attn(i):
                def finish(bank, done):
                    s, y, t = joined(bank, done)
                    yield True
                    sg = ytile[:, base + i, :]
                    sig_ready[base + i] = pool.do(lambda e: e.tensor_tensor(sg, sg, y, ALU.mult), t, sig_ready[base + i])
                    s.release(sig_ready[base + i])
                return REAL, finish

            def pooled_(i):
                j = 4 * b + i

                def finish(bank, done):
                    s, y, t = joined(bank, done)
                    yield True
                    t = dve.do(lambda e: e.tensor_tensor(y, y, ytile[:, base + 4 + i, :], ALU.mult), t,
                               sig_ready[base + 4 + i])
                    yield True
                    if to_a is None:
                        merged_ready[j] = pool.do(lambda e: e.tensor_tensor(q[:, j, :], y, ytile[:, base + i, :], ALU.add),
                                                  t, sig_ready[base + i], attended)
                        s.release(merged_ready[j])
                        return
                    t = pool.do(lambda e: e.tensor_tensor(y, y, ytile[:, base + i, :], ALU.add), t, sig_ready[base + i])
                    merged_ready[j] = t
                    yield True
                    yield from split_later(a_ready, j, a_op[:, j, 0, REAL], a_op[:, j, 1, REAL], y, None, s, t, to_a)
                return REAL, finish
            product(4, kt_plain, from_b, b_of, [attn(i) for i in range(4)])
            product(4, lambda n, i: 8 + UNIT_K * n + i, from_b, b_of, [pooled_(i) for i in range(4)])

        branches(0, 0, None)
        branches(1, 8, None)
        flush()
        for x in range(4):
            base = (0, 4, 8, 12)[x]
            product(U, kt_plain, from_a, a_of, [finish_gate(base + i, pool.now(), dve.now()) for i in range(4)])
        a_free = pe.now()
        flush()
        for j in range(KT):
            a_ready[j] = None

        def late_split(j):
            staged(split_later(a_ready, j, a_op[:, j, 0, REAL], a_op[:, j, 1, REAL], q[:, j, :], None, None,
                               merged_ready[j], a_free))
        for j in range(8):
            later(1 + j, lambda j=j: late_split(j))
        branches(2, 0, a_free)
        branches(3, 8, a_free)
        flush()

        FIRST = KT // 4
        shift_ready, rows_ready = [None], [None]
        sum_ready = [None, None]
        last_parts = [None]
        b_free = pe.now()

        def centre(j, operand):
            hr = h[:, j, REAL]
            t = dve.do(lambda e: e.tensor_tensor(hr, hr, shift[:, :], ALU.subtract), h_ready[j], shift_ready[0])
            h_ready[j] = t
            if j > 0:
                yield True
            if j == 0:
                sum_ready[0] = dve.do(lambda e: e.tensor_copy(acc[:, REAL], hr), t)
                sum_ready[1] = act.do(lambda e: e.activation(acc2[:, :], hr, ACT.Square), t, acc_free[0])
            else:
                s = work.take()
                t2 = act.do(lambda e: e.activation(s.ap[:, 0:SEQ], hr, ACT.Square), t, *s.free)
                if j == KT - 1:
                    last_parts[0] = (s, t, t2)
                else:
                    sum_ready[0] = pool.do(lambda e: e.tensor_tensor(acc[:, REAL], acc[:, REAL], hr, ALU.add),
                                           t, sum_ready[0])
                    sum_ready[1] = pool.do(lambda e: e.tensor_tensor(acc2[:, :], acc2[:, :], s.ap[:, 0:SEQ], ALU.add),
                                           t2, sum_ready[1])
                    s.release(sum_ready[1])
            if operand:
                yield from split_later(b_ready, j, b_op[:, j, 0, 0:SEQ], b_op[:, j, 1, 0:SEQ], hr,
                                       p_col("ln_mix_g", j), None, t, b_free)

        def norm_tile(j, operand):
            if j < FIRST:
                hr = h[:, j, REAL]
                if j == 0:
                    sum_ready[0] = dve.do(lambda e: e.tensor_copy(acc[:, REAL], hr), h_ready[j], acc_free[0])
                else:
                    sum_ready[0] = pool.do(lambda e: e.tensor_tensor(acc[:, REAL], acc[:, REAL], hr, ALU.add),
                                           h_ready[j], sum_ready[0])
                if j == FIRST - 1:
                    def mean():
                        b = side_banks.take()
                        t = pe.do(lambda e: e.matmul(b.ap[:, 0:SEQ], ones[:, :], acc[:, REAL], start=True, stop=True),
                                  sum_ready[0], *b.free)
                        shift_ready[0] = act.do(lambda e: e.activation(shift[:, :], b.ap[:, 0:SEQ], ACT.Copy,
                                                                       scale=1.0 / (FIRST * P)), t, *row_read[0])
                        b.release(shift_ready[0])
                    later(9, mean)
                    for x in range(FIRST):
                        later(14 + 3 * x, lambda x=x: staged(centre(x, operand)))
                return
            while shift_ready[0] is None:
                step()
            staged(centre(j, operand))
            if j == KT - 1:
                later(8 if operand else 2, lambda: staged(norm_rows(), 4 if operand else 1))

        def norm_rows():
            bank, ty = side_banks.take(), tiny.take()
            y, z, o, m2 = (ty.ap[:, i, 0:2] for i in (1, 2, 3, 4))
            means = ty.ap[:, 5, 0:4]
            warm = act.do(lambda e: e.activation(ty.ap[:, 1, 0:1], ones[:, 0:1], ACT.Sqrt), *ty.free)
            s, t, t2 = last_parts[0]
            t = sums_to_rows(bank, 0, acc, (META, META + P), sum_ready[0], more=(h[:, KT - 1, :], t))
            t = sums_to_rows(bank, 2, acc2, (0, P), sum_ready[1], more=(s.ap, t2))
            acc_free[0] = t
            s.release(t)
            yield True
            t = dve.do(lambda e: e.tensor_scalar(means, bank.ap[:, 0:4], 1.0 / D, None, ALU.mult), t, *ty.free)
            bank.release(t)
            d = means[:, 0:2]
            t = dve.do(lambda e: e.tensor_tensor(z, d, d, ALU.mult), t)
            t = dve.do(lambda e: e.scalar_tensor_tensor(m2, means[:, 2:4], LN_EPS, z, ALU.add, ALU.subtract), t)
            got = {}
            yield from rsqrt(got, m2, y, z, t, warm)
            t = got["t"]
            dg = diagonals([ty.ap[:, 1, i:i + 1] for i in range(2)], t)
            t = dve.do(lambda e: e.scalar_tensor_tensor(o, d, -1.0, y, ALU.mult, ALU.mult), t)
            dg2 = diagonals([ty.ap[:, 3, i:i + 1] for i in range(2)], t)
            ty.release(dve.now())
            yield True
            b1, b2 = side_banks.take(), side_banks.take()
            t = rows_to_bank(b1, dg, (0, P))
            r1 = act.do(lambda e: e.copy(row[:, REAL], b1.ap[:, 0:SEQ]), t, *row_read[0])
            b1.release(r1)
            t = rows_to_bank(b2, dg2, (0, P))
            r2 = dve.do(lambda e: e.tensor_copy(shift[:, :], b2.ap[:, 0:SEQ]), t, pool.now())
            b2.release(r2)
            rows_ready[0] = (r1, r2)

        def normed(j, eng, gain, bias):
            hr = h[:, j, REAL]
            t = eng.do(lambda e: e.tensor_tensor(hr, hr, row[:, REAL], ALU.mult), h_ready[j], rows_ready[0][0], *sum_ready)
            yield True
            t = eng.do(lambda e: e.tensor_tensor(hr, hr, shift[:, :], ALU.add), t, rows_ready[0][1])
            yield True
            yield True
            h_ready[j] = act.do(lambda e: e.activation(hr, hr, ACT.Identity, scale=p_col(gain, j), bias=p_col(bias, j)), t)

        def finish_mix(j):
            def finish(bank, done):
                into_h(j, bank, done, ALPHA)
                yield True
                norm_tile(j, True)
            return REAL, finish

        for j in range(KT):
            b_ready[j] = None
        for b in range(4):
            product(U, kt_plain, from_a, a_of, [finish_mix(4 * b + i) for i in range(4)], tail=2 * (b == 3))

        def residual2(j):
            while rows_ready[0] is None:
                yield True
            yield from normed(j, dve, "ln_mix_g", "ln_mix_b")
        for j in range(KT):
            later(37 + 5 * j, lambda j=j: staged(residual2(j)))

        def finish_ff1(slot, a_free):
            def finish(bank, done):
                while rows_ready[0] is None:
                    step()
                s = work.take()
                y, with_gain, with_bias = s.ap[:, 0:SEQ], s.ap[:, SEQ:SEQ + 1], s.ap[:, SEQ + 1:SEQ + 2]
                t2 = dve.do(lambda e: e.tensor_copy(s.ap[:, SEQ:SEQ + 2], bank.ap[:, SEQ:SEQ + 2]), done, *s.free)
                t = dve.do(lambda e: e.tensor_tensor(y, bank.ap[:, 0:SEQ], row[:, REAL], ALU.mult), rows_ready[0][0])
                bank.release(t)
                yield True
                t = dve.do(lambda e: e.scalar_tensor_tensor(y, shift[:, :], with_gain, y, ALU.mult, ALU.add),
                           t, t2, rows_ready[0][1])
                t = dve.do(lambda e: e.tensor_scalar(y, y, with_bias, 0.0, ALU.add, ALU.max), t)
                t = pool.do(lambda e: e.tensor_tensor(y, y, y, ALU.mult), t)
                yield True
                yield True
                yield from split_later(a_ready, slot, a_op[:, slot, 0, REAL], a_op[:, slot, 1, REAL], y, None, s,
                                       t, a_free)
            return WITH_AFFINE, finish

        b_all = lambda kt: (*need(b_ready, kt), affine)
        for gi, n in enumerate(GROUPS2):
            a_free = pe.now()
            for slot in range(n):
                a_ready[slot] = None
            for b in range(n // BLOCK):
                product(U, kt_plain, from_b, b_all, [finish_ff1(BLOCK * b + i, a_free) for i in range(4)])

            last = gi == len(GROUPS2) - 1
            if last:
                flush_until(a_ready, n)
                row_read[0] = (dve.now(), pool.now())
                shift_ready[0] = rows_ready[0] = None

            def finish_ff2(j, gi=gi, last=last):
                def finish(bank, done):
                    into_h(j, bank, done, ALPHA if gi == 0 else None)
                    yield True
                    if last:
                        norm_tile(j, False)
                return REAL, finish
            for b in range(4):
                product(n // UNIT_K, kt_plain, from_a, a_of, [finish_ff2(4 * b + i) for i in range(4)],
                        tail=SPLIT * (last and b == 3))
        flush()

        stored = 0

        def last_tile(j):
            nonlocal stored
            yield from normed(j, pool if j % 3 == 1 else dve, "ln_ff_g", "ln_ff_b")
            out_ready[j] = h_ready[j]
            first = j - j % 2
            if first in out_ready and first + 1 in out_ready:
                stored += 16
                sp.load(lambda e: e.dma_start(out[:, first:first + 2, :], h[:, first:first + 2, REAL]), s_out, stored,
                        out_ready[first], out_ready[first + 1])
        out_ready = {}
        for j in range(KT):
            later(j, lambda j=j: staged(last_tile(j), 3 if j % 3 == 1 else 1))
        flush()
        assert unit_at[0] == len(order)
        sp.wait(Ticket(s_out, stored))

        block = ctx.enter_context(nc.Block())
        block.sync(sp.play)
        block.tensor(pe.play)
        block.scalar(act.play)
        block.vector(dve.play)
        block.gpsimd(pool.play)



def pack_weight(m, tiles=None):
    rows, cols = m.shape
    m = m.reshape(rows // (UNIT_K * P), UNIT_K, P, cols // P, P)
    if tiles is not None:
        m = m[:, :, :, tiles, :]
    m = m.reshape(rows // (UNIT_K * P), UNIT_K, P, cols // (BLOCK * P), BLOCK * P)
    m = m.transpose(3, 0, 2, 1, 4)
    return np.ascontiguousarray(m).reshape(m.shape[0], m.shape[1], P, UNIT)


def feature_columns(vec):
    return vec.reshape(-1, P).T


def shape_constants():
    con = np.zeros((P, N_CONST), np.float32)
    con[:, C_IDENT:C_IDENT + P] = np.eye(P, dtype=np.float32)
    half = P // 2
    freq = np.float32(10000.0) ** (-np.arange(half, dtype=np.float32) / np.float32(half))
    con[:, C_FREQ] = np.concatenate([freq, freq])
    con[:, C_SIGN] = np.concatenate([-np.ones(half), np.ones(half)])
    for g, win in enumerate(POOL_WINDOWS):
        con[:, C_RAMP + 16 * g:C_RAMP + 16 * (g + 1)] = 1.0 / np.minimum(np.arange(1, 17), win)
    rows = np.arange(P)[:, None]
    mask1 = np.concatenate([np.where(np.arange(n)[None] <= META + i * P + rows, 0.0, NEG)
                            for i, n in enumerate(KEYS1)], axis=1).astype(np.float32)
    count = []
    for i, n in enumerate(KEYS2):
        dist = i * P + rows - np.arange(n)[None]
        count.append(sum(((dist >= 0) & (dist <= span * dil) & (dist % dil == 0)).astype(np.float32)
                         for span, dil in ((128, 1), (128, 4), (128, 16))))
    count = np.concatenate(count, axis=1)
    mask2 = np.concatenate([np.where(count > 0, 0.0, NEG), count], axis=1).astype(np.float32)
    return con, mask1, mask2


def kernel(**inputs):
    import concourse.bacc as bacc
    from concourse.bass_utils import run_bass_kernel_spmd

    a = {n: np.asarray(x) for n, x in inputs.items()}
    w_in = a["w_in"][0]
    tiles1 = list(range(8, 16)) + list(range(0, 8)) + list(range(16, 24))
    for j in range(8):
        tiles1 += [32 + j, 40 + j, 24 + j]
    n_main = 48 * P
    w_f = np.zeros((D, P), w_in.dtype)
    w_f[:, 0:HEADS] = w_in[:, n_main:]
    w_f = np.ascontiguousarray(w_f.reshape(2, 8, P, P).transpose(0, 2, 1, 3)).reshape(1, 2, P, UNIT)
    gu = np.concatenate([a["w_gate"][0], a["w_up"][0]], axis=1)
    n_ff = D_FF1 // P
    tiles_gu = [x for j in range(n_ff) for x in (j, n_ff + j)]
    tiles2 = list(range(8, 16)) + list(range(0, 8)) + list(range(16, 32))
    for b in range(4):
        tiles2 += [32 + 4 * b + i for i in range(4)] + [48 + 4 * b + i for i in range(4)]
    w_pool = a["w_pool_2"][0].reshape(2, 2, 2, P, 256).transpose(0, 3, 1, 2, 4)
    weights = {
        "w_in": pack_weight(w_in[:, 0:n_main], tiles1),
        "w_f": w_f,
        "w_out": pack_weight(a["w_out"][0]),
        "w_gu": pack_weight(gu, tiles_gu),
        "w_down": pack_weight(a["w_down"][0]),
        "w_in_2": pack_weight(a["w_in_2"][0], tiles2),
        "w_pool": np.ascontiguousarray(w_pool).reshape(1, 2, P, UNIT),
        "w_ba": pack_weight(a["w_branch_attn_2"][0]),
        "w_bp": pack_weight(a["w_branch_pool_2"][0]),
        "w_out_2": pack_weight(a["w_out_2"][0]),
        "w_ff1": pack_weight(a["w_ff1_2"][0]),
        "w_ff2": pack_weight(a["w_ff2_2"][0]),
    }
    tokens = np.concatenate([a["meta"], a["x"][0]], axis=0).T.reshape(KT, P, TOK).transpose(1, 0, 2)
    params = np.zeros((P, N_PARAMS), np.float32)

    def put(name, cols):
        params[0:cols.shape[0], PARAMS[name]:PARAMS[name] + cols.shape[1]] = cols
    put("norm_mix", feature_columns(a["norm_mix"][0]))
    put("out_gain", feature_columns(a["out_gain"][0]))
    put("norm_ffn", feature_columns(a["norm_ffn"][0]))
    put("final_norm", feature_columns(a["final_norm"]))
    put("conv_w", feature_columns(a["conv_w"][0].reshape(-1)))
    put("pool_scale", feature_columns(a["pool_scale_2"][0]))
    put("ln_mix_g", feature_columns(a["ln_mix_g_2"][0]))
    put("ln_mix_b", feature_columns(a["ln_mix_b_2"][0]))
    put("ln_ff_g", feature_columns(a["ln_ff_g_2"][0]))
    put("ln_ff_b", feature_columns(a["ln_ff_b_2"][0]))
    put("b_f", a["b_f"][0].reshape(HEADS, 1))
    con, mask1, mask2 = shape_constants()
    positions = np.broadcast_to(a["positions_2"][0][None, :], (P, SEQ))

    arrays = {f"in_{n}": x for n, x in weights.items()}
    arrays |= {"in_tokens": tokens, "in_params": params, "in_consts": con, "in_mask1": mask1,
               "in_mask2": mask2, "in_positions": positions}
    arrays = {n: np.ascontiguousarray(x) for n, x in arrays.items()}
    nc = bacc.Bacc("TRN2", target_bir_lowering=False, num_devices=1)
    aps = {n: nc.dram_tensor(n, x.shape, mybir.dt.from_np(x.dtype), kind="ExternalInput").ap()
           for n, x in arrays.items()}
    out = nc.dram_tensor("out", (P, KT, SEQ), F32, kind="ExternalOutput").ap()
    two_blocks(nc, {n: aps[f"in_{n}"] for n in weights}, aps["in_tokens"], aps["in_params"], aps["in_consts"],
               aps["in_mask1"], aps["in_mask2"], aps["in_positions"], out)
    r = run_bass_kernel_spmd(nc, [arrays], core_ids=[0])
    got = r.results[0]["out"]
    return np.ascontiguousarray(got.transpose(2, 1, 0)).reshape(1, SEQ, D)
```
